# Optimizing a Trainium2 kernel written in Bass

```python
import math
import jax
import jax.numpy as jnp
from jax import lax
import numpy as np

D_MODEL = 1024
BATCH = 1
SEQ = 2048
DEPTH = 1
DEC_BATCH = 1
DEC_SEQ = 64
PAST_LEN = 512

CHUNK = 64
EPS = 1e-6
GLA_HEADS = 4
GLA_DK = 64
GLA_DV = 128
GLA_KW = GLA_HEADS * GLA_DK
GLA_VW = GLA_HEADS * GLA_DV
GLA_RANK = 16
GLA_TAU = 16.0
POOL_WINDOWS = (2, 4, 8, 16)
POOL_GROUPS = 4
POOL_GW = 128
POOL_W = POOL_GROUPS * POOL_GW
POOL_BUF = 15
GDN_HEADS = 4
GDN_DK = 128
GDN_DV = 128
GDN_KW = GDN_HEADS * GDN_DK
GDN_VW = GDN_HEADS * GDN_DV
CONV_W = 4
GDN_CONV_CH = 2 * GDN_KW + GDN_VW
N_BRANCH = 3
SPLIT_SIZES = (GLA_KW, GLA_KW, GLA_VW, GLA_RANK, GLA_VW,
               POOL_W, POOL_W,
               GDN_CONV_CH, GDN_HEADS, GDN_HEADS, GDN_VW,
               N_BRANCH * D_MODEL)
D_IN = sum(SPLIT_SIZES)

kernel_name = 'hybrid_gla_pool_gdn_stream_step'

def _split_points():
    pts, acc = [], 0
    for s in SPLIT_SIZES[:-1]:
        acc += s
        pts.append(acc)
    return tuple(pts)

def rmsnorm(x, g):
    xf = x.astype(jnp.float32)
    r = xf * lax.rsqrt(jnp.mean(xf * xf, axis=-1, keepdims=True) + EPS)
    return (r * g.astype(jnp.float32)).astype(x.dtype)

def head_rmsnorm(o, g):
    B, H, L, DV = o.shape
    o = o.transpose(0, 2, 1, 3)
    r = o * lax.rsqrt(jnp.mean(o * o, axis=-1, keepdims=True) + EPS)
    return (r * g.astype(jnp.float32).reshape(H, DV)).reshape(B, L, H * DV)

def to_heads(a, n):
    B, L, W = a.shape
    return a.reshape(B, L, n, W // n).transpose(0, 2, 1, 3)

def l2norm(a):
    return a * lax.rsqrt(jnp.sum(a * a, axis=-1, keepdims=True) + EPS)

def gla_recurrence(q, k, v, logf, s0):
    B, H, L, DK = q.shape
    DV = v.shape[-1]
    C = min(CHUNK, L)
    n = L // C

    def to_chunks(a):
        return a.reshape(B, H, n, C, a.shape[-1]).transpose(2, 0, 1, 3, 4)

    xs = (to_chunks(q), to_chunks(k), to_chunks(v), to_chunks(logf))
    mask = jnp.tril(jnp.ones((C, C), bool))[:, :, None]

    def step(s, inp):
        qc, kc, vc, fc = inp
        b = jnp.cumsum(fc, axis=2)
        diff = b[:, :, :, None, :] - b[:, :, None, :, :]
        decay = jnp.exp(jnp.where(mask, diff, -jnp.inf))
        att = jnp.einsum('bhid,bhjd,bhijd->bhij', qc, kc, decay)
        o = (jnp.einsum('bhij,bhjv->bhiv', att, vc)
             + jnp.einsum('bhid,bhdv->bhiv', qc * jnp.exp(b), s))
        b_last = b[:, :, -1:, :]
        s = (jnp.exp(b_last[:, :, 0, :])[..., None] * s
             + jnp.einsum('bhjd,bhjv->bhdv', kc * jnp.exp(b_last - b), vc))
        return s, o

    s, o = lax.scan(step, s0, xs)
    o = o.transpose(1, 2, 0, 3, 4).reshape(B, H, L, DV)
    return o, s

def gdn_recurrence(q, k, v, g, beta, s0):
    B, H, L, DK = q.shape
    DV = v.shape[-1]
    C = min(CHUNK, L)
    n = L // C
    q, k, v = (a.reshape(B, H, n, C, a.shape[-1]) for a in (q, k, v))
    g = g.reshape(B, H, n, C)
    beta = beta.reshape(B, H, n, C)
    G = jnp.cumsum(g, axis=-1)
    gdiff = G[..., :, None] - G[..., None, :]
    incl = jnp.tril(jnp.ones((C, C), bool))
    strict = jnp.tril(jnp.ones((C, C), bool), -1)
    dec_incl = jnp.exp(jnp.where(incl, gdiff, -jnp.inf))
    dec_strict = jnp.where(strict, dec_incl, 0.0)
    m = beta[..., :, None] * jnp.einsum('bhnid,bhnjd->bhnij', k, k) * dec_strict
    rhs = jnp.concatenate([beta[..., None] * v, (beta * jnp.exp(G))[..., None] * k], axis=-1)
    sol = lax.linalg.triangular_solve(m + jnp.eye(C, dtype=m.dtype), rhs,
                                      left_side=True, lower=True, unit_diagonal=True)
    u_bar, w = sol[..., :DV], sol[..., DV:]
    a_qk = jnp.einsum('bhnid,bhnjd->bhnij', q, k) * dec_incl
    q_dec = q * jnp.exp(G)[..., None]
    k_dec = k * jnp.exp(G[..., -1:] - G)[..., None]
    g_last = jnp.exp(G[..., -1])
    xs = tuple(jnp.moveaxis(a, 2, 0) for a in (u_bar, w, a_qk, q_dec, k_dec, g_last))

    def step(s, inp):
        ub, wc, ac, qd, kd, gl = inp
        u = ub - jnp.einsum('bhcd,bhdv->bhcv', wc, s)
        o = jnp.einsum('bhcd,bhdv->bhcv', qd, s) + jnp.einsum('bhij,bhjv->bhiv', ac, u)
        s = gl[..., None, None] * s + jnp.einsum('bhcd,bhcv->bhdv', kd, u)
        return s, o

    s, o = lax.scan(step, s0, xs)
    o = jnp.moveaxis(o, 0, 2).reshape(B, H, L, DV)
    return o, s

def short_conv(u, buf, w):
    L = u.shape[1]
    ext = jnp.concatenate([buf.astype(u.dtype), u], axis=1)
    y = ext[:, 0:L] * w[0]
    for i in range(1, CONV_W):
        y = y + ext[:, i:i + L] * w[i]
    return jax.nn.silu(y), ext[:, -(CONV_W - 1):]

def pool_mix(u, buf, offset, pool_w, pool_scale):
    B, L, _ = u.shape
    ext = jnp.concatenate([buf.astype(u.dtype), u], axis=1)
    cs = jnp.cumsum(ext.astype(jnp.float32), axis=1)
    cs = jnp.concatenate([jnp.zeros((B, 1, POOL_W), jnp.float32), cs], axis=1)
    end = cs[:, POOL_BUF + 1:POOL_BUF + 1 + L]
    pos = offset + jnp.arange(L)
    means = []
    for gi, win in enumerate(POOL_WINDOWS):
        sl = slice(gi * POOL_GW, (gi + 1) * POOL_GW)
        start = cs[:, POOL_BUF + 1 - win:POOL_BUF + 1 - win + L, sl]
        cnt = jnp.minimum(pos + 1, win).astype(jnp.float32)[None, :, None]
        means.append((end[..., sl] - start) / cnt)
    d = jnp.concatenate(means, axis=-1) - u.astype(jnp.float32)
    d = d.reshape(B, L, POOL_GROUPS, POOL_GW).astype(u.dtype)
    y = jnp.einsum('blgc,gcd->blgd', d, pool_w).reshape(B, L, POOL_W)
    return y * pool_scale, ext[:, -POOL_BUF:]

def layer(x, s_gla, s_gdn, conv_buf, pool_buf, offset,
          norm_pre, w_in, gla_wf2, gla_bf, gla_norm, gla_wo,
          pool_w, pool_scale, pool_wo,
          gdn_conv, gdn_a_log, gdn_dt_bias, gdn_norm, gdn_wo,
          w_out, norm_post):
    f32 = jnp.float32
    B, L, _ = x.shape
    h = rmsnorm(x, norm_pre)
    proj = jnp.einsum('bld,de->ble', h, w_in)
    (gla_q, gla_k, gla_v, gla_f, gla_z, pool_u, pool_z,
     gdn_qkv, gdn_a, gdn_b, gdn_z, gates) = jnp.split(proj, _split_points(), axis=-1)

    q = to_heads(gla_q, GLA_HEADS).astype(f32) * (GLA_DK ** -0.5)
    k = to_heads(gla_k, GLA_HEADS).astype(f32)
    v = to_heads(gla_v, GLA_HEADS).astype(f32)
    logf = jax.nn.log_sigmoid((gla_f @ gla_wf2 + gla_bf).astype(f32)) / GLA_TAU
    logf = to_heads(logf, GLA_HEADS)
    o, s_gla_new = gla_recurrence(q, k, v, logf, s_gla.astype(f32))
    o = head_rmsnorm(o, gla_norm) * jax.nn.silu(gla_z.astype(f32))
    y_gla = o.astype(x.dtype) @ gla_wo

    pooled, pool_buf_new = pool_mix(pool_u, pool_buf, offset, pool_w, pool_scale)
    y_pool = (pooled * jax.nn.silu(pool_z)) @ pool_wo

    qkv, conv_buf_new = short_conv(gdn_qkv, conv_buf, gdn_conv)
    cq, ck, cv = jnp.split(qkv, (GDN_KW, 2 * GDN_KW), axis=-1)
    q = l2norm(to_heads(cq, GDN_HEADS).astype(f32)) * (GDN_DK ** -0.5)
    k = l2norm(to_heads(ck, GDN_HEADS).astype(f32))
    v = to_heads(cv, GDN_HEADS).astype(f32)
    g = -jnp.exp(gdn_a_log.astype(f32)) * jax.nn.softplus(gdn_a.astype(f32) + gdn_dt_bias.astype(f32))
    beta = jax.nn.sigmoid(gdn_b.astype(f32))
    o, s_gdn_new = gdn_recurrence(q, k, v, g.transpose(0, 2, 1), beta.transpose(0, 2, 1),
                                  s_gdn.astype(f32))
    o = head_rmsnorm(o, gdn_norm) * jax.nn.silu(gdn_z.astype(f32))
    y_gdn = o.astype(x.dtype) @ gdn_wo

    gts = jax.nn.sigmoid(gates.astype(f32)).reshape(B, L, N_BRANCH, D_MODEL)
    merged = gts[:, :, 0] * y_gla + gts[:, :, 1] * y_pool + gts[:, :, 2] * y_gdn
    y = merged.astype(x.dtype) @ w_out
    x = x + rmsnorm(y, norm_post)
    return (x, s_gla_new.astype(x.dtype), s_gdn_new.astype(x.dtype),
            conv_buf_new.astype(x.dtype), pool_buf_new.astype(x.dtype))

def setup_inputs(seed: int = 0) -> dict:
    key = jax.random.key(seed)
    ks = jax.random.split(key, 24)
    f32 = jnp.float32

    def nrm(k, shape, scale):
        return jax.random.normal(k, shape, f32) * scale

    dt = jnp.exp(jax.random.uniform(ks[21], (DEPTH, GDN_HEADS), f32, math.log(1e-3), math.log(1e-1)))
    return {
        'x_prompt': nrm(ks[0], (BATCH, SEQ, D_MODEL), 1.0),
        'x_sample': nrm(ks[1], (DEC_BATCH, DEC_SEQ, D_MODEL), 1.0),
        'state_gla': nrm(ks[2], (DEPTH, DEC_BATCH, GLA_HEADS, GLA_DK, GLA_DV), 0.3),
        'state_gdn': nrm(ks[3], (DEPTH, DEC_BATCH, GDN_HEADS, GDN_DK, GDN_DV), 0.1),
        'cache_gdn_conv': nrm(ks[4], (DEPTH, DEC_BATCH, CONV_W - 1, GDN_CONV_CH), 1.0),
        'cache_pool': nrm(ks[5], (DEPTH, DEC_BATCH, POOL_BUF, POOL_W), 1.0),
        'norm_pre': 1.0 + nrm(ks[6], (DEPTH, D_MODEL), 0.05),
        'w_in': nrm(ks[7], (DEPTH, D_MODEL, D_IN), D_MODEL ** -0.5),
        'gla_wf2': nrm(ks[8], (DEPTH, GLA_RANK, GLA_KW), GLA_RANK ** -0.5),
        'gla_bf': nrm(ks[9], (DEPTH, GLA_KW), 0.1),
        'gla_norm': 1.0 + nrm(ks[10], (DEPTH, GLA_VW), 0.05),
        'gla_wo': nrm(ks[11], (DEPTH, GLA_VW, D_MODEL), GLA_VW ** -0.5),
        'pool_w': nrm(ks[12], (DEPTH, POOL_GROUPS, POOL_GW, POOL_GW), POOL_GW ** -0.5),
        'pool_scale': 1.0 + nrm(ks[13], (DEPTH, POOL_W), 0.1),
        'pool_wo': nrm(ks[14], (DEPTH, POOL_W, D_MODEL), POOL_W ** -0.5),
        'gdn_conv': nrm(ks[15], (DEPTH, CONV_W, GDN_CONV_CH), CONV_W ** -0.5),
        'gdn_a_log': jnp.log(jax.random.uniform(ks[16], (DEPTH, GDN_HEADS), f32, 1.0, 16.0)),
        'gdn_dt_bias': dt + jnp.log(-jnp.expm1(-dt)),
        'gdn_norm': 1.0 + nrm(ks[17], (DEPTH, GDN_VW), 0.05),
        'gdn_wo': nrm(ks[18], (DEPTH, GDN_VW, D_MODEL), GDN_VW ** -0.5),
        'w_out': nrm(ks[19], (DEPTH, D_MODEL, D_MODEL), D_MODEL ** -0.5),
        'norm_post': 1.0 + nrm(ks[20], (DEPTH, D_MODEL), 0.05),
    }

def reference(x_prompt, x_sample, state_gla, state_gdn, cache_gdn_conv, cache_pool,
              norm_pre, w_in, gla_wf2, gla_bf, gla_norm, gla_wo,
              pool_w, pool_scale, pool_wo,
              gdn_conv, gdn_a_log, gdn_dt_bias, gdn_norm, gdn_wo,
              w_out, norm_post):
    dtp = x_prompt.dtype
    bp = x_prompt.shape[0]
    yp, ys = x_prompt, x_sample
    p_gla, p_gdn, p_conv, p_pool = [], [], [], []
    s_gla, s_gdn, s_conv, s_pool = [], [], [], []
    for i in range(DEPTH):
        lp = (norm_pre[i], w_in[i], gla_wf2[i], gla_bf[i], gla_norm[i], gla_wo[i],
              pool_w[i], pool_scale[i], pool_wo[i],
              gdn_conv[i], gdn_a_log[i], gdn_dt_bias[i], gdn_norm[i], gdn_wo[i],
              w_out[i], norm_post[i])
        yp, a, b, c, d = layer(yp,
                               jnp.zeros((bp, GLA_HEADS, GLA_DK, GLA_DV), dtp),
                               jnp.zeros((bp, GDN_HEADS, GDN_DK, GDN_DV), dtp),
                               jnp.zeros((bp, CONV_W - 1, GDN_CONV_CH), dtp),
                               jnp.zeros((bp, POOL_BUF, POOL_W), dtp),
                               0, *lp)
        p_gla.append(a); p_gdn.append(b); p_conv.append(c); p_pool.append(d)
        ys, a, b, c, d = layer(ys, state_gla[i], state_gdn[i], cache_gdn_conv[i], cache_pool[i],
                               PAST_LEN, *lp)
        s_gla.append(a); s_gdn.append(b); s_conv.append(c); s_pool.append(d)
    return (yp, ys,
            jnp.stack(p_gla), jnp.stack(p_gdn), jnp.stack(p_conv), jnp.stack(p_pool),
            jnp.stack(s_gla), jnp.stack(s_gdn), jnp.stack(s_conv), jnp.stack(s_pool))


_drawn_inputs = setup_inputs


def setup_inputs(seed=0):
    import zlib

    import numpy as np

    out = dict(_drawn_inputs(seed))
    spreads = {}
    factors = {}
    for name, (base, spread) in spreads.items():
        noise = np.random.default_rng([zlib.crc32(name.encode()), seed]).standard_normal(out[name].shape)
        drawn = base * np.exp(spread * noise) if base else spread * noise
        out[name] = jnp.asarray(drawn.astype(out[name].dtype))
    for name, factor in factors.items():
        out[name] = (out[name] * factor).astype(out[name].dtype)
    return out
```

```python
from contextlib import ExitStack

import concourse.bass as bass
from concourse import mybir

F32 = mybir.dt.float32
F32R = mybir.dt.float32r
ALU = mybir.AluOpType
ACT = mybir.ActivationFunctionType

P = 128
DM = 1024
KD = DM // P
NP_ = 2048
NS_ = 64
NT = NP_ + NS_
TILES = 6
TW = NT // TILES
HEADS = 4
CHUNKS = NP_ // P
EPS = 1e-6
LEVELS = 7
ROW = 2144
POOL_HALO = 15
CONV_HALO = 3

C_IDENT = 0
C_ONES = C_IDENT + P
C_CNT = C_ONES + P
C_END = C_CNT + 16

M_UPPER = 0
M_NEG = M_UPPER + P
M_POS = M_NEG + P
M_LOW = M_POS + P
M_LOWT = M_LOW + LEVELS * P
M_END = M_LOWT + (LEVELS + 1) * P

F_SPECIAL = 0
F_COPY = 1
F_SILU = F_COPY + 8
F_POOL = F_SILU + 8
F_CONV = F_POOL + 8
F_GATE = F_CONV + 12
F_END = F_GATE + 24

A_SPECIAL = 0
A_COPY = 1
A_POOL = A_COPY + 8
A_CONV = A_POOL + 4
A_GATE = A_CONV + 12

R_GLA_Q, R_GLA_K, R_GLA_V = 0, 2, 4
R_LOGF = 8
R_GB = 10
R_GLA_Z = 11
R_GDN_Z = 15
R_GDN_Q, R_GDN_K, R_GDN_V = 19, 23, 27
R_END = 31

S_NEGA, S_DT, S_BF, S_PSCALE, S_ZNORM, S_CONV, S_EPS, S_QS = 0, 1, 2, 4, 8, 16, 64, 65
S_END = 66

AT_F, AT_G, AT_B = 0, 32, 64


def at_least(eng, sem, value):
    if isinstance(value, int) and value <= 0:
        return
    eng.wait_ge(sem, value)


class Held:

    def __init__(self, nc):
        self.nc, self.semaphores = nc, []

    def add(self, semaphore):
        self.semaphores.append(semaphore)
        return semaphore

    def __enter__(self):
        return self

    def __exit__(self, *error):
        self.nc.clear_and_free_semaphores(self.semaphores)
        self.nc.all_engine_barrier()


def column(tensor, n):
    return tensor[:, n:n + 1] if isinstance(n, int) else tensor[:, bass.ds(n, 1)]


def norm_phase(nc, d, hi, lo, consts):
    tiles = CHUNKS + 1
    with ExitStack() as ctx, Held(nc) as held:
        def sb(name, shape, dt=F32):
            return ctx.enter_context(nc.sbuf_tensor(name, shape, dt))

        def sem(name):
            return held.add(nc.alloc_semaphore(name))

        x_in = sb("x_in", [P, 2, DM])
        x_scaled = sb("x_scaled", [P, 2, DM])
        squares = sb("squares", [P, DM])
        gain = sb("gain", [P, DM])
        sums = sb("sums", [P, 2])
        logs = sb("logs", [P, 2])
        rstd = sb("rstd", [P, 2])
        eps = sb("eps", [P, 1])
        turned = ctx.enter_context(nc.psum_tensor("turned", [P, 2, KD, P], F32))
        ident = consts[:, C_IDENT:C_IDENT + P]

        gain_landed = sem("gain_landed")
        x_landed = [sem("x_landed0"), sem("x_landed1")]
        eps_set = sem("eps_set")
        sums_ready = sem("sums_ready")
        logs_ready = sem("logs_ready")
        rstd_ready = sem("rstd_ready")
        scaled_ready = sem("scaled_ready")
        turned_ready = sem("turned_ready")
        hi_ready = sem("hi_ready")
        lo_ready = sem("lo_ready")

        with nc.Block() as block:
            @block.sync
            def _(sp):
                sp.dma_start(consts[:, :], d["consts"]).then_inc(gain_landed, 16)
                sp.dma_start(gain[:, :], d["norm_pre"].to_broadcast([P, DM])).then_inc(gain_landed, 16)
                sp.dma_start(x_in[:, 0], d["x_prompt"][0:P, :]).then_inc(x_landed[0], 16)
                sp.dma_start(x_in[:, 1], d["x_prompt"][P:2 * P, :]).then_inc(x_landed[1], 16)
                with sp.Fori(1, CHUNKS // 2) as i:
                    for u in range(2):
                        sp.wait_ge(scaled_ready, i * 2 + (u - 1))
                        sp.dma_start(x_in[:, u], d["x_prompt"][bass.ds((i * 2 + u) * P, P), :]) \
                            .then_inc(x_landed[u], 16)
                sp.wait_ge(scaled_ready, CHUNKS - 1)
                sp.dma_start(x_in[0:NS_, 0], d["x_sample"]).then_inc(x_landed[0], 16)

            @block.scalar
            def _(act):
                def statistics(t, i, u):
                    act.wait_ge(x_landed[u], i * 16 + 16)
                    nc.scalar.activation(squares[:, :], x_in[:, u], ACT.Square,
                                         accum_out=sums[:, u:u + 1]).then_inc(sums_ready, 1)
                    act.wait_ge(sums_ready, t + 1)
                    nc.scalar.activation(logs[:, u:u + 1], sums[:, u:u + 1], ACT.Ln, bias=eps[:, 0:1],
                                         scale=1.0 / DM).then_inc(logs_ready, 1)
                    act.wait_ge(logs_ready, t + 1)
                    nc.scalar.activation(rstd[:, u:u + 1], logs[:, u:u + 1], ACT.Exp,
                                         scale=-0.5).then_inc(rstd_ready, 1)

                def high(t, u, n=P):
                    act.wait_ge(turned_ready, t + 1)
                    nc.scalar.copy(hi[:, :, bass.ds(t * P, n)], turned[:, u, :, 0:n]).then_inc(hi_ready, 1)

                act.wait_ge(eps_set, 1)
                statistics(0, 0, 0)
                with act.Fori(0, CHUNKS // 2) as i:
                    statistics(i * 2 + 1, i, 1)
                    high(i * 2, 0)
                    statistics(i * 2 + 2, i + 1, 0)
                    high(i * 2 + 1, 1)
                high(CHUNKS, 0, NS_)

            @block.vector
            def _(dve):
                nc.vector.memset(eps[:, :], EPS).then_inc(eps_set, 1)

                def scale(t, u):
                    dve.wait_ge(rstd_ready, t + 1)
                    nc.vector.scalar_tensor_tensor(x_scaled[:, u], x_in[:, u], rstd[:, u:u + 1], gain[:, :],
                                                   ALU.mult, ALU.mult).then_inc(scaled_ready, 1)

                def low(t, u, n=P):
                    dve.wait_ge(hi_ready, t + 1)
                    nc.vector.tensor_tensor(lo[:, :, bass.ds(t * P, n)], turned[:, u, :, 0:n],
                                            hi[:, :, bass.ds(t * P, n)].bitcast(F32),
                                            ALU.subtract).then_inc(lo_ready, 1)

                dve.wait_ge(gain_landed, 32)
                scale(0, 0)
                dve.wait_ge(rstd_ready, 2)
                scale(1, 1)
                low(0, 0)
                dve.wait_ge(turned_ready, 1)
                scale(2, 0)
                low(1, 1)
                with dve.Fori(1, CHUNKS // 2) as i:
                    dve.wait_ge(turned_ready, i * 2)
                    scale(i * 2 + 1, 1)
                    low(i * 2, 0)
                    dve.wait_ge(turned_ready, i * 2 + 1)
                    scale(i * 2 + 2, 0)
                    low(i * 2 + 1, 1)
                low(CHUNKS, 0, NS_)

            @block.tensor
            def _(pe):
                def turn(t, u):
                    pe.wait_ge(scaled_ready, t + 1)
                    for k in range(KD):
                        mm = nc.tensor.transpose(turned[:, u, k], x_scaled[:, u, k * P:(k + 1) * P], ident)
                    mm.then_inc(turned_ready, 1)

                pe.wait_ge(gain_landed, 32)
                turn(0, 0)
                turn(1, 1)
                with pe.Fori(1, CHUNKS // 2) as i:
                    for u in range(2):
                        pe.wait_ge(lo_ready, i * 2 + (u - 1))
                        turn(i * 2 + u, u)
                pe.wait_ge(lo_ready, CHUNKS - 1)
                turn(CHUNKS, 0)


def project_phase(nc, d, hi, lo, consts):
    with ExitStack() as ctx, Held(nc) as held:
        def sb(name, shape, dt=F32):
            return ctx.enter_context(nc.sbuf_tensor(name, shape, dt))

        def sem(name):
            return held.add(nc.alloc_semaphore(name))

        w_raw = sb("w_raw", [P, 2, DM])
        w_hi = sb("w_hi", [P, 2, KD, P], F32R)
        w_lo = sb("w_lo", [P, 2, KD, P], F32R)
        X = sb("row_x", [P, 2, ROW])
        Y = sb("row_y", [P, 2, ROW])
        T = sb("row_t", [P, ROW])
        sig = sb("sig", [P, 2, TW])
        small = sb("small", [P, S_END])
        wf2 = sb("wf2", [16, 256])
        pool_w = sb("pool_w", [P, 4, P])
        conv_cache = sb("conv_cache", [P, 12, CONV_HALO])
        conv_out = sb("conv_out", [P, 2, 12, CONV_HALO])
        pool_out = sb("pool_out", [P, 2, 4, POOL_HALO])
        dense = ctx.enter_context(nc.psum_tensor("dense", [P, 2, 512], F32))
        side = ctx.enter_context(nc.psum_tensor("side", [P, 2, 512], F32))
        zero = sb("zero", [P, 1])
        zeros = zero[:, 0:1].rearrange("p (a b) -> p a b", b=1).to_broadcast([P, KD, P])
        ones = consts[:, C_ONES:C_ONES + P]

        zero_set = sem("zero_set")
        params_landed = sem("params_landed")
        w_landed = [sem("w_landed0"), sem("w_landed1")]
        w_high = sem("w_high")
        w_split = sem("w_split")
        dense_ready = sem("dense_ready")
        act_free = sem("act_free")
        dve_free = sem("dve_free")
        side_ready = sem("side_ready")
        side_free = sem("side_free")
        norm_free = sem("norm_free")
        act_done = sem("act_done")
        dve_done = sem("dve_done")
        special_ready = sem("special_ready")
        special_stored = sem("special_stored")
        logf_ready = sem("logf_ready")
        copy_stored = [sem("copy_stored0"), sem("copy_stored1")]
        sig_ready = sem("sig_ready")
        silu_stored = [sem("silu_stored0"), sem("silu_stored1")]
        pool_step = sem("pool_step")
        pool_d_ready = sem("pool_d_ready")
        pool_stored = sem("pool_stored")
        halo_set = sem("halo_set")
        conv_step = sem("conv_step")
        special_step = sem("special_step")
        conv_ready = sem("conv_ready")
        conv_sig_ready = sem("conv_sig_ready")
        conv_silu_ready = sem("conv_silu_ready")
        squares_ready = sem("squares_ready")
        norm_logs_ready = sem("norm_logs_ready")
        norm_ready = sem("norm_ready")
        qkv_ready = sem("qkv_ready")
        qkv_stored = [sem("qkv_stored0"), sem("qkv_stored1")]
        caches_stored = sem("caches_stored")
        gate_stored = [sem("gate_stored0"), sem("gate_stored1")]

        feat, gates, outs = d["feat"], d["gates"], d["branch_out"]
        PARAMS = 12 * 16

        with nc.Block() as block:
            @block.gpsimd
            def _(pool):
                def split(i, f, p):
                    pool.wait_ge(w_landed[p], i * 16 + 16)
                    raw = w_raw[:, p].rearrange("p (k m) -> p k m", k=KD)
                    nc.gpsimd.tensor_tensor(w_hi[:, p], raw, zeros, ALU.add).then_inc(w_high, 1)
                    pool.wait_ge(w_high, f + 1)
                    nc.gpsimd.tensor_tensor(w_lo[:, p], raw, w_hi[:, p].bitcast(F32),
                                            ALU.subtract).then_inc(w_split, 1)

                nc.gpsimd.memset(zero[:, :], 0.0).then_inc(zero_set, 1)
                pool.wait_ge(zero_set, 1)
                split(0, 0, 0)
                split(0, 1, 1)
                with pool.Fori(1, F_END // 2) as i:
                    for p in range(2):
                        pool.wait_ge(dense_ready, i * (2 * TILES) + (p - 1) * TILES)
                        split(i, i * 2 + p, p)
                pool.wait_ge(dense_ready, (F_END - 2) * TILES)
                split(F_END // 2, F_END - 1, 0)

            @block.tensor
            def _(pe):
                def project(f, p, own, before):
                    pe.wait_ge(w_split, f + 1)
                    for t in range(TILES):
                        if t >= 2:
                            pe.wait_ge(own[0], own[1] * TILES + (t - 1))
                        elif before is not None:
                            pe.wait_ge(before[0], before[1] * TILES + (TILES + t - 1))
                        for k in range(KD):
                            cols = slice(t * TW, (t + 1) * TW)
                            out = dense[:, t % 2, 0:TW]
                            nc.tensor.matmul(out, w_hi[:, p, k], hi[:, k, cols], start=(k == 0), stop=False)
                            nc.tensor.matmul(out, w_hi[:, p, k], lo[:, k, cols], start=False, stop=False)
                            mm = nc.tensor.matmul(out, w_lo[:, p, k], hi[:, k, cols], start=False,
                                                  stop=(k == KD - 1))
                        mm.then_inc(dense_ready, 1)

                def by_act(n):
                    return act_free, n

                def by_dve(n):
                    return dve_free, n

                project(F_SPECIAL, 0, by_act(A_SPECIAL), None)
                pe.wait_ge(special_ready, 1)
                for b in range(2):
                    for t in range(TILES):
                        n = b * TILES + t
                        at_least(pe, side_free, n - 1)
                        nc.tensor.matmul(side[:, n % 2, 0:TW], wf2[:, b * P:(b + 1) * P],
                                         X[0:16, 0, t * TW:(t + 1) * TW], start=True, stop=True) \
                            .then_inc(side_ready, 1)
                with pe.Fori(0, 4) as i:
                    for u in range(2):
                        project(i * 2 + (F_COPY + u), 1 - u, by_act(i * 2 + (A_COPY + u)),
                                by_act(i * 2 + (A_COPY + u - 1)))
                project(F_SILU, 1, by_dve(0), by_act(A_COPY + 7))
                project(F_SILU + 1, 0, by_dve(1), by_dve(0))
                with pe.Fori(1, 4) as i:
                    for u in range(2):
                        project(i * 2 + (F_SILU + u), 1 - u, by_dve(i * 2 + u), by_dve(i * 2 + (u - 1)))
                for g in range(4):
                    project(F_POOL + 2 * g, 1, by_act(A_POOL + g), by_dve(7 + g))
                    project(F_POOL + 2 * g + 1, 0, by_dve(8 + g), by_act(A_POOL + g))
                    pe.wait_ge(pool_d_ready, g + 1)
                    for t in range(TILES):
                        n = (2 + g) * TILES + t
                        pe.wait_ge(side_free, n - 1)
                        nc.tensor.matmul(side[:, n % 2, 0:TW], pool_w[:, g], X[:, 1, t * TW:(t + 1) * TW],
                                         start=True, stop=True).then_inc(side_ready, 1)

                def square_sums(j):
                    pe.wait_ge(squares_ready, j + 1)
                    for t in range(TILES):
                        if isinstance(j, int) and j == 0 and t < 2:
                            pe.wait_ge(side_free, 6 * TILES + t - 1)
                        elif t < 2:
                            pe.wait_ge(norm_free, j * TILES + (t - 1))
                        else:
                            pe.wait_ge(norm_free, j * TILES + (t - 1))
                        nc.tensor.matmul(side[:, t % 2, 0:TW], ones, T[:, t * TW:(t + 1) * TW],
                                         start=True, stop=True).then_inc(side_ready, 1)

                def conv_project(j, p):
                    project(j + F_CONV, p, by_act(j + A_CONV), by_act(j + (A_CONV - 1)))

                project(F_CONV, 1, by_act(A_CONV), by_dve(11))
                conv_project(1, 0)
                square_sums(0)
                with pe.Fori(0, 3) as i:
                    conv_project(i * 2 + 2, 1)
                    square_sums(i * 2 + 1)
                    conv_project(i * 2 + 3, 0)
                    square_sums(i * 2 + 2)
                conv_project(8, 1)
                square_sums(7)
                conv_project(9, 0)
                with pe.Fori(0, 13) as i:
                    conv_project(i * 2 + 10, 1)
                    conv_project(i * 2 + 11, 0)

            @block.scalar
            def _(act):
                def tiles(f, write):
                    for t in range(TILES):
                        act.wait_ge(dense_ready, f * TILES + (t + 1))
                        write(t, dense[:, t % 2, 0:TW])

                act.wait_ge(params_landed, PARAMS)
                nc.scalar.activation(small[AT_G:AT_G + 4, S_NEGA:S_NEGA + 1],
                                     small[AT_G:AT_G + 4, S_NEGA:S_NEGA + 1], ACT.Exp).then_inc(act_done, 1)

                def special(t, tile):
                    mm = nc.scalar.copy(X[:, 0, t * TW:(t + 1) * TW], tile)
                    mm.then_inc(act_free, 1)
                tiles(F_SPECIAL, special)
                act.wait_ge(act_free, TILES)
                nc.scalar.activation(X[AT_B:AT_B + 4, 0, 0:NT], X[AT_B:AT_B + 4, 0, 0:NT], ACT.Exp,
                                     scale=-1.0).then_inc(special_ready, 1)
                for n in range(3):
                    act.wait_ge(dve_done, n + 1)
                    rows = slice(AT_G, AT_G + 4) if n == 0 else slice(0, P)
                    nc.scalar.activation(T[rows, 0:NT] if n == 0 else X[:, 1, 0:NT],
                                         T[rows, 0:NT] if n == 0 else X[:, 1, 0:NT], ACT.Exp,
                                         scale=-1.0).then_inc(act_done, 1)
                    act.wait_ge(act_done, 2 * n + 2)
                    nc.scalar.activation(T[rows, 0:NT] if n == 0 else X[:, 1, 0:NT],
                                         T[rows, 0:NT] if n == 0 else X[:, 1, 0:NT], ACT.Ln,
                                         bias=1.0).then_inc(act_done, 1)
                act.wait_ge(special_stored, 3 * 16)

                def copy_block(i, f, p, scale=1.0):
                    def write(t, tile):
                        out = Y[:, p, t * TW:(t + 1) * TW]
                        nc.scalar.mul(out, tile, scale).then_inc(act_free, 1)
                    tiles(f, write)

                copy_block(0, F_COPY, 1, 0.125)
                copy_block(0, F_COPY + 1, 0, 0.125)
                with act.Fori(1, 4) as i:
                    for p in (1, 0):
                        act.wait_ge(copy_stored[p], i * 16)
                        copy_block(i, i * 2 + (F_COPY + 1 - p), p)

                def sigmoid_tiles(f, m):
                    def write(t, tile):
                        if not (isinstance(m, int) and m == 0 and t < 2):
                            act.wait_ge(dve_free, m * TILES + (t - 1))
                        nc.scalar.activation(sig[:, t % 2], tile, ACT.Sigmoid).then_inc(sig_ready, 1)
                    tiles(f, write)

                sigmoid_tiles(F_SILU, 0)
                sigmoid_tiles(F_SILU + 1, 1)
                with act.Fori(1, 4) as i:
                    sigmoid_tiles(i * 2 + F_SILU, i * 2)
                    sigmoid_tiles(i * 2 + (F_SILU + 1), i * 2 + 1)

                for g in range(4):
                    f = F_POOL + 2 * g
                    if g >= 1:
                        act.wait_ge(pool_d_ready, g)

                    def write(t, tile):
                        if t < TILES - 1:
                            nc.scalar.copy(X[:, 0, POOL_HALO + t * TW:POOL_HALO + (t + 1) * TW],
                                           tile).then_inc(act_free, 1)
                        else:
                            cut = NP_ - t * TW
                            nc.scalar.copy(X[:, 0, POOL_HALO + t * TW:POOL_HALO + NP_], tile[:, 0:cut])
                            nc.scalar.copy(X[:, 0, 2 * POOL_HALO + NP_:2 * POOL_HALO + NT],
                                           tile[:, cut:TW]).then_inc(act_free, 1)
                    tiles(f, write)
                    sigmoid_tiles(f + 1, 8 + g)

                def conv_block(p):
                    def write(t, tile):
                        if t < TILES - 1:
                            nc.scalar.copy(X[:, p, CONV_HALO + t * TW:CONV_HALO + (t + 1) * TW],
                                           tile).then_inc(act_free, 1)
                        else:
                            cut = NP_ - t * TW
                            nc.scalar.copy(X[:, p, CONV_HALO + t * TW:CONV_HALO + NP_], tile[:, 0:cut])
                            nc.scalar.copy(X[:, p, 2 * CONV_HALO + NP_:2 * CONV_HALO + NT],
                                           tile[:, cut:TW]).then_inc(act_free, 1)
                    return write

                def conv_sigmoid(j, p):
                    act.wait_ge(conv_ready, j + 1)
                    nc.scalar.activation(T[:, 0:NT], Y[:, p, 0:NT], ACT.Sigmoid).then_inc(conv_sig_ready, 1)

                def squares(j, p):
                    act.wait_ge(conv_silu_ready, j + 1)
                    nc.scalar.activation(T[:, 0:NT], Y[:, p, 0:NT], ACT.Square).then_inc(squares_ready, 1)

                def norm_logs(j, t):
                    act.wait_ge(side_ready, j * TILES + (6 * TILES + t + 1))
                    nc.scalar.activation(T[:, t * TW:(t + 1) * TW], side[:, t % 2, 0:TW], ACT.Ln,
                                         bias=small[:, S_EPS:S_EPS + 1]).then_inc(norm_free, 1)

                def norm_exp(j, q_scale):
                    act.wait_ge(norm_free, j * TILES + TILES)
                    if q_scale:
                        nc.scalar.activation(T[:, 0:NT], T[:, 0:NT], ACT.Exp, scale=-0.5,
                                             bias=small[:, S_QS:S_QS + 1]).then_inc(norm_ready, 1)
                    else:
                        nc.scalar.activation(T[:, 0:NT], T[:, 0:NT], ACT.Exp,
                                             scale=-0.5).then_inc(norm_ready, 1)

                def conv_slot(j, p, normed=None, square=True):
                    write = conv_block(p)
                    if normed is not None:
                        for t in range(TILES):
                            norm_logs(j - 2, t)
                    at_least(act, conv_ready, j - 1)
                    for t in range(TILES):
                        act.wait_ge(dense_ready, j * TILES + (F_CONV * TILES + t + 1))
                        write(t, dense[:, t % 2, 0:TW])
                        if t == 0 and normed is not None:
                            norm_exp(j - 2, normed)
                        if t == 3 and not (isinstance(j, int) and j == 0):
                            at_least(act, qkv_ready, j - 1)
                            conv_sigmoid(j - 1, 1 - p)
                        if t == 4 and square:
                            squares(j - 1, 1 - p)

                act.wait_ge(halo_set, 1)
                act.wait_ge(side_free, 6 * TILES)
                conv_slot(0, 1, square=False)
                conv_slot(1, 0)
                with act.Fori(0, 2) as i:
                    conv_slot(i * 2 + 2, 1, True)
                    conv_slot(i * 2 + 3, 0, True)
                conv_slot(6, 1, False)
                conv_slot(7, 0, False)
                conv_slot(8, 1, False)
                conv_slot(9, 0, False, square=False)
                conv_slot(10, 1, square=False)
                conv_slot(11, 0, square=False)

                def gate_block(i, f, p):
                    def write(t, tile):
                        nc.scalar.activation(Y[:, p, t * TW:(t + 1) * TW], tile,
                                             ACT.Sigmoid).then_inc(act_free, 1)
                    tiles(f, write)

                act.wait_ge(qkv_ready, 11)
                conv_sigmoid(11, 0)
                act.wait_ge(qkv_stored[1], 6 * 16)
                gate_block(0, F_GATE, 1)
                act.wait_ge(qkv_stored[0], 6 * 16)
                gate_block(0, F_GATE + 1, 0)
                with act.Fori(1, 12) as i:
                    for p in (1, 0):
                        act.wait_ge(gate_stored[p], i * 16)
                        gate_block(i, i * 2 + (F_GATE + 1 - p), p)

            @block.vector
            def _(dve):
                dve.wait_ge(params_landed, PARAMS)
                g_rows = slice(AT_G, AT_G + 4)
                b_rows = slice(AT_B, AT_B + 4)
                dve.wait_ge(special_ready, 1)
                links = [0]

                def link(ins):
                    links[0] += 1
                    ins.then_inc(special_step, 1)
                    dve.wait_ge(special_step, links[0])

                link(nc.vector.tensor_scalar(X[g_rows, 0, 0:NT], X[g_rows, 0, 0:NT],
                                             small[g_rows, S_DT:S_DT + 1], None, ALU.add))
                nc.vector.scalar_tensor_tensor(T[g_rows, 0:NT], X[g_rows, 0, 0:NT], -1.0, X[g_rows, 0, 0:NT],
                                               ALU.mult, ALU.max).then_inc(dve_done, 1)
                link(nc.vector.tensor_scalar(X[b_rows, 0, 0:NT], X[b_rows, 0, 0:NT], 1.0, None, ALU.add))
                nc.vector.reciprocal(X[b_rows, 0, 0:NT], X[b_rows, 0, 0:NT])
                dve.wait_ge(act_done, 3)
                link(nc.vector.scalar_tensor_tensor(X[g_rows, 0, 0:NT], X[g_rows, 0, 0:NT], 0.0,
                                                    T[g_rows, 0:NT], ALU.max, ALU.add))
                link(nc.vector.tensor_scalar(X[g_rows, 0, 0:NT], X[g_rows, 0, 0:NT],
                                             small[g_rows, S_NEGA:S_NEGA + 1], -1.0, ALU.mult, ALU.mult))
                for b in range(2):
                    for t in range(TILES):
                        n = b * TILES + t
                        dve.wait_ge(side_ready, n + 1)
                        nc.vector.tensor_scalar(T[:, t * TW:(t + 1) * TW], side[:, n % 2, 0:TW],
                                                small[:, S_BF + b:S_BF + b + 1], None,
                                                ALU.add).then_inc(side_free, 1)
                    dve.wait_ge(side_free, (b + 1) * TILES)
                    nc.vector.tensor_scalar(Y[:, b, 0:NT], T[:, 0:NT], 0.0, None, ALU.min)
                    nc.vector.scalar_tensor_tensor(X[:, 1, 0:NT], T[:, 0:NT], -1.0, T[:, 0:NT],
                                                   ALU.mult, ALU.max).then_inc(dve_done, 1)
                    dve.wait_ge(act_done, 5 + 2 * b)
                    nc.vector.tensor_tensor(Y[:, b, 0:NT], Y[:, b, 0:NT], X[:, 1, 0:NT],
                                            ALU.subtract).then_inc(logf_ready, 1)

                def silu_block(f, m, p):
                    for t in range(TILES):
                        dve.wait_ge(sig_ready, m * TILES + (t + 1))
                        b = f - F_SILU
                        nc.vector.scalar_tensor_tensor(Y[:, p, t * TW:(t + 1) * TW], dense[:, t % 2, 0:TW],
                                                       column(small, b + S_ZNORM), sig[:, t % 2],
                                                       ALU.mult, ALU.mult).then_inc(dve_free, 1)

                dve.wait_ge(copy_stored[1], 4 * 16)
                silu_block(F_SILU, 0, 1)
                dve.wait_ge(copy_stored[0], 4 * 16)
                silu_block(F_SILU + 1, 1, 0)
                with dve.Fori(1, 4) as i:
                    for p in (1, 0):
                        dve.wait_ge(silu_stored[p], i * 16)
                        silu_block(i * 2 + (F_SILU + 1 - p), i * 2 + (1 - p), p)

                def step(ins):
                    steps[0] += 1
                    ins.then_inc(pool_step, 1)
                    dve.wait_ge(pool_step, steps[0])
                steps = [0]
                dve.wait_ge(special_stored, 3 * 16)
                dve.wait_ge(silu_stored[0], 4 * 16)
                dve.wait_ge(silu_stored[1], 4 * 16)
                for g in range(4):
                    win = 2 << g
                    span = NT + 2 * POOL_HALO
                    dve.wait_ge(act_free, (A_POOL + g) * TILES + TILES)
                    U = X[:, 0]
                    nc.vector.memset(U[:, 0:POOL_HALO], 0.0)
                    step(nc.vector.tensor_copy(U[:, POOL_HALO + NP_:2 * POOL_HALO + NP_],
                                               pool_out[:, 1, g]))
                    nc.vector.tensor_copy(pool_out[:, 0, g], U[:, NP_:NP_ + POOL_HALO])
                    step(nc.vector.tensor_copy(pool_out[:, 1, g], U[:, NT + POOL_HALO:NT + 2 * POOL_HALO]))
                    src, w = U, 1
                    turn = [T, X[:, 1]]
                    for n in range(g + 1):
                        dst = turn[(g - n) % 2]
                        step(nc.vector.tensor_tensor(dst[:, 2 * w - 1:span], src[:, 2 * w - 1:span],
                                                     src[:, w - 1:span - w], ALU.add))
                        src, w = dst, 2 * w
                    step(nc.vector.scalar_tensor_tensor(
                        src[:, POOL_HALO:POOL_HALO + win - 1], src[:, POOL_HALO:POOL_HALO + win - 1],
                        float(win), consts[:, C_CNT:C_CNT + win - 1], ALU.mult, ALU.mult))
                    D = X[:, 1]
                    nc.vector.scalar_tensor_tensor(D[:, 0:NP_], src[:, POOL_HALO:POOL_HALO + NP_], 1.0 / win,
                                                   U[:, POOL_HALO:POOL_HALO + NP_], ALU.mult, ALU.subtract)
                    nc.vector.scalar_tensor_tensor(
                        D[:, NP_:NT], src[:, 2 * POOL_HALO + NP_:2 * POOL_HALO + NT], 1.0 / win,
                        U[:, 2 * POOL_HALO + NP_:2 * POOL_HALO + NT], ALU.mult,
                        ALU.subtract).then_inc(pool_d_ready, 1)
                    for t in range(TILES):
                        dve.wait_ge(sig_ready, (8 + g) * TILES + t + 1)
                        nc.vector.tensor_tensor(Y[:, 0, t * TW:(t + 1) * TW], dense[:, t % 2, 0:TW],
                                                sig[:, t % 2], ALU.mult).then_inc(dve_free, 1)
                    if g >= 1:
                        dve.wait_ge(pool_stored, 16 * g)
                    for t in range(TILES):
                        n = (2 + g) * TILES + t
                        dve.wait_ge(side_ready, n + 1)
                        nc.vector.scalar_tensor_tensor(
                            Y[:, 1, t * TW:(t + 1) * TW], side[:, n % 2, 0:TW],
                            small[:, S_PSCALE + g:S_PSCALE + g + 1], Y[:, 0, t * TW:(t + 1) * TW],
                            ALU.mult, ALU.mult).then_inc(side_free, 1)

                for p in range(2):
                    last = nc.vector.memset(X[:, p, 0:CONV_HALO], 0.0)
                last.then_inc(halo_set, 1)
                SLOT_LINKS = 4

                def conv(j, p, stored=None):
                    def tap(n, ins):
                        ins.then_inc(conv_step, 1)
                        dve.wait_ge(conv_step, j * SLOT_LINKS + n)

                    dve.wait_ge(act_free, j * TILES + (A_CONV * TILES + TILES))
                    tap(1, nc.vector.tensor_copy(X[:, p, CONV_HALO + NP_:2 * CONV_HALO + NP_],
                                                 conv_cache[:, bass.ds(j, 1), :].rearrange("p a b -> p (a b)")))
                    for s, end in ((0, CONV_HALO + NP_), (1, 2 * CONV_HALO + NT)):
                        nc.vector.tensor_copy(conv_out[:, s, bass.ds(j, 1), :].rearrange("p a b -> p (a b)"),
                                              X[:, p, end - CONV_HALO:end])
                    if stored is not None:
                        dve.wait_ge(qkv_stored[p], stored)

                    def w(i):
                        return small[:, bass.ds(j * 4 + (S_CONV + i), 1)]
                    runs = ((0, NP_, 0), (NP_, NT, CONV_HALO))
                    for i in range(4):
                        for a, b, off in runs:
                            src = X[:, p, a + off + i:b + off + i]
                            if i == 0:
                                ins = nc.vector.tensor_scalar(Y[:, p, a:b], src, w(0), None, ALU.mult)
                            else:
                                ins = nc.vector.scalar_tensor_tensor(Y[:, p, a:b], src, w(i), Y[:, p, a:b],
                                                                     ALU.mult, ALU.add)
                        if i < 3:
                            tap(2 + i, ins)
                        else:
                            ins.then_inc(conv_ready, 1)

                def conv_silu(j, p, last=False):
                    dve.wait_ge(conv_sig_ready, j + 1)
                    ins = nc.vector.tensor_tensor(Y[:, p, 0:NT], Y[:, p, 0:NT], T[:, 0:NT], ALU.mult)
                    ins.then_inc(qkv_ready if last else conv_silu_ready, 1)

                def conv_norm(j, p):
                    dve.wait_ge(norm_ready, j + 1)
                    nc.vector.tensor_tensor(Y[:, p, 0:NT], Y[:, p, 0:NT], T[:, 0:NT],
                                            ALU.mult).then_inc(qkv_ready, 1)

                dve.wait_ge(pool_stored, 4 * 16)
                conv(0, 1)
                conv_silu(0, 1)
                conv(1, 0)
                conv_norm(0, 1)
                conv_silu(1, 0)
                with dve.Fori(0, 3) as i:
                    conv(i * 2 + 2, 1, i * 16 + 16)
                    conv_norm(i * 2 + 1, 0)
                    conv_silu(i * 2 + 2, 1)
                    conv(i * 2 + 3, 0, i * 16 + 16)
                    conv_norm(i * 2 + 2, 1)
                    conv_silu(i * 2 + 3, 0)
                conv(8, 1, 4 * 16)
                conv_norm(7, 0)
                conv_silu(8, 1, last=True)
                conv(9, 0, 4 * 16)
                conv_silu(9, 0, last=True)
                conv(10, 1, 5 * 16)
                conv_silu(10, 1, last=True)
                conv(11, 0, 5 * 16)
                conv_silu(11, 0, last=True)

            @block.sync
            def _(sp):
                def load(i, f, p):
                    sp.dma_start(w_raw[:, p], d["w_in"][bass.ds(f, 1)].rearrange("a p n -> p (a n)")) \
                        .then_inc(w_landed[p], 16)

                load(0, 0, 0)
                for dst, src in (
                        (small[:, S_BF:S_BF + 2], d["gla_bf"]),
                        (small[:, S_PSCALE:S_PSCALE + 4], d["pool_scale"]),
                        (small[:, S_ZNORM:S_ZNORM + 4], d["gla_norm"]),
                        (small[:, S_ZNORM + 4:S_ZNORM + 8], d["gdn_norm"]),
                        (small[:, S_CONV:S_CONV + 48], d["gdn_conv"]),
                        (small[:, S_EPS:S_EPS + 2], d["scalars"]),
                        (small[AT_G:AT_G + 4, S_NEGA:S_NEGA + 1], d["gdn_a_log"]),
                        (small[AT_G:AT_G + 4, S_DT:S_DT + 1], d["gdn_dt_bias"]),
                        (wf2[:, :], d["gla_wf2"]),
                        (pool_w[:, :, :], d["pool_w"]),
                        (conv_cache[:, :, :], d["conv_cache"]),
                        (pool_out[:, 1], d["pool_cache"]),
                ):
                    sp.dma_start(dst, src).then_inc(params_landed, 16)
                load(0, 1, 1)

                def load_next(f, p):
                    sp.wait_ge(w_split, f + 1)
                    load(None, f + 2, p)

                def store(dst, row, ready, count, stored):
                    sp.wait_ge(ready, count)
                    sp.dma_start(dst, row).then_inc(stored, 16)

                load_next(0, 0)
                store(feat[:, R_LOGF], Y[:, 0, 0:NT], logf_ready, 1, special_stored)
                store(feat[:, R_LOGF + 1], Y[:, 1, 0:NT], logf_ready, 2, special_stored)
                store(feat[:, R_GB], X[:, 0, 0:NT], logf_ready, 2, special_stored)
                with sp.Fori(0, 4) as i:
                    for p in (1, 0):
                        load_next(i * 2 + (F_COPY + 1 - p), p)
                        sp.wait_ge(act_free, i * (2 * TILES) + (A_COPY + 2 - p) * TILES)
                        sp.dma_start(feat[:, bass.ds(i * 2 + (1 - p), 1)].rearrange("p a n -> p (a n)"),
                                     Y[:, p, 0:NT]).then_inc(copy_stored[p], 16)
                with sp.Fori(0, 4) as i:
                    for p in (1, 0):
                        load_next(i * 2 + (F_SILU + 1 - p), p)
                        sp.wait_ge(dve_free, i * (2 * TILES) + (2 - p) * TILES)
                        sp.dma_start(feat[:, bass.ds(i * 2 + (R_GLA_Z + 1 - p), 1)]
                                     .rearrange("p a n -> p (a n)"), Y[:, p, 0:NT]) \
                            .then_inc(silu_stored[p], 16)
                for g in range(4):
                    load_next(F_POOL + 2 * g, 1)
                    load_next(F_POOL + 2 * g + 1, 0)
                    store(outs[:, 4 + g], Y[:, 1, 0:NT], side_free, (3 + g) * TILES, pool_stored)
                load_next(F_CONV, 1)
                load_next(F_CONV + 1, 0)
                with sp.Fori(0, 5) as i:
                    for p in (1, 0):
                        load_next(i * 2 + (F_CONV + 3 - p), p)
                        sp.wait_ge(qkv_ready, i * 2 + (2 - p))
                        sp.dma_start(feat[:, bass.ds(i * 2 + (R_GDN_Q + 1 - p), 1)]
                                     .rearrange("p a n -> p (a n)"), Y[:, p, 0:NT]) \
                            .then_inc(qkv_stored[p], 16)
                load_next(F_GATE, 1)
                store(feat[:, R_GDN_V + 2], Y[:, 1, 0:NT], qkv_ready, 11, qkv_stored[1])
                load_next(F_GATE + 1, 0)
                store(feat[:, R_GDN_V + 3], Y[:, 0, 0:NT], qkv_ready, 12, qkv_stored[0])
                sp.dma_start(d["new_pool_prompt"], pool_out[:, 0]).then_inc(caches_stored, 16)
                sp.dma_start(d["new_pool_sample"], pool_out[:, 1]).then_inc(caches_stored, 16)
                sp.dma_start(d["new_conv_prompt"], conv_out[:, 0]).then_inc(caches_stored, 16)
                sp.dma_start(d["new_conv_sample"], conv_out[:, 1]).then_inc(caches_stored, 16)
                with sp.Fori(0, 10) as i:
                    for p in (1, 0):
                        load_next(i * 2 + (F_GATE + 3 - p), p)
                        sp.wait_ge(act_free, i * (2 * TILES) + (A_GATE + 2 - p) * TILES)
                        sp.dma_start(gates[:, bass.ds(i * 2 + (1 - p), 1)].rearrange("p a n -> p (a n)"),
                                     Y[:, p, 0:NT]).then_inc(gate_stored[p], 16)
                for n in range(20, 24):
                    p = 1 - n % 2
                    store(gates[:, n], Y[:, p, 0:NT], act_free, (A_GATE + n + 1) * TILES, gate_stored[p])
                sp.wait_ge(caches_stored, 4 * 16)
                for p in range(2):
                    sp.wait_ge(gate_stored[p], 12 * 16)


def chunk_phase(nc, d, consts):
    UPDATES = 2 * (LEVELS - 1) - 1
    with ExitStack() as ctx, Held(nc) as held:
        def sb(name, shape, dt=F32):
            return ctx.enter_context(nc.sbuf_tensor(name, shape, dt))

        def bank(name, shape=(P, HEADS, P)):
            return ctx.enter_context(nc.psum_tensor(name, list(shape), F32))

        masks = sb("masks", [P, M_END])
        eps = sb("chunk_eps", [P, 1])
        inputs = sb("inputs", [P, 2, R_END, P])
        decay_beta = sb("decay_beta", [P, 2, HEADS])
        g_col = sb("g_col", [P, HEADS])
        g_row = sb("g_row", [P, HEADS, P])
        e_row = sb("e_row", [P, HEADS, P])
        d_col = sb("d_col", [P, HEADS])
        diff = sb("diff", [P, HEADS, P])
        dec_kk = sb("dec_kk", [P, HEADS, P])
        dec_qk = sb("dec_qk", [P, HEADS, P])
        M = sb("M", [P, HEADS, P])
        M0 = sb("M0", [P, HEADS, P])
        X = sb("X", [P, HEADS, P])
        XT = sb("XT", [P, HEADS, P])
        XTb = sb("XTb", [P, HEADS, P])
        Z = sb("Z", [P, HEADS, P])
        att = sb("att", [P, HEADS, P])
        k_dec = sb("k_dec", [P, HEADS, P])
        q_dec = sb("q_dec", [P, HEADS, P])
        k_tok = sb("k_tok", [P, HEADS, P])
        v_tok = sb("v_tok", [P, HEADS, P])
        rhs = sb("rhs", [P, HEADS, P])
        U = sb("U", [P, HEADS, P])
        state = sb("state", [P, HEADS, P])
        b_sum = sb("b_sum", [P, 2, P])
        F = sb("F", [P, LEVELS + 2, 2, P])
        KF = sb("KF", [P, LEVELS + 1, 2, P])
        QF = sb("QF", [P, LEVELS + 1, 2, P])
        masked = sb("masked", [P, LEVELS + 1, P])
        gla_att = sb("gla_att", [P, HEADS, P])
        gla_v = sb("gla_v", [P, HEADS, P])
        gla_k = sb("gla_k", [P, 2, P])
        gla_state = sb("gla_state", [P, HEADS, P])
        sq = [sb("sq_gdn", [P, HEADS, P]), sb("sq_gla", [P, HEADS, P])]
        oz = [sb("oz_gdn", [P, HEADS, P]), sb("oz_gla", [P, HEADS, P])]
        out_sb = [sb("out_gdn", [P, HEADS, P]), sb("out_gla", [P, HEADS, P])]

        z_bank = bank("z_bank")
        xt_bank = bank("xt_bank")
        x_bank = bank("x_bank")
        pair_bank = bank("pair_bank", (P, LEVELS + 1, P))
        ring = [bank("ring0"), bank("ring1"), bank("ring2")]

        ident = consts[:, C_IDENT:C_IDENT + P]
        ones = consts[:, C_ONES:C_ONES + P]
        upper = masks[:, M_UPPER:M_UPPER + P]

        ITEMS = ("gbt", "gcol", "vt", "kt", "grow", "KK", "QK", "vtg", "m0t", "R", "kdtg", "Og", "U", "O", "dS",
                 "dSg", "SSQ", "SSQg")
        PE_ = ITEMS
        DVE_ = ("gb_taken", "gcol_taken", "kt_taken", "KK_taken", "QK_taken", "m0t_taken", "R_taken",
                "O_scaled", "Og_scaled", "dS_taken", "dSg_taken", "b_ready", "F_diffs", "KF_ready",
                "XTb_ready", "gla_att_ready", "dcol_diff")
        ACT_ = ("vt_taken", "grow_taken", "e_row_ready", "d_col_ready", "dec_qk_ready", "dec_kk_ready",
                "vtg_taken", "kdtg_taken", "U_taken", "F_abs", "F_ready", "O_squared", "Og_squared", "SSQ_taken",
                "SSQg_taken", "rs_ready", "rsg_ready")
        POOL_ = ("diff_ready", "dec_args", "M0_ready", "X_ready", "k_dec_ready", "q_dec_ready", "QF_ready",
                 "out_ready", "outg_ready")
        EARLY = {"SSQ_taken", "SSQg_taken", "dSg_taken", "dSg", "dS_taken", "O", "Og", "out_ready", "outg_ready",
                 "R_taken", "dec_args", "KK_taken", "QK_taken", "QF_ready", "q_dec_ready", "kdtg"}
        S = {n: held.add(nc.alloc_semaphore(n)) for n in PE_ + DVE_ + ACT_ + POOL_}
        z_ready = held.add(nc.alloc_semaphore("z_ready"))
        z_taken = held.add(nc.alloc_semaphore("z_taken"))
        x_products = held.add(nc.alloc_semaphore("x_products"))
        x_updated = held.add(nc.alloc_semaphore("x_updated"))
        pairs_ready = held.add(nc.alloc_semaphore("pairs_ready"))
        pairs_masked = held.add(nc.alloc_semaphore("pairs_masked"))
        in_landed = [held.add(nc.alloc_semaphore(f"in_landed{p}")) for p in range(2)]
        masks_landed = held.add(nc.alloc_semaphore("masks_landed"))
        eps_ready = held.add(nc.alloc_semaphore("eps_ready"))
        state_landed = held.add(nc.alloc_semaphore("state_landed"))
        state_stored = held.add(nc.alloc_semaphore("state_stored"))
        state_zero = held.add(nc.alloc_semaphore("state_zero"))
        out_stored = held.add(nc.alloc_semaphore("out_stored"))
        outg_stored = held.add(nc.alloc_semaphore("outg_stored"))
        feat, outs = d["feat"], d["branch_out"]

        def now(eng, name, c):
            eng.wait_ge(S[name], c + (2 if name in EARLY else 1))

        def before(eng, name, c):
            assert name in EARLY, name
            eng.wait_ge(S[name], c + 1)

        def preload(eng, names):
            for name in names:
                if name in EARLY:
                    eng.sem_inc(S[name], 1)

        def half_of(h):
            return slice(64 * (h % 2), 64 * (h % 2) + 64)

        def levels_of(n):
            return n.bit_length() - 1

        with nc.Block() as block:
            @block.sync
            def _(sp):
                def load(c, p, n=P):
                    sp.dma_start(inputs[:, p, :, 0:n], feat[:, :, bass.ds(c * P, n)]).then_inc(in_landed[p], 16)

                def store(c, n=P):
                    now(sp, "outg_ready", c)
                    sp.dma_start(outs[:, 0:4, bass.ds(c * P, n)], out_sb[1][:, :, 0:n]).then_inc(outg_stored, 16)
                    now(sp, "out_ready", c)
                    sp.dma_start(outs[:, 8:12, bass.ds(c * P, n)], out_sb[0][:, :, 0:n]).then_inc(out_stored, 16)

                sp.sem_inc(out_stored, 16)
                sp.sem_inc(outg_stored, 16)
                load(0, 0)
                sp.dma_start(masks[:, :], d["masks"]).then_inc(masks_landed, 16)
                load(1, 1)
                with sp.Fori(0, CHUNKS // 2 - 1) as i:
                    for p in range(2):
                        c = i * 2 + p
                        store(c)
                        load(i * 2 + (p + 2), p)
                store(CHUNKS - 2)
                load(CHUNKS, 0, NS_)
                store(CHUNKS - 1)
                now(sp, "dS_taken", CHUNKS - 1)
                now(sp, "dSg_taken", CHUNKS - 1)
                sp.dma_start(d["new_gdn_prompt"].rearrange("h d v -> d h v"), state[:, :, :]).then_inc(state_stored, 16)
                for h in range(HEADS):
                    sp.dma_start(d["new_gla_prompt"][h], gla_state[half_of(h), h]).then_inc(state_stored, 16)
                sp.wait_ge(state_stored, 5 * 16)
                sp.dma_start(state[:, :, :], d["state_gdn"].rearrange("h d v -> d h v")).then_inc(state_landed, 16)
                for h in range(HEADS):
                    sp.dma_start(gla_state[half_of(h), h], d["state_gla"][h]).then_inc(state_landed, 16)
                store(CHUNKS, NS_)
                now(sp, "dS_taken", CHUNKS)
                now(sp, "dSg_taken", CHUNKS)
                sp.dma_start(d["new_gdn_sample"].rearrange("h d v -> d h v"), state[:, :, :]).then_inc(state_stored, 16)
                for h in range(HEADS):
                    sp.dma_start(d["new_gla_sample"][h], gla_state[half_of(h), h]).then_inc(state_stored, 16)
                sp.wait_ge(state_stored, 10 * 16)
                sp.wait_ge(out_stored, 16 * (CHUNKS + 2))
                sp.wait_ge(outg_stored, 16 * (CHUNKS + 2))

            def per_chunk(eng, chunk):
                with eng.Fori(0, CHUNKS // 2) as i:
                    chunk(i * 2, i, 0, P)
                    chunk(i * 2 + 1, i, 1, P)
                chunk(CHUNKS, CHUNKS // 2, 0, NS_)

            @block.tensor
            def _(pe):
                matmul, transpose = nc.tensor.matmul, nc.tensor.transpose

                def chunk(c, i, p, n):
                    I = inputs[:, p]
                    L = levels_of(n)
                    pe.wait_ge(in_landed[p], i * 16 + 16)
                    before(pe, "SSQ_taken", c)
                    transpose(ring[0][0:n, 0], I[:, R_GB, 0:n], ident).then_inc(S["gbt"], 1)
                    before(pe, "SSQg_taken", c)
                    for h in range(HEADS):
                        mm = transpose(ring[1][0:n, h], I[:, R_GDN_V + h, 0:n], ident)
                    mm.then_inc(S["vt"], 1)
                    before(pe, "dSg_taken", c)
                    for h in range(HEADS):
                        mm = transpose(ring[2][0:n, h], I[:, R_GDN_K + h, 0:n], ident)
                    mm.then_inc(S["kt"], 1)
                    now(pe, "gb_taken", c)
                    matmul(ring[0][0:n, 1, 0:HEADS], upper[0:n, 0:n], decay_beta[0:n, 0, :],
                           start=True, stop=True).then_inc(S["gcol"], 1)
                    now(pe, "gcol_taken", c)
                    for h in range(HEADS):
                        mm = matmul(ring[0][:, h, 0:n], decay_beta[0:n, 0, h:h + 1].to_broadcast([n, P]),
                                    upper[0:n, 0:n], start=True, stop=True)
                    mm.then_inc(S["grow"], 1)
                    now(pe, "vt_taken", c)
                    for h in range(HEADS):
                        k = I[:, R_GDN_K + h, 0:n]
                        mm = matmul(ring[1][0:n, h, 0:n], k, k, start=True, stop=True)
                    mm.then_inc(S["KK"], 1)
                    now(pe, "kt_taken", c)
                    for h in range(HEADS):
                        mm = matmul(ring[2][0:n, h, 0:n], I[:, R_GDN_K + h, 0:n], I[:, R_GDN_Q + h, 0:n],
                                    start=True, stop=True)
                    mm.then_inc(S["QK"], 1)
                    now(pe, "grow_taken", c)
                    for h in range(HEADS):
                        mm = transpose(ring[0][0:n, h], I[:, R_GLA_V + h, 0:n], ident)
                    mm.then_inc(S["vtg"], 1)
                    now(pe, "M0_ready", c)
                    now(pe, "KK_taken", c)
                    for h in range(HEADS):
                        mm = transpose(ring[1][0:n, h, 0:n], M0[0:n, h, 0:n], ident[0:n, 0:n])
                    mm.then_inc(S["m0t"], 1)
                    now(pe, "QK_taken", c)
                    now(pe, "k_dec_ready", c)
                    before(pe, "dS_taken", c)
                    if isinstance(c, int) and c == CHUNKS:
                        pe.wait_ge(state_landed, 5 * 16)
                    for h in range(HEADS):
                        mm = matmul(ring[2][0:n, h], k_dec[:, h, 0:n], state[:, h], start=True, stop=True)
                    mm.then_inc(S["R"], 1)

                    def pairs(h):
                        rows = half_of(h)
                        b = h // 2
                        if h == 0:
                            now(pe, "KF_ready", c)
                            now(pe, "QF_ready", c)
                            pe.wait_ge(pairs_masked, c * HEADS + 1)
                        else:
                            pe.wait_ge(pairs_masked, c * HEADS + h + 1)
                        matmul(pair_bank[0:n, 0, 0:n], I[rows, R_GLA_K + b, 0:n], I[rows, R_GLA_Q + b, 0:n],
                               start=True, stop=True)
                        for l in range(L):
                            mm = matmul(pair_bank[0:n, l + 1, 0:n], KF[rows, l, b, 0:n], QF[rows, l + 1, b, 0:n],
                                        start=True, stop=True)
                        mm.then_inc(pairs_ready, 1)

                    def key_turns():
                        now(pe, "vtg_taken", c)
                        for b in range(2):
                            mm = transpose(ring[0][0:n, b], KF[:, LEVELS, b, 0:n], ident)
                        mm.then_inc(S["kdtg"], 1)

                    between = {0: lambda: pairs(0), 1: lambda: pairs(1), 2: lambda: pairs(2),
                               3: lambda: pairs(3), 4: key_turns}
                    for l in range(1, L):
                        if l == 1:
                            now(pe, "m0t_taken", c)
                            now(pe, "X_ready", c)
                        else:
                            pe.wait_ge(x_updated, c * UPDATES + 2 * (l - 1))
                        for h in range(HEADS):
                            mm = matmul(z_bank[0:n, h, 0:n], M[0:n, h, 0:n], XT[0:n, h, 0:n], start=True, stop=True)
                        mm.then_inc(z_ready, 1)
                        if l - 1 in between:
                            between[l - 1]()
                        pe.wait_ge(z_taken, c * (LEVELS - 1) + l)
                        for h in range(HEADS):
                            mm = matmul(xt_bank[0:n, h, 0:n], X[0:n, h, 0:n], Z[0:n, h, 0:n],
                                        start=True, stop=True)
                        if l < L - 1:
                            for h in range(HEADS):
                                mm = matmul(x_bank[0:n, h, 0:n], Z[0:n, h, 0:n], X[0:n, h, 0:n],
                                            start=True, stop=True)
                        mm.then_inc(x_products, 1)
                    if L - 1 < 5:
                        key_turns()
                    now(pe, "gla_att_ready", c)
                    now(pe, "m0t_taken", c)
                    before(pe, "dSg_taken", c)
                    for h in range(HEADS):
                        matmul(ring[1][:, h, 0:n], gla_v[0:n, h], gla_att[0:n, h, 0:n], start=True, stop=False)
                        mm = matmul(ring[1][:, h, 0:n], gla_state[:, h], QF[:, 0, h // 2, 0:n],
                                    start=False, stop=True)
                    mm.then_inc(S["Og"], 1)
                    now(pe, "R_taken", c)
                    now(pe, "XTb_ready", c)
                    for h in range(HEADS):
                        mm = matmul(ring[2][0:n, h], XTb[0:n, h, 0:n], rhs[0:n, h], start=True, stop=True)
                    mm.then_inc(S["U"], 1)
                    now(pe, "kdtg_taken", c)
                    now(pe, "q_dec_ready", c)
                    now(pe, "U_taken", c)
                    for h in range(HEADS):
                        matmul(ring[0][:, h, 0:n], U[0:n, h], att[0:n, h, 0:n], start=True, stop=False)
                        mm = matmul(ring[0][:, h, 0:n], state[:, h], q_dec[:, h, 0:n], start=False, stop=True)
                    mm.then_inc(S["O"], 1)
                    now(pe, "Og_scaled", c)
                    now(pe, "Og_squared", c)
                    for h in range(HEADS):
                        mm = matmul(ring[1][:, h], k_tok[0:n, h], U[0:n, h], start=True, stop=True)
                    mm.then_inc(S["dS"], 1)
                    for h in range(HEADS):
                        mm = matmul(ring[2][:, h], gla_k[0:n, h // 2], gla_v[0:n, h], start=True, stop=True)
                    mm.then_inc(S["dSg"], 1)
                    now(pe, "O_scaled", c)
                    now(pe, "O_squared", c)
                    matmul(ring[0][:, :, 0:n], ones, sq[0][:, :, 0:n], start=True, stop=True).then_inc(S["SSQ"], 1)
                    now(pe, "dS_taken", c)
                    matmul(ring[1][:, :, 0:n], ones, sq[1][:, :, 0:n], start=True, stop=True).then_inc(S["SSQg"], 1)

                pe.wait_ge(masks_landed, 16)
                preload(pe, PE_)
                per_chunk(pe, chunk)

            @block.scalar
            def _(act):
                copy, activation = nc.scalar.copy, nc.scalar.activation

                def head_norm(c, n, which, ready, taken, done):
                    s = sq[which][:, :, 0:n]
                    now(act, ready, c)
                    activation(s, ring[which][:, :, 0:n], ACT.Ln, bias=eps[:, 0:1], scale=1.0 / P) \
                        .then_inc(S[taken], 1)
                    now(act, taken, c)
                    activation(s, s, ACT.Exp, scale=-0.5).then_inc(S[done], 1)

                def chunk(c, i, p, n):
                    L = levels_of(n)
                    now(act, "vt", c)
                    before(act, "R_taken", c)
                    copy(v_tok[0:n], ring[1][0:n]).then_inc(S["vt_taken"], 1)
                    now(act, "grow", c)
                    before(act, "dec_args", c)
                    copy(g_row[:, :, 0:n], ring[0][:, :, 0:n]).then_inc(S["grow_taken"], 1)
                    now(act, "grow_taken", c)
                    before(act, "dS_taken", c)
                    before(act, "q_dec_ready", c)
                    activation(e_row[:, :, 0:n], g_row[:, :, 0:n], ACT.Exp).then_inc(S["e_row_ready"], 1)
                    now(act, "dcol_diff", c)
                    activation(d_col[0:n], d_col[0:n], ACT.Exp).then_inc(S["d_col_ready"], 1)
                    now(act, "dec_args", c)
                    activation(dec_kk[0:n, :, 0:n], dec_kk[0:n, :, 0:n], ACT.Exp, scale=-1.0) \
                        .then_inc(S["dec_kk_ready"], 1)
                    activation(dec_qk[0:n, :, 0:n], dec_qk[0:n, :, 0:n], ACT.Exp) \
                        .then_inc(S["dec_qk_ready"], 1)
                    now(act, "F_diffs", c)
                    activation(F[:, :, :, 0:n], F[:, :, :, 0:n], ACT.Abs).then_inc(S["F_abs"], 1)
                    now(act, "F_abs", c)
                    activation(F[:, :, :, 0:n], F[:, :, :, 0:n], ACT.Exp, scale=-1.0 / 16).then_inc(S["F_ready"], 1)
                    now(act, "vtg", c)
                    before(act, "dSg", c)
                    copy(gla_v[0:n], ring[0][0:n]).then_inc(S["vtg_taken"], 1)
                    now(act, "kdtg", c)
                    copy(gla_k[0:n], ring[0][0:n, 0:2]).then_inc(S["kdtg_taken"], 1)
                    now(act, "Og", c)
                    before(act, "outg_ready", c)
                    activation(sq[1][:, :, 0:n], ring[1][:, :, 0:n], ACT.Square).then_inc(S["Og_squared"], 1)
                    now(act, "U", c)
                    copy(U[0:n], ring[2][0:n]).then_inc(S["U_taken"], 1)
                    now(act, "O", c)
                    before(act, "out_ready", c)
                    activation(sq[0][:, :, 0:n], ring[0][:, :, 0:n], ACT.Square).then_inc(S["O_squared"], 1)
                    head_norm(c, n, 0, "SSQ", "SSQ_taken", "rs_ready")
                    head_norm(c, n, 1, "SSQg", "SSQg_taken", "rsg_ready")

                act.wait_ge(eps_ready, 1)
                preload(act, ACT_)
                per_chunk(act, chunk)

            @block.gpsimd
            def _(pool):
                tt = nc.gpsimd.tensor_tensor

                def chunk(c, i, p, n):
                    I = inputs[:, p]

                    def over_heads(x):
                        return x.rearrange("p (a b) -> p a b", a=1).to_broadcast([n, HEADS, n])
                    now(pool, "grow_taken", c)
                    now(pool, "gcol_taken", c)
                    tt(diff[0:n, :, 0:n], g_row[0:n, :, 0:n],
                       g_col[0:n].rearrange("p (a b) -> p a b", b=1).to_broadcast([n, HEADS, n]),
                       ALU.subtract).then_inc(S["diff_ready"], 1)
                    now(pool, "diff_ready", c)
                    before(pool, "KK_taken", c)
                    tt(dec_kk[0:n, :, 0:n], diff[0:n, :, 0:n], over_heads(masks[0:n, M_POS:M_POS + n]), ALU.add)
                    before(pool, "QK_taken", c)
                    tt(dec_qk[0:n, :, 0:n], diff[0:n, :, 0:n], over_heads(masks[0:n, M_NEG:M_NEG + n]),
                       ALU.add).then_inc(S["dec_args"], 1)
                    now(pool, "e_row_ready", c)
                    before(pool, "O", c)
                    tt(k_dec[:, :, 0:n], I[:, R_GDN_K:R_GDN_K + 4, 0:n], e_row[:, :, 0:n],
                       ALU.mult).then_inc(S["k_dec_ready"], 1)
                    now(pool, "KK_taken", c)
                    tt(M0[0:n, :, 0:n], M[0:n, :, 0:n], over_heads(masks[0:n, M_LOW:M_LOW + n]),
                       ALU.mult).then_inc(S["M0_ready"], 1)
                    now(pool, "M0_ready", c)
                    tt(X[0:n, :, 0:n], over_heads(ident[0:n, 0:n]), M0[0:n, :, 0:n],
                       ALU.subtract).then_inc(S["X_ready"], 1)
                    now(pool, "F_ready", c)
                    before(pool, "Og", c)
                    q = I[:, R_GLA_Q:R_GLA_Q + 2, 0:n].rearrange("p (l b) t -> p l b t", l=1)
                    for b in range(2):
                        last = tt(QF[:, :, b, 0:n], q[:, :, b].to_broadcast([P, LEVELS + 1, n]),
                                  F[:, 0:LEVELS + 1, b, 0:n], ALU.mult)
                    last.then_inc(S["QF_ready"], 1)
                    tt(q_dec[:, :, 0:n], I[:, R_GDN_Q:R_GDN_Q + 4, 0:n], e_row[:, :, 0:n],
                       ALU.mult).then_inc(S["q_dec_ready"], 1)
                    now(pool, "rs_ready", c)
                    now(pool, "O_scaled", c)
                    pool.wait_ge(out_stored, c * 16 + 16)
                    tt(out_sb[0][:, :, 0:n], oz[0][:, :, 0:n], sq[0][:, :, 0:n], ALU.mult).then_inc(S["out_ready"], 1)
                    now(pool, "rsg_ready", c)
                    pool.wait_ge(outg_stored, c * 16 + 16)
                    tt(out_sb[1][:, :, 0:n], oz[1][:, :, 0:n], sq[1][:, :, 0:n], ALU.mult).then_inc(S["outg_ready"], 1)

                preload(pool, POOL_)
                per_chunk(pool, chunk)

            @block.vector
            def _(dve):
                tt, stt, cp = nc.vector.tensor_tensor, nc.vector.scalar_tensor_tensor, nc.vector.tensor_copy

                def chunk(c, i, p, n):
                    I = inputs[:, p]
                    L = levels_of(n)

                    def over_heads(x, m=HEADS):
                        return x.rearrange("p (a b) -> p a b", a=1).to_broadcast([n, m, n])

                    def per_token(x, w=P):
                        return x.rearrange("p (a b) -> p a b", b=1).to_broadcast([n, HEADS, w])
                    beta = decay_beta[0:n, 1]
                    dve.wait_ge(in_landed[p], i * 16 + 16)
                    for b in range(2):
                        last = nc.vector.tensor_tensor_scan(b_sum[:, b, 0:n], ones[:, 0:n], I[:, R_LOGF + b, 0:n],
                                                            0.0, ALU.mult, ALU.add)
                    last.then_inc(S["b_ready"], 1)
                    now(dve, "gbt", c)
                    cp(decay_beta[0:n], ring[0][0:n, 0].rearrange("p (a b) -> p a b", b=32)[:, 1:3, 0:HEADS]) \
                        .then_inc(S["gb_taken"], 1)
                    now(dve, "b_ready", c)
                    before(dve, "QF_ready", c)
                    for b in range(2):
                        bs = b_sum[:, b, 0:n]
                        cp(F[:, 0, b, 0:n], bs)
                        for l in range(LEVELS):
                            s = 1 << l
                            if l >= L:
                                cp(F[:, l + 1, b, 0:n], bs)
                                continue
                            blocks = bs.rearrange("p (m t) -> p m t", t=2 * s)
                            tt(F[:, l + 1, b, 0:n].rearrange("p (m t) -> p m t", t=2 * s), blocks,
                               blocks[:, :, s - 1:s].to_broadcast([P, n // (2 * s), 2 * s]), ALU.subtract)
                        last = tt(F[:, LEVELS + 1, b, 0:n], bs, bs[:, n - 1:n].to_broadcast([P, n]), ALU.subtract)
                    last.then_inc(S["F_diffs"], 1)
                    now(dve, "gcol", c)
                    cp(g_col[0:n], ring[0][0:n, 1, 0:HEADS]).then_inc(S["gcol_taken"], 1)
                    now(dve, "grow_taken", c)
                    now(dve, "gcol_taken", c)
                    tt(d_col[0:n], g_row[0:n, :, n - 1], g_col[0:n], ALU.subtract).then_inc(S["dcol_diff"], 1)
                    now(dve, "d_col_ready", c)
                    now(dve, "kt", c)
                    tt(k_tok[0:n], ring[2][0:n], per_token(d_col[0:n]), ALU.mult).then_inc(S["kt_taken"], 1)
                    now(dve, "KK", c)
                    now(dve, "dec_kk_ready", c)
                    for h in range(HEADS):
                        last = stt(M[0:n, h, 0:n], ring[1][0:n, h, 0:n], beta[:, h:h + 1], dec_kk[0:n, h, 0:n],
                                   ALU.mult, ALU.mult)
                    last.then_inc(S["KK_taken"], 1)
                    now(dve, "QK", c)
                    now(dve, "dec_qk_ready", c)
                    tt(att[0:n, :, 0:n], ring[2][0:n, :, 0:n], dec_qk[0:n, :, 0:n], ALU.mult).then_inc(S["QK_taken"], 1)
                    now(dve, "F_ready", c)
                    before(dve, "kdtg", c)
                    for b in range(2):
                        k = I[:, R_GLA_K + b:R_GLA_K + b + 1, 0:n].to_broadcast([P, LEVELS + 1, n])
                        last = tt(KF[:, :, b, 0:n], k, F[:, 1:LEVELS + 2, b, 0:n], ALU.mult)
                    last.then_inc(S["KF_ready"], 1)
                    now(dve, "m0t", c)
                    tt(XT[0:n, :, 0:n], over_heads(ident[0:n, 0:n]), ring[1][0:n, :, 0:n],
                       ALU.subtract).then_inc(S["m0t_taken"], 1)
                    now(dve, "R", c)
                    now(dve, "vt_taken", c)
                    tt(rhs[0:n], v_tok[0:n], ring[2][0:n], ALU.subtract).then_inc(S["R_taken"], 1)

                    def take_pairs(h):
                        dve.wait_ge(pairs_ready, c * HEADS + h + 1)
                        lt = masks[0:n, M_LOWT:M_END].rearrange("p (l t) -> p l t", t=P)[:, 0:L + 1, 0:n]
                        tt(masked[0:n, 0:L + 1, 0:n], pair_bank[0:n, 0:L + 1, 0:n], lt,
                           ALU.mult).then_inc(pairs_masked, 1)
                        dve.wait_ge(pairs_masked, c * HEADS + h + 2)
                        last = nc.vector.tensor_reduce(
                            gla_att[0:n, h, 0:n], masked[0:n, 0:L + 1, 0:n].rearrange("p l t -> p t l"),
                            mybir.AxisListType.X, ALU.add)
                        if h == HEADS - 1:
                            last.then_inc(S["gla_att_ready"], 1)

                    for l in range(1, L):
                        dve.wait_ge(z_ready, c * (LEVELS - 1) + l)
                        lt = masks[0:n, M_LOWT + (l + 1) * P:M_LOWT + (l + 1) * P + n]
                        tt(Z[0:n, :, 0:n], z_bank[0:n, :, 0:n], over_heads(lt), ALU.mult).then_inc(z_taken, 1)
                        if l <= HEADS:
                            take_pairs(l - 1)
                        dve.wait_ge(x_products, c * (LEVELS - 1) + l)
                        tt(XT[0:n, :, 0:n], XT[0:n, :, 0:n], xt_bank[0:n, :, 0:n], ALU.subtract).then_inc(x_updated, 1)
                        if l < L - 1:
                            tt(X[0:n, :, 0:n], X[0:n, :, 0:n], x_bank[0:n, :, 0:n], ALU.subtract) \
                                .then_inc(x_updated, 1)
                    dve.wait_ge(x_updated, c * UPDATES + 2 * (L - 1) - 1)
                    tt(XTb[0:n, :, 0:n], XT[0:n, :, 0:n], per_token(beta, n), ALU.mult).then_inc(S["XTb_ready"], 1)

                    def scale_outputs(name, which, z):
                        now(dve, name + "_squared", c)
                        before(dve, "out_ready" if which == 0 else "outg_ready", c)
                        tt(oz[which][:, :, 0:n], ring[which][:, :, 0:n], I[:, z:z + 4, 0:n],
                           ALU.mult).then_inc(S[name + "_scaled"], 1)
                    scale_outputs("Og", 1, R_GLA_Z)
                    scale_outputs("O", 0, R_GDN_Z)
                    now(dve, "dS", c)
                    for h in range(HEADS):
                        last = stt(state[:, h], state[:, h], e_row[:, h, n - 1:n], ring[1][:, h], ALU.mult, ALU.add)
                    last.then_inc(S["dS_taken"], 1)
                    now(dve, "dSg", c)
                    for h in range(HEADS):
                        rows = half_of(h)
                        last = stt(gla_state[rows, h], gla_state[rows, h], F[rows, 0, h // 2, n - 1:n],
                                   ring[2][rows, h], ALU.mult, ALU.add)
                    last.then_inc(S["dSg_taken"], 1)

                nc.vector.memset(eps[:, :], EPS).then_inc(eps_ready, 1)
                nc.vector.memset(state[:, :, :], 0.0)
                nc.vector.memset(gla_state[:, :, :], 0.0).then_inc(state_zero, 1)
                dve.wait_ge(state_zero, 1)
                dve.wait_ge(masks_landed, 16)
                preload(dve, DVE_)
                dve.sem_inc(pairs_masked, 1)
                per_chunk(dve, chunk)


def split_weights(nc, block, raw_of, rows, src, w_hi, w_lo, landed, high, split):
    @block.sync
    def _(sp):
        for k in range(rows):
            at_least(sp, split, k - 1)
            sp.dma_start(raw_of(k), src(k)).then_inc(landed[k % 2], 16)

    @block.scalar
    def _(act):
        for k in range(rows):
            act.wait_ge(landed[k % 2], 16 * (k // 2 + 1))
            nc.scalar.copy(w_hi[:, k], raw_of(k)).then_inc(high, 1)

    @block.vector
    def _(dve):
        for k in range(rows):
            dve.wait_ge(high, k + 1)
            nc.vector.tensor_tensor(w_lo[:, k], raw_of(k), w_hi[:, k].bitcast(F32),
                                    ALU.subtract).then_inc(split, 1)


def branch_phase(nc, d):
    K = 12
    TT = 256
    TILES_B = NP_ // TT
    with ExitStack() as ctx, Held(nc) as held:
        def sb(name, shape, dt=F32):
            return ctx.enter_context(nc.sbuf_tensor(name, shape, dt))

        def sem(name):
            return held.add(nc.alloc_semaphore(name))

        wo_hi = sb("wo_hi", [P, K, DM], F32R)
        wo_lo = sb("wo_lo", [P, K, DM], F32R)
        wo_raw = sb("wo_raw", [P, 2, DM])
        o_raw = sb("o_raw", [P, K, TT])
        o_hi = sb("o_hi", [P, 2, K, TT], F32R)
        o_lo = sb("o_lo", [P, 2, K, TT], F32R)
        gate = sb("gate", [P, 2, 12, TT])
        prod = sb("prod", [P, 2, 3, TT])
        part = sb("part", [P, 2, TT])
        merged = sb("merged", [P, 2, TT])
        y = ctx.enter_context(nc.psum_tensor("y", [P, 2, 4, TT], F32))

        wo_landed = [sem("wo_landed0"), sem("wo_landed1")]
        wo_high, wo_split = sem("wo_high"), sem("wo_split")
        o_landed, o_high, o_split = sem("o_landed"), sem("o_high"), sem("o_split")
        gate_landed = [sem("gate_landed0"), sem("gate_landed1")]
        y_ready, y_gated = sem("y_ready"), sem("y_gated")
        part_ready, merged_ready = sem("part_ready"), sem("merged_ready")
        merged_stored = [sem("merged_stored0"), sem("merged_stored1")]
        outs, gates = d["branch_out"], d["gates"]

        with nc.Block() as block:
            split_weights(nc, block, lambda k: wo_raw[:, k % 2], K, lambda k: d["wo"][k * P:(k + 1) * P, :],
                          wo_hi, wo_lo, wo_landed, wo_high, wo_split)

        with nc.Block() as block:
            def per_tile(eng, tile):
                tile(0, 0, 0, TT)
                tile(1, 0, 1, TT)
                with eng.Fori(1, TILES_B // 2) as i:
                    tile(i * 2, i, 0, TT)
                    tile(i * 2 + 1, i, 1, TT)
                tile(TILES_B, TILES_B // 2, 0, NS_)

            @block.sync
            def _(sp):
                def load_o(t, n=TT):
                    at_least(sp, o_split, t)
                    sp.dma_start(o_raw[:, :, 0:n], outs[:, :, bass.ds(t * TT, n)]).then_inc(o_landed, 16)

                def load_gates(t, half, n=TT):
                    sp.dma_start(gate[:, half, :, 0:n],
                                 gates[:, half * 12:half * 12 + 12, bass.ds(t * TT, n)]) \
                        .then_inc(gate_landed[half], 16)

                def store(t, m, n=TT):
                    sp.wait_ge(merged_ready, t * KD + (m + 1))
                    sp.dma_start(d["merged"][:, m, bass.ds(t * TT, n)], merged[:, m % 2, 0:n]) \
                        .then_inc(merged_stored[m % 2], 16)

                load_o(0)
                load_gates(0, 0)
                load_gates(0, 1)

                def tile(t, n=TT, ahead=TT):
                    if ahead:
                        load_o(t + 1, ahead)
                    for m in range(KD):
                        store(t, m, n)
                        if ahead and m % 4 == 3:
                            load_gates(t + 1, m // 4, ahead)
                tile(0)
                with sp.Fori(1, TILES_B - 1) as t:
                    tile(t)
                tile(TILES_B - 1, TT, NS_)
                tile(TILES_B, NS_, 0)
                for q in range(2):
                    sp.wait_ge(merged_stored[q], 16 * 4 * (TILES_B + 1))

            @block.scalar
            def _(act):
                def tile(t, i, p, n):
                    act.wait_ge(o_landed, t * 16 + 16)
                    if not (isinstance(t, int) and t < 2):
                        act.wait_ge(y_ready, (t - 1) * KD)
                    nc.scalar.copy(o_hi[:, p, :, 0:n], o_raw[:, :, 0:n]).then_inc(o_high, 1)
                per_tile(act, tile)

            @block.tensor
            def _(pe):
                def tile(t, i, p, n):
                    pe.wait_ge(o_split, t + 1)
                    for m in range(KD):
                        if not (isinstance(t, int) and t == 0 and m < 2):
                            pe.wait_ge(y_gated, t * KD + (m - 1))
                        cols = slice(m * P, (m + 1) * P)
                        for b in range(3):
                            out = y[:, m % 2, b, 0:n]
                            for k in range(4 * b, 4 * b + 4):
                                nc.tensor.matmul(out, wo_hi[:, k, cols], o_hi[:, p, k, 0:n],
                                                 start=(k == 4 * b), stop=False)
                                nc.tensor.matmul(out, wo_hi[:, k, cols], o_lo[:, p, k, 0:n],
                                                 start=False, stop=False)
                                mm = nc.tensor.matmul(out, wo_lo[:, k, cols], o_hi[:, p, k, 0:n],
                                                      start=False, stop=(k == 4 * b + 3))
                        mm.then_inc(y_ready, 1)
                per_tile(pe, tile)

            @block.vector
            def _(dve):
                def low(t, p, n):
                    dve.wait_ge(o_high, t + 1)
                    nc.vector.tensor_tensor(o_lo[:, p, :, 0:n], o_raw[:, :, 0:n],
                                            o_hi[:, p, :, 0:n].bitcast(F32), ALU.subtract).then_inc(o_split, 1)

                def gated(t, m, n):
                    dve.wait_ge(y_ready, t * KD + (m + 1))
                    if m % 4 == 0:
                        dve.wait_ge(gate_landed[m // 4], t * 16 + 16)
                    if not (isinstance(t, int) and t == 0 and m < 2):
                        dve.wait_ge(merged_ready, t * KD + (m - 1))
                    g = gate[:, m // 4, 3 * (m % 4):3 * (m % 4) + 3, 0:n]
                    nc.vector.tensor_tensor(prod[:, m % 2, :, 0:n], y[:, m % 2, 0:3, 0:n], g,
                                            ALU.mult).then_inc(y_gated, 1)

                def tile(t, i, p, n):
                    for m in range(KD):
                        gated(t, m, n)
                        if m == 3 and not (isinstance(t, int) and t == TILES_B):
                            if isinstance(t, int):
                                low(t + 1, 1 - p, TT)
                            else:
                                low(t + 1, 1 - p, TT)
                low(0, 0, TT)
                tile(0, 0, 0, TT)
                with dve.Fori(0, TILES_B // 2 - 1) as i:
                    tile(i * 2 + 1, i, 1, TT)
                    tile(i * 2 + 2, i, 0, TT)
                for m in range(KD):
                    gated(TILES_B - 1, m, TT)
                    if m == 3:
                        low(TILES_B, 0, NS_)
                for m in range(KD):
                    gated(TILES_B, m, NS_)

            @block.gpsimd
            def _(pool):
                def tile(t, i, p, n):
                    for m in range(KD):
                        q = m % 2
                        pool.wait_ge(y_gated, t * KD + (m + 1))
                        nc.gpsimd.tensor_tensor(part[:, q, 0:n], prod[:, q, 0, 0:n], prod[:, q, 1, 0:n],
                                                ALU.add).then_inc(part_ready, 1)
                        pool.wait_ge(part_ready, t * KD + (m + 1))
                        if not (isinstance(t, int) and t == 0 and m < 2):
                            pool.wait_ge(merged_stored[q], t * (4 * 16) + (m // 2) * 16)
                        nc.gpsimd.tensor_tensor(merged[:, q, 0:n], part[:, q, 0:n], prod[:, q, 2, 0:n],
                                                ALU.add).then_inc(merged_ready, 1)
                per_tile(pool, tile)


def output_phase(nc, d):
    with ExitStack() as ctx, Held(nc) as held:
        def sb(name, shape, dt=F32):
            return ctx.enter_context(nc.sbuf_tensor(name, shape, dt))

        def sem(name):
            return held.add(nc.alloc_semaphore(name))

        w_hi = sb("wout_hi", [P, KD, DM], F32R)
        w_lo = sb("wout_lo", [P, KD, DM], F32R)
        w_raw = sb("wout_raw", [P, 2, DM])
        m_raw = sb("m_raw", [P, 2, KD, P])
        m_hi = sb("m_hi", [P, 2, KD, P], F32R)
        m_lo = sb("m_lo", [P, 2, KD, P], F32R)
        x_in = sb("x_again", [P, 2, DM])
        squares = sb("y_squares", [P, DM])
        normed = sb("normed", [P, 2, DM])
        result = sb("result", [P, 2, DM])
        gain = sb("post_gain", [P, DM])
        stat = sb("stat", [P, 2, 3])
        eps = sb("post_eps", [P, 1])
        y = ctx.enter_context(nc.psum_tensor("y_tok", [P, 2, DM], F32))

        w_landed = [sem("wout_landed0"), sem("wout_landed1")]
        w_high, w_split = sem("wout_high"), sem("wout_split")
        gain_landed = sem("post_gain_landed")
        m_landed = [sem("m_landed0"), sem("m_landed1")]
        x_landed = [sem("x_again0"), sem("x_again1")]
        m_high, m_split = sem("m_high"), sem("m_split")
        y_ready = sem("y_tok_ready")
        sum_ready, log_ready, rstd_ready = sem("sum_ready"), sem("log_ready"), sem("post_rstd_ready")
        normed_ready, result_ready = sem("normed_ready"), sem("result_ready")
        stored = [sem("stored0"), sem("stored1")]
        eps_set = sem("post_eps_set")

        with nc.Block() as block:
            split_weights(nc, block, lambda k: w_raw[:, k % 2], KD, lambda k: d["w_out"][k * P:(k + 1) * P, :],
                          w_hi, w_lo, w_landed, w_high, w_split)

        with nc.Block() as block:
            def per_tile(eng, tile):
                tile(0, 0, 0, P)
                tile(1, 0, 1, P)
                with eng.Fori(1, CHUNKS // 2) as i:
                    tile(i * 2, i, 0, P)
                    tile(i * 2 + 1, i, 1, P)
                tile(CHUNKS, CHUNKS // 2, 0, NS_)

            @block.sync
            def _(sp):
                def load(t, p, n=P):
                    x = d["x_prompt"][bass.ds(t * P, P), :] if n == P else d["x_sample"]
                    sp.dma_start(m_raw[:, p, :, 0:n], d["merged"][:, :, bass.ds(t * P, n)]).then_inc(m_landed[p], 16)
                    sp.dma_start(x_in[0:n, p], x).then_inc(x_landed[p], 16)

                def store(t, p, n=P):
                    y_out = d["y_prompt"][bass.ds(t * P, P), :] if n == P else d["y_sample"]
                    sp.wait_ge(result_ready, t + 1)
                    sp.dma_start(y_out, result[0:n, p]).then_inc(stored[p], 16)

                sp.dma_start(gain[:, :], d["norm_post"].to_broadcast([P, DM])).then_inc(gain_landed, 16)
                load(0, 0)
                load(1, 1)
                with sp.Fori(0, CHUNKS // 2 - 1) as i:
                    for p in range(2):
                        store(i * 2 + p, p)
                        load(i * 2 + (p + 2), p)
                store(CHUNKS - 2, 0)
                load(CHUNKS, 0, NS_)
                store(CHUNKS - 1, 1)
                store(CHUNKS, 0, NS_)
                sp.wait_ge(stored[0], 16 * (CHUNKS // 2 + 1))
                sp.wait_ge(stored[1], 16 * (CHUNKS // 2))

            @block.scalar
            def _(act):
                def high(t, i, p, n):
                    act.wait_ge(m_landed[p], i * 16 + 16)
                    if not (isinstance(t, int) and t < 2):
                        act.wait_ge(y_ready, t - 1)
                    nc.scalar.copy(m_hi[:, p, :, 0:n], m_raw[:, p, :, 0:n]).then_inc(m_high, 1)

                def statistics(t, p, n):
                    act.wait_ge(y_ready, t + 1)
                    if not (isinstance(t, int) and t < 2):
                        act.wait_ge(normed_ready, t - 1)
                    nc.scalar.activation(squares[0:n], y[0:n, p], ACT.Square,
                                         accum_out=stat[0:n, p, 0:1]).then_inc(sum_ready, 1)
                    act.wait_ge(sum_ready, t + 1)
                    nc.scalar.activation(stat[0:n, p, 1:2], stat[0:n, p, 0:1], ACT.Ln, bias=eps[0:n, 0:1],
                                         scale=1.0 / DM).then_inc(log_ready, 1)
                    act.wait_ge(log_ready, t + 1)
                    nc.scalar.activation(stat[0:n, p, 2:3], stat[0:n, p, 1:2], ACT.Exp,
                                         scale=-0.5).then_inc(rstd_ready, 1)

                act.wait_ge(eps_set, 1)
                high(0, 0, 0, P)
                high(1, 0, 1, P)
                for p in range(2):
                    statistics(p, p, P)
                    high(p + 2, 1, p, P)
                with act.Fori(1, CHUNKS // 2 - 1) as i:
                    for p in range(2):
                        statistics(i * 2 + p, p, P)
                        high(i * 2 + (p + 2), i + 1, p, P)
                statistics(CHUNKS - 2, 0, P)
                high(CHUNKS, CHUNKS // 2, 0, NS_)
                statistics(CHUNKS - 1, 1, P)
                statistics(CHUNKS, 0, NS_)

            @block.tensor
            def _(pe):
                def tile(t, i, p, n):
                    pe.wait_ge(m_split, t + 1)
                    if not (isinstance(t, int) and t < 2):
                        pe.wait_ge(normed_ready, t - 1)
                    for half in range(2):
                        cols = slice(half * 512, half * 512 + 512)
                        out = y[0:n, p, cols]
                        for k in range(KD):
                            nc.tensor.matmul(out, m_hi[:, p, k, 0:n], w_hi[:, k, cols], start=(k == 0), stop=False)
                            nc.tensor.matmul(out, m_hi[:, p, k, 0:n], w_lo[:, k, cols], start=False, stop=False)
                            mm = nc.tensor.matmul(out, m_lo[:, p, k, 0:n], w_hi[:, k, cols], start=False,
                                                  stop=(k == KD - 1))
                    mm.then_inc(y_ready, 1)
                per_tile(pe, tile)

            @block.vector
            def _(dve):
                def low(t, p, n):
                    dve.wait_ge(m_high, t + 1)
                    nc.vector.tensor_tensor(m_lo[:, p, :, 0:n], m_raw[:, p, :, 0:n],
                                            m_hi[:, p, :, 0:n].bitcast(F32), ALU.subtract).then_inc(m_split, 1)

                def norm(t, p, n):
                    dve.wait_ge(rstd_ready, t + 1)
                    if not (isinstance(t, int) and t < 2):
                        dve.wait_ge(result_ready, t - 1)
                    nc.vector.scalar_tensor_tensor(normed[0:n, p], y[0:n, p], stat[0:n, p, 2:3], gain[0:n],
                                                   ALU.mult, ALU.mult).then_inc(normed_ready, 1)

                nc.vector.memset(eps[:, :], EPS).then_inc(eps_set, 1)
                dve.wait_ge(gain_landed, 16)
                low(0, 0, P)
                low(1, 1, P)
                norm(0, 0, P)
                low(2, 0, P)
                norm(1, 1, P)
                low(3, 1, P)
                with dve.Fori(1, CHUNKS // 2 - 1) as i:
                    for p in range(2):
                        norm(i * 2 + p, p, P)
                        low(i * 2 + (p + 2), p, P)
                norm(CHUNKS - 2, 0, P)
                low(CHUNKS, 0, NS_)
                norm(CHUNKS - 1, 1, P)
                norm(CHUNKS, 0, NS_)

            @block.gpsimd
            def _(pool):
                def tile(t, i, p, n):
                    pool.wait_ge(x_landed[p], i * 16 + 16)
                    if not (isinstance(t, int) and t < 2):
                        pool.wait_ge(stored[p], i * 16)
                    pool.wait_ge(normed_ready, t + 1)
                    nc.gpsimd.tensor_tensor(result[0:n, p], normed[0:n, p], x_in[0:n, p],
                                            ALU.add).then_inc(result_ready, 1)
                per_tile(pool, tile)


def program(nc, d):
    with ExitStack() as ctx:
        consts = ctx.enter_context(nc.sbuf_tensor("constants", [P, C_END], F32))
        with ExitStack() as early:
            hi = early.enter_context(nc.sbuf_tensor("h_hi", [P, KD, NT], F32R))
            lo = early.enter_context(nc.sbuf_tensor("h_lo", [P, KD, NT], F32R))
            norm_phase(nc, d, hi, lo, consts)
            project_phase(nc, d, hi, lo, consts)
        chunk_phase(nc, d, consts)
    branch_phase(nc, d)
    output_phase(nc, d)


def shape_constants():
    import numpy as np
    c = np.zeros((P, C_END), np.float32)
    m = np.zeros((P, M_END), np.float32)
    i = np.arange(P)
    row, col = i[:, None], i[None, :]
    c[:, C_IDENT:C_IDENT + P] = np.eye(P)
    c[:, C_ONES:C_ONES + P] = 1
    c[:, C_CNT:C_CNT + 16] = 1.0 / (1 + np.arange(16))
    m[:, M_UPPER:M_UPPER + P] = row <= col
    m[:, M_NEG:M_NEG + P] = np.where(row <= col, 0, -1e30)
    m[:, M_POS:M_POS + P] = np.where(row > col, 0, 1e30)
    m[:, M_LOWT:M_LOWT + P] = np.eye(P)
    for n in range(LEVELS):
        s = 1 << n
        low = (row // (2 * s) == col // (2 * s)) & (row // s % 2 == 1) & (col // s % 2 == 0)
        m[:, M_LOW + n * P:M_LOW + (n + 1) * P] = low
        m[:, M_LOWT + (n + 1) * P:M_LOWT + (n + 2) * P] = low.T
    return c, m


def laid_out(x):
    import numpy as np
    x = {k: np.asarray(v) for k, v in x.items()}
    w = x["w_in"][0]
    blocks = np.zeros((F_END, P, DM), np.float32)

    def put(f, cols):
        part = w[:, cols:cols + P]
        blocks[f] = part.reshape(KD, P, P).transpose(1, 0, 2).reshape(P, DM)
    special = np.zeros((DM, P), np.float32)
    special[:, AT_F:AT_F + 16] = w[:, 1024:1040]
    special[:, AT_G:AT_G + 4] = w[:, 4112:4116]
    special[:, AT_B:AT_B + 4] = w[:, 4116:4120]
    blocks[F_SPECIAL] = special.reshape(KD, P, P).transpose(1, 0, 2).reshape(P, DM)
    for n in range(8):
        put(F_COPY + n, n * P)
    for n in range(4):
        put(F_SILU + n, 1040 + n * P)
        put(F_SILU + 4 + n, 4120 + n * P)
        put(F_POOL + 2 * n, 1552 + n * P)
        put(F_POOL + 2 * n + 1, 2064 + n * P)
    for n in range(12):
        put(F_CONV + n, 2576 + n * P)
    for n in range(24):
        put(F_GATE + n, 4632 + (n % 3) * DM + (n // 3) * P)

    def columns(v, n):
        return np.ascontiguousarray(v.reshape(n, P).T)
    return {
        "x_prompt": x["x_prompt"][0], "x_sample": x["x_sample"][0], "norm_pre": x["norm_pre"],
        "consts": shape_constants()[0], "masks": shape_constants()[1], "w_in": blocks, "gla_bf": columns(x["gla_bf"], 2),
        "pool_scale": columns(x["pool_scale"], 4), "gla_norm": columns(x["gla_norm"], 4),
        "gdn_norm": columns(x["gdn_norm"], 4),
        "gdn_conv": np.ascontiguousarray(x["gdn_conv"][0].reshape(4, 12, P).transpose(2, 1, 0)).reshape(P, 48),
        "scalars": np.tile(np.array([[EPS, np.log(P ** -0.5)]], np.float32), (P, 1)),
        "gdn_a_log": x["gdn_a_log"].reshape(4, 1), "gdn_dt_bias": x["gdn_dt_bias"].reshape(4, 1),
        "gla_wf2": x["gla_wf2"][0], "pool_w": np.ascontiguousarray(x["pool_w"][0].transpose(1, 0, 2)),
        "conv_cache": np.ascontiguousarray(x["cache_gdn_conv"][0, 0].reshape(3, 12, P).transpose(2, 1, 0)),
        "pool_cache": np.ascontiguousarray(x["cache_pool"][0, 0].reshape(15, 4, P).transpose(2, 1, 0)),
        "state_gla": x["state_gla"][0, 0], "state_gdn": x["state_gdn"][0, 0],
        "wo": np.concatenate([x["gla_wo"][0], x["pool_wo"][0], x["gdn_wo"][0]]),
        "w_out": x["w_out"][0], "norm_post": x["norm_post"],
    }


_OUTS = {
    "y_prompt": (NP_, DM), "y_sample": (NS_, DM),
    "new_gla_prompt": (HEADS, 64, P), "new_gdn_prompt": (HEADS, P, P),
    "new_conv_prompt": (P, 12, CONV_HALO), "new_pool_prompt": (P, 4, POOL_HALO),
    "new_gla_sample": (HEADS, 64, P), "new_gdn_sample": (HEADS, P, P),
    "new_conv_sample": (P, 12, CONV_HALO), "new_pool_sample": (P, 4, POOL_HALO),
}
_SCRATCH = {"feat": (P, R_END, NT), "gates": (P, 24, NT), "branch_out": (P, 12, NT), "merged": (P, KD, NT)}


def kernel(**inputs):
    import numpy as np
    import concourse.bacc as bacc
    from concourse.bass_utils import run_bass_kernel_spmd

    nc = bacc.Bacc("TRN2", target_bir_lowering=False, num_devices=1)
    arrays, d = {}, {}
    for name, a in laid_out(inputs).items():
        a = np.ascontiguousarray(a)
        arrays[f"in_{name}"] = a
        d[name] = nc.dram_tensor(f"in_{name}", a.shape, F32, kind="ExternalInput").ap()
    for name, shape in _OUTS.items():
        d[name] = nc.dram_tensor(f"out_{name}", shape, F32, kind="ExternalOutput").ap()
    for name, shape in _SCRATCH.items():
        d[name] = nc.dram_tensor(f"scratch_{name}", shape, F32, kind="Internal").ap()
    program(nc, d)
    r = run_bass_kernel_spmd(nc, [arrays], core_ids=[0]).results[0]
    got = {name: r[f"out_{name}"] for name in _OUTS}

    def cache(a):
        return np.ascontiguousarray(a.transpose(2, 1, 0)).reshape(1, 1, a.shape[2], -1)
    out = [got["y_prompt"][None], got["y_sample"][None]]
    for group in ("prompt", "sample"):
        out += [got[f"new_gla_{group}"][None, None], got[f"new_gdn_{group}"][None, None],
                cache(got[f"new_conv_{group}"]), cache(got[f"new_pool_{group}"])]
    return tuple(out)
```

```python
from contextlib import ExitStack

import concourse.bass as bass
from concourse import mybir

F32 = mybir.dt.float32
F32R = mybir.dt.float32r
ALU = mybir.AluOpType
ACT = mybir.ActivationFunctionType

P = 128
DM = 1024
KD = DM // P
NP_ = 2048
NS_ = 64
NT = NP_ + NS_
TILES = 6
TW = NT // TILES
HEADS = 4
CHUNKS = NP_ // P
EPS = 1e-6
LEVELS = 7
ROW = 2144
POOL_HALO = 15
CONV_HALO = 3

C_IDENT = 0
C_ONES = C_IDENT + P
C_CNT = C_ONES + P
C_END = C_CNT + 16

M_UPPER = 0
M_NEG = M_UPPER + P
M_POS = M_NEG + P
M_LOW = M_POS + P
M_PAIRS = M_LOW + P
HALF = P // 2
M_END = M_PAIRS + LEVELS * HALF

F_SPECIAL = 0
F_COPY = 1
F_SILU = F_COPY + 8
F_POOL = F_SILU + 8
F_CONV = F_POOL + 8
F_GATE = F_CONV + 12
F_END = F_GATE + 24

LATE_GATES = CHUNKS
EARLY_GATES = 24 - LATE_GATES
F_LATE = F_GATE + EARLY_GATES

A_SPECIAL = 0
A_COPY = 1
A_POOL = A_COPY + 8
A_CONV = A_POOL + 4
A_GATE = A_CONV + 12

R_GLA_Q, R_GLA_K, R_GLA_V = 0, 2, 4
R_LOGF = 8
R_GB = 10
R_GLA_Z = 11
R_GDN_Z = 15
R_GDN_Q, R_GDN_K, R_GDN_V = 19, 23, 27
R_END = 31

S_NEGA, S_DT, S_BF, S_PSCALE, S_ZNORM, S_CONV, S_EPS, S_QS = 0, 1, 2, 4, 8, 16, 64, 65
S_END = 66

AT_F, AT_G, AT_B = 0, 32, 64


def at_least(eng, sem, value):
    if isinstance(value, int) and value <= 0:
        return
    eng.wait_ge(sem, value)


class Held:

    def __init__(self, nc):
        self.nc, self.semaphores = nc, []

    def add(self, semaphore):
        self.semaphores.append(semaphore)
        return semaphore

    def __enter__(self):
        return self

    def __exit__(self, *error):
        self.nc.clear_and_free_semaphores(self.semaphores)
        self.nc.all_engine_barrier()


def use_log_exp_tables(nc):
    nc.scalar.preload_act_table_set("natural_log_exp_and_others")


def second_halves(x, s):
    return x.rearrange("p h (m t) -> p h m t", t=2 * s)[:, :, :, s:2 * s]


def halves_packed(x, s):
    return x.rearrange("p h (m t) -> p h m t", t=s)


def column(tensor, n):
    return tensor[:, n:n + 1] if isinstance(n, int) else tensor[:, bass.ds(n, 1)]


def norm_phase(nc, d, hi, lo, consts):
    tiles = CHUNKS + 1
    with ExitStack() as ctx, Held(nc) as held:
        def sb(name, shape, dt=F32):
            return ctx.enter_context(nc.sbuf_tensor(name, shape, dt))

        def sem(name):
            return held.add(nc.alloc_semaphore(name))

        x_in = sb("x_in", [P, 2, DM])
        x_scaled = sb("x_scaled", [P, 2, DM])
        squares = sb("squares", [P, DM])
        gain = sb("gain", [P, DM])
        sums = sb("sums", [P, 2])
        logs = sb("logs", [P, 2])
        rstd = sb("rstd", [P, 2])
        eps = sb("eps", [P, 1])
        turned = ctx.enter_context(nc.psum_tensor("turned", [P, 2, KD, P], F32))
        ident = consts[:, C_IDENT:C_IDENT + P]

        gain_landed = sem("gain_landed")
        x_landed = [sem("x_landed0"), sem("x_landed1")]
        eps_set = sem("eps_set")
        sums_ready = sem("sums_ready")
        logs_ready = sem("logs_ready")
        rstd_ready = sem("rstd_ready")
        scaled_ready = sem("scaled_ready")
        turned_ready = sem("turned_ready")
        hi_ready = sem("hi_ready")
        lo_ready = sem("lo_ready")

        with nc.Block() as block:
            @block.sync
            def _(sp):
                sp.dma_start(consts[:, :], d["consts"]).then_inc(gain_landed, 16)
                sp.dma_start(gain[:, :], d["norm_pre"].to_broadcast([P, DM])).then_inc(gain_landed, 16)
                sp.dma_start(x_in[:, 0], d["x_prompt"][0:P, :]).then_inc(x_landed[0], 16)
                sp.dma_start(x_in[:, 1], d["x_prompt"][P:2 * P, :]).then_inc(x_landed[1], 16)
                with sp.Fori(1, CHUNKS // 2) as i:
                    for u in range(2):
                        sp.wait_ge(scaled_ready, i * 2 + (u - 1))
                        sp.dma_start(x_in[:, u], d["x_prompt"][bass.ds((i * 2 + u) * P, P), :]) \
                            .then_inc(x_landed[u], 16)
                sp.wait_ge(scaled_ready, CHUNKS - 1)
                sp.dma_start(x_in[0:NS_, 0], d["x_sample"]).then_inc(x_landed[0], 16)

            @block.scalar
            def _(act):
                def statistics(t, i, u):
                    act.wait_ge(x_landed[u], i * 16 + 16)
                    nc.scalar.activation(squares[:, :], x_in[:, u], ACT.Square,
                                         accum_out=sums[:, u:u + 1]).then_inc(sums_ready, 1)
                    act.wait_ge(sums_ready, t + 1)
                    nc.scalar.activation(logs[:, u:u + 1], sums[:, u:u + 1], ACT.Ln, bias=eps[:, 0:1],
                                         scale=1.0 / DM).then_inc(logs_ready, 1)
                    act.wait_ge(logs_ready, t + 1)
                    nc.scalar.activation(rstd[:, u:u + 1], logs[:, u:u + 1], ACT.Exp,
                                         scale=-0.5).then_inc(rstd_ready, 1)

                def high(t, u, n=P):
                    act.wait_ge(turned_ready, t + 1)
                    nc.scalar.copy(hi[:, :, bass.ds(t * P, n)], turned[:, u, :, 0:n]).then_inc(hi_ready, 1)

                use_log_exp_tables(nc)
                act.wait_ge(eps_set, 1)
                statistics(0, 0, 0)
                with act.Fori(0, CHUNKS // 2) as i:
                    statistics(i * 2 + 1, i, 1)
                    high(i * 2, 0)
                    statistics(i * 2 + 2, i + 1, 0)
                    high(i * 2 + 1, 1)
                high(CHUNKS, 0, NS_)

            @block.vector
            def _(dve):
                nc.vector.memset(eps[:, :], EPS).then_inc(eps_set, 1)

                def scale(t, u):
                    dve.wait_ge(rstd_ready, t + 1)
                    nc.vector.scalar_tensor_tensor(x_scaled[:, u], x_in[:, u], rstd[:, u:u + 1], gain[:, :],
                                                   ALU.mult, ALU.mult).then_inc(scaled_ready, 1)

                def low(t, u, n=P):
                    dve.wait_ge(hi_ready, t + 1)
                    nc.vector.tensor_tensor(lo[:, :, bass.ds(t * P, n)], turned[:, u, :, 0:n],
                                            hi[:, :, bass.ds(t * P, n)].bitcast(F32),
                                            ALU.subtract).then_inc(lo_ready, 1)

                dve.wait_ge(gain_landed, 32)
                scale(0, 0)
                dve.wait_ge(rstd_ready, 2)
                scale(1, 1)
                low(0, 0)
                dve.wait_ge(turned_ready, 1)
                scale(2, 0)
                low(1, 1)
                with dve.Fori(1, CHUNKS // 2) as i:
                    dve.wait_ge(turned_ready, i * 2)
                    scale(i * 2 + 1, 1)
                    low(i * 2, 0)
                    dve.wait_ge(turned_ready, i * 2 + 1)
                    scale(i * 2 + 2, 0)
                    low(i * 2 + 1, 1)
                low(CHUNKS, 0, NS_)

            @block.tensor
            def _(pe):
                def turn(t, u):
                    pe.wait_ge(scaled_ready, t + 1)
                    for k in range(KD):
                        mm = nc.tensor.transpose(turned[:, u, k], x_scaled[:, u, k * P:(k + 1) * P], ident)
                    mm.then_inc(turned_ready, 1)

                pe.wait_ge(gain_landed, 32)
                turn(0, 0)
                turn(1, 1)
                with pe.Fori(1, CHUNKS // 2) as i:
                    for u in range(2):
                        pe.wait_ge(lo_ready, i * 2 + (u - 1))
                        turn(i * 2 + u, u)
                pe.wait_ge(lo_ready, CHUNKS - 1)
                turn(CHUNKS, 0)


def project_phase(nc, d, hi, lo, h_all, consts):
    with ExitStack() as ctx, Held(nc) as held:
        def sb(name, shape, dt=F32):
            return ctx.enter_context(nc.sbuf_tensor(name, shape, dt))

        def sem(name):
            return held.add(nc.alloc_semaphore(name))

        w_raw = sb("w_raw", [P, 2, DM])
        w_hi = sb("w_hi", [P, 2, KD, P], F32R)
        w_lo = sb("w_lo", [P, 2, KD, P], F32R)
        X = sb("row_x", [P, 2, ROW])
        Y = sb("row_y", [P, 2, ROW])
        T = sb("row_t", [P, ROW])
        sig = sb("sig", [P, 2, TW])
        small = sb("small", [P, S_END])
        wf2 = sb("wf2", [16, 256])
        pool_w = sb("pool_w", [P, 4, P])
        conv_cache = sb("conv_cache", [P, 12, CONV_HALO])
        conv_out = sb("conv_out", [P, 2, 12, CONV_HALO])
        pool_out = sb("pool_out", [P, 2, 4, POOL_HALO])
        dense = ctx.enter_context(nc.psum_tensor("dense", [P, 2, 512], F32))
        side = ctx.enter_context(nc.psum_tensor("side", [P, 2, 512], F32))
        zero = sb("zero", [P, 1])
        zeros = zero[:, 0:1].rearrange("p (a b) -> p a b", b=1).to_broadcast([P, KD, P])
        ones = consts[:, C_ONES:C_ONES + P]

        zero_set = sem("zero_set")
        params_landed = sem("params_landed")
        w_landed = [sem("w_landed0"), sem("w_landed1")]
        w_high = sem("w_high")
        w_split = sem("w_split")
        dense_ready = sem("dense_ready")
        act_free = sem("act_free")
        dve_free = sem("dve_free")
        side_ready = sem("side_ready")
        side_free = sem("side_free")
        norm_free = sem("norm_free")
        act_done = sem("act_done")
        dve_done = sem("dve_done")
        special_ready = sem("special_ready")
        special_stored = sem("special_stored")
        logf_ready = sem("logf_ready")
        copy_stored = [sem("copy_stored0"), sem("copy_stored1")]
        sig_ready = sem("sig_ready")
        silu_stored = [sem("silu_stored0"), sem("silu_stored1")]
        pool_step = sem("pool_step")
        pool_d_ready = sem("pool_d_ready")
        pool_stored = sem("pool_stored")
        halo_set = sem("halo_set")
        conv_step = sem("conv_step")
        special_step = sem("special_step")
        conv_ready = sem("conv_ready")
        conv_sig_ready = sem("conv_sig_ready")
        conv_silu_ready = sem("conv_silu_ready")
        squares_ready = sem("squares_ready")
        norm_logs_ready = sem("norm_logs_ready")
        norm_ready = sem("norm_ready")
        qkv_ready = sem("qkv_ready")
        qkv_stored = [sem("qkv_stored0"), sem("qkv_stored1")]
        caches_stored = sem("caches_stored")
        gate_stored = [sem("gate_stored0"), sem("gate_stored1")]

        feat, gates, outs = d["feat"], d["gates"], d["branch_out"]
        PARAMS = 12 * 16

        with nc.Block() as block:
            @block.gpsimd
            def _(pool):
                def split(i, f, p):
                    pool.wait_ge(w_landed[p], i * 16 + 16)
                    raw = w_raw[:, p].rearrange("p (k m) -> p k m", k=KD)
                    nc.gpsimd.tensor_tensor(w_hi[:, p], raw, zeros, ALU.add).then_inc(w_high, 1)
                    pool.wait_ge(w_high, f + 1)
                    nc.gpsimd.tensor_tensor(w_lo[:, p], raw, w_hi[:, p].bitcast(F32),
                                            ALU.subtract).then_inc(w_split, 1)

                nc.gpsimd.memset(zero[:, :], 0.0).then_inc(zero_set, 1)
                pool.wait_ge(zero_set, 1)
                split(0, 0, 0)
                split(0, 1, 1)
                with pool.Fori(1, F_LATE // 2) as i:
                    for p in range(2):
                        pool.wait_ge(dense_ready, i * (2 * TILES) + (p - 1) * TILES)
                        split(i, i * 2 + p, p)
                pool.wait_ge(dense_ready, (F_LATE - 2) * TILES)
                split(F_LATE // 2, F_LATE - 1, 0)

            @block.tensor
            def _(pe):
                def project(f, p, own, before):
                    pe.wait_ge(w_split, f + 1)
                    for t in range(TILES):
                        if t >= 2:
                            pe.wait_ge(own[0], own[1] * TILES + (t - 1))
                        elif before is not None:
                            pe.wait_ge(before[0], before[1] * TILES + (TILES + t - 1))
                        for k in range(KD):
                            cols = slice(t * TW, (t + 1) * TW)
                            out = dense[:, t % 2, 0:TW]
                            nc.tensor.matmul(out, w_hi[:, p, k], hi[:, k, cols], start=(k == 0), stop=False)
                            nc.tensor.matmul(out, w_hi[:, p, k], lo[:, k, cols], start=False, stop=False)
                            mm = nc.tensor.matmul(out, w_lo[:, p, k], hi[:, k, cols], start=False,
                                                  stop=(k == KD - 1))
                        mm.then_inc(dense_ready, 1)

                def by_act(n):
                    return act_free, n

                def by_dve(n):
                    return dve_free, n

                def forget_gates(b):
                    for t in range(TILES):
                        n = b * TILES + t
                        at_least(pe, side_free, n - 1)
                        nc.tensor.matmul(side[:, n % 2, 0:TW], wf2[:, b * P:(b + 1) * P],
                                         X[0:16, 0, t * TW:(t + 1) * TW], start=True, stop=True) \
                            .then_inc(side_ready, 1)

                project(F_SPECIAL, 0, by_act(A_SPECIAL), None)
                project(F_COPY, 1, by_act(A_COPY), by_act(A_SPECIAL))
                pe.wait_ge(special_ready, 1)
                forget_gates(0)
                project(F_COPY + 1, 0, by_act(A_COPY + 1), by_act(A_COPY))
                project(F_COPY + 2, 1, by_act(A_COPY + 2), by_act(A_COPY + 1))
                forget_gates(1)
                project(F_COPY + 3, 0, by_act(A_COPY + 3), by_act(A_COPY + 2))
                with pe.Fori(2, 4) as i:
                    for u in range(2):
                        project(i * 2 + (F_COPY + u), 1 - u, by_act(i * 2 + (A_COPY + u)),
                                by_act(i * 2 + (A_COPY + u - 1)))
                project(F_SILU, 1, by_dve(0), by_act(A_COPY + 7))
                project(F_SILU + 1, 0, by_dve(1), by_dve(0))
                with pe.Fori(1, 4) as i:
                    for u in range(2):
                        project(i * 2 + (F_SILU + u), 1 - u, by_dve(i * 2 + u), by_dve(i * 2 + (u - 1)))
                for g in range(4):
                    project(F_POOL + 2 * g, 1, by_act(A_POOL + g), by_dve(7 + g))
                    project(F_POOL + 2 * g + 1, 0, by_dve(8 + g), by_act(A_POOL + g))
                    pe.wait_ge(pool_d_ready, g + 1)
                    for t in range(TILES):
                        n = (2 + g) * TILES + t
                        pe.wait_ge(side_free, n - 1)
                        nc.tensor.matmul(side[:, n % 2, 0:TW], pool_w[:, g], X[:, 1, t * TW:(t + 1) * TW],
                                         start=True, stop=True).then_inc(side_ready, 1)

                def square_sums(j):
                    pe.wait_ge(squares_ready, j + 1)
                    for t in range(TILES):
                        if isinstance(j, int) and j == 0 and t < 2:
                            pe.wait_ge(side_free, 6 * TILES + t - 1)
                        elif t < 2:
                            pe.wait_ge(norm_free, j * TILES + (t - 1))
                        else:
                            pe.wait_ge(norm_free, j * TILES + (t - 1))
                        nc.tensor.matmul(side[:, t % 2, 0:TW], ones, T[:, t * TW:(t + 1) * TW],
                                         start=True, stop=True).then_inc(side_ready, 1)

                def conv_project(j, p):
                    project(j + F_CONV, p, by_act(j + A_CONV), by_act(j + (A_CONV - 1)))

                project(F_CONV, 1, by_act(A_CONV), by_dve(11))
                conv_project(1, 0)
                square_sums(0)
                with pe.Fori(0, 3) as i:
                    conv_project(i * 2 + 2, 1)
                    square_sums(i * 2 + 1)
                    conv_project(i * 2 + 3, 0)
                    square_sums(i * 2 + 2)
                conv_project(8, 1)
                square_sums(7)
                conv_project(9, 0)
                with pe.Fori(0, 1 + EARLY_GATES // 2) as i:
                    conv_project(i * 2 + 10, 1)
                    conv_project(i * 2 + 11, 0)

            @block.scalar
            def _(act):
                def tiles(f, write):
                    for t in range(TILES):
                        act.wait_ge(dense_ready, f * TILES + (t + 1))
                        write(t, dense[:, t % 2, 0:TW])

                use_log_exp_tables(nc)
                act.wait_ge(params_landed, PARAMS)
                nc.scalar.activation(small[AT_G:AT_G + 4, S_NEGA:S_NEGA + 1],
                                     small[AT_G:AT_G + 4, S_NEGA:S_NEGA + 1], ACT.Exp).then_inc(act_done, 1)

                def special(t, tile):
                    mm = nc.scalar.copy(X[:, 0, t * TW:(t + 1) * TW], tile)
                    mm.then_inc(act_free, 1)
                tiles(F_SPECIAL, special)
                act.wait_ge(act_free, TILES)
                nc.scalar.activation(X[AT_B:AT_B + 4, 0, 0:NT], X[AT_B:AT_B + 4, 0, 0:NT], ACT.Exp,
                                     scale=-1.0).then_inc(special_ready, 1)

                def softplus_part(n):
                    act.wait_ge(dve_done, n + 1)
                    v = T[AT_G:AT_G + 4, 0:NT] if n == 0 else X[:, 1, 0:NT]
                    nc.scalar.activation(v, v, ACT.Exp, scale=-1.0).then_inc(act_done, 1)
                    act.wait_ge(act_done, 2 * n + 2)
                    nc.scalar.activation(v, v, ACT.Ln, bias=1.0).then_inc(act_done, 1)

                def copy_block(i, f, p, scale=1.0):
                    def write(t, tile):
                        out = Y[:, p, t * TW:(t + 1) * TW]
                        nc.scalar.mul(out, tile, scale).then_inc(act_free, 1)
                    tiles(f, write)

                softplus_part(0)
                copy_block(0, F_COPY, 1, 0.125)
                copy_block(0, F_COPY + 1, 0, 0.125)
                softplus_part(1)
                act.wait_ge(copy_stored[1], 16)
                copy_block(1, F_COPY + 2, 1)
                act.wait_ge(copy_stored[0], 16)
                copy_block(1, F_COPY + 3, 0)
                softplus_part(2)
                with act.Fori(2, 4) as i:
                    for p in (1, 0):
                        act.wait_ge(copy_stored[p], i * 16)
                        copy_block(i, i * 2 + (F_COPY + 1 - p), p)

                def sigmoid_tiles(f, m):
                    def write(t, tile):
                        if not (isinstance(m, int) and m == 0 and t < 2):
                            act.wait_ge(dve_free, m * TILES + (t - 1))
                        nc.scalar.activation(sig[:, t % 2], tile, ACT.Sigmoid).then_inc(sig_ready, 1)
                    tiles(f, write)

                sigmoid_tiles(F_SILU, 0)
                sigmoid_tiles(F_SILU + 1, 1)
                with act.Fori(1, 4) as i:
                    sigmoid_tiles(i * 2 + F_SILU, i * 2)
                    sigmoid_tiles(i * 2 + (F_SILU + 1), i * 2 + 1)

                for g in range(4):
                    f = F_POOL + 2 * g
                    if g >= 1:
                        act.wait_ge(pool_d_ready, g)

                    def write(t, tile):
                        if t < TILES - 1:
                            nc.scalar.copy(X[:, 0, POOL_HALO + t * TW:POOL_HALO + (t + 1) * TW],
                                           tile).then_inc(act_free, 1)
                        else:
                            cut = NP_ - t * TW
                            nc.scalar.copy(X[:, 0, POOL_HALO + t * TW:POOL_HALO + NP_], tile[:, 0:cut])
                            nc.scalar.copy(X[:, 0, 2 * POOL_HALO + NP_:2 * POOL_HALO + NT],
                                           tile[:, cut:TW]).then_inc(act_free, 1)
                    tiles(f, write)
                    sigmoid_tiles(f + 1, 8 + g)

                def conv_block(p):
                    def write(t, tile):
                        if t < TILES - 1:
                            nc.scalar.copy(X[:, p, CONV_HALO + t * TW:CONV_HALO + (t + 1) * TW],
                                           tile).then_inc(act_free, 1)
                        else:
                            cut = NP_ - t * TW
                            nc.scalar.copy(X[:, p, CONV_HALO + t * TW:CONV_HALO + NP_], tile[:, 0:cut])
                            nc.scalar.copy(X[:, p, 2 * CONV_HALO + NP_:2 * CONV_HALO + NT],
                                           tile[:, cut:TW]).then_inc(act_free, 1)
                    return write

                def conv_sigmoid(j, p):
                    act.wait_ge(conv_ready, j + 1)
                    nc.scalar.activation(T[:, 0:NT], Y[:, p, 0:NT], ACT.Sigmoid).then_inc(conv_sig_ready, 1)

                def squares(j, p):
                    act.wait_ge(conv_silu_ready, j + 1)
                    nc.scalar.activation(T[:, 0:NT], Y[:, p, 0:NT], ACT.Square).then_inc(squares_ready, 1)

                def norm_logs(j, t):
                    act.wait_ge(side_ready, j * TILES + (6 * TILES + t + 1))
                    nc.scalar.activation(T[:, t * TW:(t + 1) * TW], side[:, t % 2, 0:TW], ACT.Ln,
                                         bias=small[:, S_EPS:S_EPS + 1]).then_inc(norm_free, 1)

                def norm_exp(j, q_scale):
                    act.wait_ge(norm_free, j * TILES + TILES)
                    if q_scale:
                        nc.scalar.activation(T[:, 0:NT], T[:, 0:NT], ACT.Exp, scale=-0.5,
                                             bias=small[:, S_QS:S_QS + 1]).then_inc(norm_ready, 1)
                    else:
                        nc.scalar.activation(T[:, 0:NT], T[:, 0:NT], ACT.Exp,
                                             scale=-0.5).then_inc(norm_ready, 1)

                def conv_slot(j, p, normed=None, square=True):
                    write = conv_block(p)
                    if normed is not None:
                        use_log_exp_tables(nc)
                        for t in range(TILES):
                            norm_logs(j - 2, t)
                    at_least(act, conv_ready, j - 1)
                    for t in range(TILES):
                        act.wait_ge(dense_ready, j * TILES + (F_CONV * TILES + t + 1))
                        write(t, dense[:, t % 2, 0:TW])
                        if t == 0 and normed is not None:
                            norm_exp(j - 2, normed)
                        if t == 3 and not (isinstance(j, int) and j == 0):
                            at_least(act, qkv_ready, j - 1)
                            conv_sigmoid(j - 1, 1 - p)
                        if t == 4 and square:
                            squares(j - 1, 1 - p)

                act.wait_ge(halo_set, 1)
                act.wait_ge(side_free, 6 * TILES)
                conv_slot(0, 1, square=False)
                conv_slot(1, 0)
                with act.Fori(0, 2) as i:
                    conv_slot(i * 2 + 2, 1, True)
                    conv_slot(i * 2 + 3, 0, True)
                conv_slot(6, 1, False)
                conv_slot(7, 0, False)
                conv_slot(8, 1, False)
                conv_slot(9, 0, False, square=False)
                conv_slot(10, 1, square=False)
                conv_slot(11, 0, square=False)

                def gate_block(i, f, p):
                    def write(t, tile):
                        nc.scalar.copy(Y[:, p, t * TW:(t + 1) * TW], tile).then_inc(act_free, 1)
                    tiles(f, write)

                act.wait_ge(qkv_ready, 11)
                conv_sigmoid(11, 0)
                act.wait_ge(qkv_stored[1], 6 * 16)
                gate_block(0, F_GATE, 1)
                act.wait_ge(qkv_stored[0], 6 * 16)
                gate_block(0, F_GATE + 1, 0)
                with act.Fori(1, EARLY_GATES // 2) as i:
                    for p in (1, 0):
                        act.wait_ge(gate_stored[p], i * 16)
                        gate_block(i, i * 2 + (F_GATE + 1 - p), p)

            @block.vector
            def _(dve):
                dve.wait_ge(params_landed, PARAMS)
                g_rows = slice(AT_G, AT_G + 4)
                b_rows = slice(AT_B, AT_B + 4)
                dve.wait_ge(special_ready, 1)
                links = [0]

                def link(ins):
                    links[0] += 1
                    ins.then_inc(special_step, 1)
                    dve.wait_ge(special_step, links[0])

                link(nc.vector.tensor_scalar(X[g_rows, 0, 0:NT], X[g_rows, 0, 0:NT],
                                             small[g_rows, S_DT:S_DT + 1], None, ALU.add))
                nc.vector.scalar_tensor_tensor(T[g_rows, 0:NT], X[g_rows, 0, 0:NT], -1.0, X[g_rows, 0, 0:NT],
                                               ALU.mult, ALU.max).then_inc(dve_done, 1)
                link(nc.vector.tensor_scalar(X[b_rows, 0, 0:NT], X[b_rows, 0, 0:NT], 1.0, None, ALU.add))
                nc.vector.reciprocal(X[b_rows, 0, 0:NT], X[b_rows, 0, 0:NT])
                dve.wait_ge(act_done, 3)
                link(nc.vector.scalar_tensor_tensor(X[g_rows, 0, 0:NT], X[g_rows, 0, 0:NT], 0.0,
                                                    T[g_rows, 0:NT], ALU.max, ALU.add))
                link(nc.vector.tensor_scalar(X[g_rows, 0, 0:NT], X[g_rows, 0, 0:NT],
                                             small[g_rows, S_NEGA:S_NEGA + 1], -1.0, ALU.mult, ALU.mult))
                for b in range(2):
                    if b == 1:
                        dve.wait_ge(special_stored, 16)
                    for t in range(TILES):
                        n = b * TILES + t
                        dve.wait_ge(side_ready, n + 1)
                        nc.vector.tensor_scalar(T[:, t * TW:(t + 1) * TW], side[:, n % 2, 0:TW],
                                                small[:, S_BF + b:S_BF + b + 1], None,
                                                ALU.add).then_inc(side_free, 1)
                    dve.wait_ge(side_free, (b + 1) * TILES)
                    nc.vector.scalar_tensor_tensor(X[:, 1, 0:NT], T[:, 0:NT], -1.0, T[:, 0:NT],
                                                   ALU.mult, ALU.max).then_inc(dve_done, 1)
                    dve.wait_ge(act_done, 5 + 2 * b)
                    nc.vector.scalar_tensor_tensor(T[:, 0:NT], T[:, 0:NT], 0.0, X[:, 1, 0:NT],
                                                   ALU.min, ALU.subtract).then_inc(logf_ready, 1)

                def silu_block(f, m, p):
                    for t in range(TILES):
                        dve.wait_ge(sig_ready, m * TILES + (t + 1))
                        b = f - F_SILU
                        nc.vector.scalar_tensor_tensor(Y[:, p, t * TW:(t + 1) * TW], dense[:, t % 2, 0:TW],
                                                       column(small, b + S_ZNORM), sig[:, t % 2],
                                                       ALU.mult, ALU.mult).then_inc(dve_free, 1)

                dve.wait_ge(copy_stored[1], 4 * 16)
                silu_block(F_SILU, 0, 1)
                dve.wait_ge(copy_stored[0], 4 * 16)
                silu_block(F_SILU + 1, 1, 0)
                with dve.Fori(1, 4) as i:
                    for p in (1, 0):
                        dve.wait_ge(silu_stored[p], i * 16)
                        silu_block(i * 2 + (F_SILU + 1 - p), i * 2 + (1 - p), p)

                def step(ins):
                    steps[0] += 1
                    ins.then_inc(pool_step, 1)
                    dve.wait_ge(pool_step, steps[0])
                steps = [0]
                dve.wait_ge(special_stored, 3 * 16)
                dve.wait_ge(silu_stored[0], 4 * 16)
                dve.wait_ge(silu_stored[1], 4 * 16)
                for g in range(4):
                    win = 2 << g
                    span = NT + 2 * POOL_HALO
                    dve.wait_ge(act_free, (A_POOL + g) * TILES + TILES)
                    U = X[:, 0]
                    nc.vector.memset(U[:, 0:POOL_HALO], 0.0)
                    step(nc.vector.tensor_copy(U[:, POOL_HALO + NP_:2 * POOL_HALO + NP_],
                                               pool_out[:, 1, g]))
                    nc.vector.tensor_copy(pool_out[:, 0, g], U[:, NP_:NP_ + POOL_HALO])
                    step(nc.vector.tensor_copy(pool_out[:, 1, g], U[:, NT + POOL_HALO:NT + 2 * POOL_HALO]))
                    src, w = U, 1
                    turn = [T, X[:, 1]]
                    for n in range(g + 1):
                        dst = turn[(g - n) % 2]
                        step(nc.vector.tensor_tensor(dst[:, 2 * w - 1:span], src[:, 2 * w - 1:span],
                                                     src[:, w - 1:span - w], ALU.add))
                        src, w = dst, 2 * w
                    step(nc.vector.scalar_tensor_tensor(
                        src[:, POOL_HALO:POOL_HALO + win - 1], src[:, POOL_HALO:POOL_HALO + win - 1],
                        float(win), consts[:, C_CNT:C_CNT + win - 1], ALU.mult, ALU.mult))
                    D = X[:, 1]
                    nc.vector.scalar_tensor_tensor(D[:, 0:NP_], src[:, POOL_HALO:POOL_HALO + NP_], 1.0 / win,
                                                   U[:, POOL_HALO:POOL_HALO + NP_], ALU.mult, ALU.subtract)
                    nc.vector.scalar_tensor_tensor(
                        D[:, NP_:NT], src[:, 2 * POOL_HALO + NP_:2 * POOL_HALO + NT], 1.0 / win,
                        U[:, 2 * POOL_HALO + NP_:2 * POOL_HALO + NT], ALU.mult,
                        ALU.subtract).then_inc(pool_d_ready, 1)
                    for t in range(TILES):
                        dve.wait_ge(sig_ready, (8 + g) * TILES + t + 1)
                        nc.vector.tensor_tensor(Y[:, 0, t * TW:(t + 1) * TW], dense[:, t % 2, 0:TW],
                                                sig[:, t % 2], ALU.mult).then_inc(dve_free, 1)
                    if g >= 1:
                        dve.wait_ge(pool_stored, 16 * g)
                    for t in range(TILES):
                        n = (2 + g) * TILES + t
                        dve.wait_ge(side_ready, n + 1)
                        nc.vector.scalar_tensor_tensor(
                            Y[:, 1, t * TW:(t + 1) * TW], side[:, n % 2, 0:TW],
                            small[:, S_PSCALE + g:S_PSCALE + g + 1], Y[:, 0, t * TW:(t + 1) * TW],
                            ALU.mult, ALU.mult).then_inc(side_free, 1)

                for p in range(2):
                    last = nc.vector.memset(X[:, p, 0:CONV_HALO], 0.0)
                last.then_inc(halo_set, 1)
                SLOT_LINKS = 4

                def conv(j, p, stored=None):
                    def tap(n, ins):
                        ins.then_inc(conv_step, 1)
                        dve.wait_ge(conv_step, j * SLOT_LINKS + n)

                    dve.wait_ge(act_free, j * TILES + (A_CONV * TILES + TILES))
                    tap(1, nc.vector.tensor_copy(X[:, p, CONV_HALO + NP_:2 * CONV_HALO + NP_],
                                                 conv_cache[:, bass.ds(j, 1), :].rearrange("p a b -> p (a b)")))
                    for s, end in ((0, CONV_HALO + NP_), (1, 2 * CONV_HALO + NT)):
                        nc.vector.tensor_copy(conv_out[:, s, bass.ds(j, 1), :].rearrange("p a b -> p (a b)"),
                                              X[:, p, end - CONV_HALO:end])
                    if stored is not None:
                        dve.wait_ge(qkv_stored[p], stored)

                    def w(i):
                        return small[:, bass.ds(j * 4 + (S_CONV + i), 1)]
                    runs = ((0, NP_, 0), (NP_, NT, CONV_HALO))
                    for i in range(4):
                        for a, b, off in runs:
                            src = X[:, p, a + off + i:b + off + i]
                            if i == 0:
                                ins = nc.vector.tensor_scalar(Y[:, p, a:b], src, w(0), None, ALU.mult)
                            else:
                                ins = nc.vector.scalar_tensor_tensor(Y[:, p, a:b], src, w(i), Y[:, p, a:b],
                                                                     ALU.mult, ALU.add)
                        if i < 3:
                            tap(2 + i, ins)
                        else:
                            ins.then_inc(conv_ready, 1)

                def conv_silu(j, p, last=False):
                    dve.wait_ge(conv_sig_ready, j + 1)
                    ins = nc.vector.tensor_tensor(Y[:, p, 0:NT], Y[:, p, 0:NT], T[:, 0:NT], ALU.mult)
                    ins.then_inc(qkv_ready if last else conv_silu_ready, 1)

                def conv_norm(j, p):
                    dve.wait_ge(norm_ready, j + 1)
                    nc.vector.tensor_tensor(Y[:, p, 0:NT], Y[:, p, 0:NT], T[:, 0:NT],
                                            ALU.mult).then_inc(qkv_ready, 1)

                dve.wait_ge(pool_stored, 4 * 16)
                conv(0, 1)
                conv_silu(0, 1)
                conv(1, 0)
                conv_norm(0, 1)
                conv_silu(1, 0)
                with dve.Fori(0, 3) as i:
                    conv(i * 2 + 2, 1, i * 16 + 16)
                    conv_norm(i * 2 + 1, 0)
                    conv_silu(i * 2 + 2, 1)
                    conv(i * 2 + 3, 0, i * 16 + 16)
                    conv_norm(i * 2 + 2, 1)
                    conv_silu(i * 2 + 3, 0)
                conv(8, 1, 4 * 16)
                conv_norm(7, 0)
                conv_silu(8, 1, last=True)
                conv(9, 0, 4 * 16)
                conv_silu(9, 0, last=True)
                conv(10, 1, 5 * 16)
                conv_silu(10, 1, last=True)
                conv(11, 0, 5 * 16)
                conv_silu(11, 0, last=True)
                for t in range(TILES):
                    dve.wait_ge(dense_ready, (F_LATE - 1) * TILES + t + 1)
                    cols = slice(t * TW, (t + 1) * TW)
                    nc.vector.tensor_tensor(h_all[:, :, cols], hi[:, :, cols].bitcast(F32),
                                            lo[:, :, cols].bitcast(F32), ALU.add)

            @block.sync
            def _(sp):
                def load(i, f, p):
                    sp.dma_start(w_raw[:, p], d["w_in"][bass.ds(f, 1)].rearrange("a p n -> p (a n)")) \
                        .then_inc(w_landed[p], 16)

                load(0, 0, 0)
                for dst, src in (
                        (small[:, S_BF:S_BF + 2], d["gla_bf"]),
                        (small[:, S_PSCALE:S_PSCALE + 4], d["pool_scale"]),
                        (small[:, S_ZNORM:S_ZNORM + 4], d["gla_norm"]),
                        (small[:, S_ZNORM + 4:S_ZNORM + 8], d["gdn_norm"]),
                        (small[:, S_CONV:S_CONV + 48], d["gdn_conv"]),
                        (small[:, S_EPS:S_EPS + 2], d["scalars"]),
                        (small[AT_G:AT_G + 4, S_NEGA:S_NEGA + 1], d["gdn_a_log"]),
                        (small[AT_G:AT_G + 4, S_DT:S_DT + 1], d["gdn_dt_bias"]),
                        (wf2[:, :], d["gla_wf2"]),
                        (pool_w[:, :, :], d["pool_w"]),
                        (conv_cache[:, :, :], d["conv_cache"]),
                        (pool_out[:, 1], d["pool_cache"]),
                ):
                    sp.dma_start(dst, src).then_inc(params_landed, 16)
                load(0, 1, 1)

                def load_next(f, p):
                    sp.wait_ge(w_split, f + 1)
                    load(None, f + 2, p)

                def store(dst, row, ready, count, stored):
                    sp.wait_ge(ready, count)
                    sp.dma_start(dst, row).then_inc(stored, 16)

                load_next(0, 0)

                def copied(i, p):
                    load_next(i * 2 + (F_COPY + 1 - p), p)
                    sp.wait_ge(act_free, i * (2 * TILES) + (A_COPY + 2 - p) * TILES)
                    sp.dma_start(feat[:, bass.ds(i * 2 + (1 - p), 1)].rearrange("p a n -> p (a n)"),
                                 Y[:, p, 0:NT]).then_inc(copy_stored[p], 16)

                copied(0, 1)
                copied(0, 0)
                store(feat[:, R_LOGF], T[:, 0:NT], logf_ready, 1, special_stored)
                copied(1, 1)
                copied(1, 0)
                store(feat[:, R_LOGF + 1], T[:, 0:NT], logf_ready, 2, special_stored)
                store(feat[:, R_GB], X[:, 0, 0:NT], logf_ready, 2, special_stored)
                with sp.Fori(2, 4) as i:
                    for p in (1, 0):
                        copied(i, p)
                with sp.Fori(0, 4) as i:
                    for p in (1, 0):
                        load_next(i * 2 + (F_SILU + 1 - p), p)
                        sp.wait_ge(dve_free, i * (2 * TILES) + (2 - p) * TILES)
                        sp.dma_start(feat[:, bass.ds(i * 2 + (R_GLA_Z + 1 - p), 1)]
                                     .rearrange("p a n -> p (a n)"), Y[:, p, 0:NT]) \
                            .then_inc(silu_stored[p], 16)
                for g in range(4):
                    load_next(F_POOL + 2 * g, 1)
                    load_next(F_POOL + 2 * g + 1, 0)
                    store(outs[:, 4 + g], Y[:, 1, 0:NT], side_free, (3 + g) * TILES, pool_stored)
                load_next(F_CONV, 1)
                load_next(F_CONV + 1, 0)
                with sp.Fori(0, 5) as i:
                    for p in (1, 0):
                        load_next(i * 2 + (F_CONV + 3 - p), p)
                        sp.wait_ge(qkv_ready, i * 2 + (2 - p))
                        sp.dma_start(feat[:, bass.ds(i * 2 + (R_GDN_Q + 1 - p), 1)]
                                     .rearrange("p a n -> p (a n)"), Y[:, p, 0:NT]) \
                            .then_inc(qkv_stored[p], 16)
                load_next(F_GATE, 1)
                store(feat[:, R_GDN_V + 2], Y[:, 1, 0:NT], qkv_ready, 11, qkv_stored[1])
                load_next(F_GATE + 1, 0)
                store(feat[:, R_GDN_V + 3], Y[:, 0, 0:NT], qkv_ready, 12, qkv_stored[0])
                sp.dma_start(d["new_pool_prompt"], pool_out[:, 0]).then_inc(caches_stored, 16)
                sp.dma_start(d["new_pool_sample"], pool_out[:, 1]).then_inc(caches_stored, 16)
                sp.dma_start(d["new_conv_prompt"], conv_out[:, 0]).then_inc(caches_stored, 16)
                sp.dma_start(d["new_conv_sample"], conv_out[:, 1]).then_inc(caches_stored, 16)
                with sp.Fori(0, EARLY_GATES // 2 - 2) as i:
                    for p in (1, 0):
                        load_next(i * 2 + (F_GATE + 3 - p), p)
                        sp.wait_ge(act_free, i * (2 * TILES) + (A_GATE + 2 - p) * TILES)
                        sp.dma_start(gates[:, bass.ds(i * 2 + (1 - p), 1)].rearrange("p a n -> p (a n)"),
                                     Y[:, p, 0:NT]).then_inc(gate_stored[p], 16)
                for n in range(EARLY_GATES - 4, EARLY_GATES):
                    p = 1 - n % 2
                    store(gates[:, n], Y[:, p, 0:NT], act_free, (A_GATE + n + 1) * TILES, gate_stored[p])
                sp.wait_ge(caches_stored, 4 * 16)
                for p in range(2):
                    sp.wait_ge(gate_stored[p], EARLY_GATES // 2 * 16)


def chunk_phase(nc, d, consts, h_all, late):
    TURNS = LEVELS - 2
    with ExitStack() as ctx, Held(nc) as held:
        def sb(name, shape, dt=F32):
            return ctx.enter_context(nc.sbuf_tensor(name, shape, dt))

        def bank(name, shape=(P, HEADS, P)):
            return ctx.enter_context(nc.psum_tensor(name, list(shape), F32))

        masks = sb("masks", [P, M_END])
        gate_w = sb("gate_w", [P, 2, KD, P])
        gate_row = sb("gate_row", [P, 2, TW])
        eps = sb("chunk_eps", [P, 1])
        inputs = sb("inputs", [P, 2, R_END, P])
        decay_beta = sb("decay_beta", [P, 2, HEADS])
        g_col = sb("g_col", [P, HEADS])
        g_row = sb("g_row", [P, HEADS, P])
        e_row = sb("e_row", [P, HEADS, P])
        d_col = sb("d_col", [P, HEADS])
        diff = sb("diff", [P, HEADS, P])
        dec_kk = sb("dec_kk", [P, HEADS, P])
        dec_qk = sb("dec_qk", [P, HEADS, P])
        M = sb("M", [P, HEADS, P])
        M0 = sb("M0", [P, HEADS, P])
        X = sb("X", [P, HEADS, P])
        XT = sb("XT", [P, HEADS, P])
        XTb = sb("XTb", [P, HEADS, P])
        Z = sb("Z", [P, HEADS, HALF])
        att = sb("att", [P, HEADS, P])
        k_dec = sb("k_dec", [P, HEADS, P])
        q_dec = sb("q_dec", [P, HEADS, P])
        k_tok = sb("k_tok", [P, HEADS, P])
        v_tok = sb("v_tok", [P, HEADS, P])
        rhs = sb("rhs", [P, HEADS, P])
        U = sb("U", [P, HEADS, P])
        state = sb("state", [P, HEADS, P])
        b_sum = sb("b_sum", [P, 2, P])
        F = sb("F", [P, LEVELS + 2, 2, P])
        KF = sb("KF", [P, LEVELS + 1, 2, P])
        QF = sb("QF", [P, LEVELS + 1, 2, P])
        masked = sb("masked", [P, HEADS, LEVELS, HALF])
        gla_att = sb("gla_att", [P, HEADS, P])
        gla_v = sb("gla_v", [P, HEADS, P])
        gla_k = sb("gla_k", [P, 2, P])
        gla_state = sb("gla_state", [P, HEADS, P])
        sq = [sb("sq_gdn", [P, HEADS, P]), sb("sq_gla", [P, HEADS, P])]
        oz = [sb("oz_gdn", [P, HEADS, P]), sb("oz_gla", [P, HEADS, P])]
        out_sb = [sb("out_gdn", [P, HEADS, P]), sb("out_gla", [P, HEADS, P])]

        level_bank = bank("level_bank", (P, 2, HEADS, HALF))
        z_bank, xt_bank = level_bank[:, 0], level_bank[:, 1]
        x_bank = bank("x_bank")
        pair_bank = bank("pair_bank", (P, 8, HALF))
        gate_bank = bank("gate_bank", (P, 2, 512))
        ring = [bank("ring0"), bank("ring1"), bank("ring2")]

        ident = consts[:, C_IDENT:C_IDENT + P]
        ones = consts[:, C_ONES:C_ONES + P]
        upper = masks[:, M_UPPER:M_UPPER + P]
        level_masks = masks[:, M_PAIRS:M_END].rearrange("p (l t) -> p l t", t=HALF)

        ITEMS = ("gbt", "gcol", "vt", "kt", "grow", "KK", "QK", "vtg", "diag_even", "diag", "m0t", "R", "kdtg", "Og", "U", "O", "dS",
                 "dSg", "SSQ", "SSQg")
        PE_ = ITEMS
        DVE_ = ("gb_taken", "gcol_taken", "kt_taken", "KK_taken", "QK_taken", "m0t_taken", "R_taken",
                "O_scaled", "Og_scaled", "dS_taken", "dSg_taken", "b_ready", "F_diffs", "KF_ready",
                "XTb_ready", "dcol_diff",
                "diag_taken")
        ACT_ = ("vt_taken", "grow_taken", "e_row_ready", "d_col_ready", "dec_qk_ready", "dec_kk_ready",
                "vtg_taken", "kdtg_taken", "U_taken", "F_abs", "F_ready", "O_squared", "Og_squared", "SSQ_taken",
                "SSQg_taken", "rs_ready", "rsg_ready")
        POOL_ = ("diff_ready", "dec_args", "M0_ready", "X_ready", "k_dec_ready", "q_dec_ready", "QF_ready",
                 "gla_att_ready", "out_ready", "outg_ready")
        EARLY = {"SSQ_taken", "SSQg_taken", "dSg_taken", "dSg", "dS_taken", "O", "Og", "out_ready", "outg_ready",
                 "R_taken", "dec_args", "KK_taken", "QK_taken", "QF_ready", "q_dec_ready", "kdtg"}
        S = {n: held.add(nc.alloc_semaphore(n)) for n in PE_ + DVE_ + ACT_ + POOL_}
        z_ready = held.add(nc.alloc_semaphore("z_ready"))
        z_taken = held.add(nc.alloc_semaphore("z_taken"))
        xt_products = held.add(nc.alloc_semaphore("xt_products"))
        xt_updated = held.add(nc.alloc_semaphore("xt_updated"))
        x_turned = held.add(nc.alloc_semaphore("x_turned"))
        x_taken = held.add(nc.alloc_semaphore("x_taken"))
        pairs_ready = held.add(nc.alloc_semaphore("pairs_ready"))
        pairs_masked = held.add(nc.alloc_semaphore("pairs_masked"))
        att_added = held.add(nc.alloc_semaphore("att_added"))
        gate_w_landed = [held.add(nc.alloc_semaphore(f"gate_w_landed{p}")) for p in range(2)]
        gate_ready = held.add(nc.alloc_semaphore("gate_ready"))
        gate_taken = held.add(nc.alloc_semaphore("gate_taken"))
        gate_stored = [held.add(nc.alloc_semaphore(f"late_gate_stored{p}")) for p in range(2)]
        in_landed = [held.add(nc.alloc_semaphore(f"in_landed{p}")) for p in range(2)]
        masks_landed = held.add(nc.alloc_semaphore("masks_landed"))
        eps_ready = held.add(nc.alloc_semaphore("eps_ready"))
        state_landed = held.add(nc.alloc_semaphore("state_landed"))
        state_stored = held.add(nc.alloc_semaphore("state_stored"))
        state_zero = held.add(nc.alloc_semaphore("state_zero"))
        out_stored = held.add(nc.alloc_semaphore("out_stored"))
        outg_stored = held.add(nc.alloc_semaphore("outg_stored"))
        feat, outs, gates = d["feat"], d["branch_out"], d["gates"]

        def now(eng, name, c):
            eng.wait_ge(S[name], c + (2 if name in EARLY else 1))

        def before(eng, name, c):
            assert name in EARLY, name
            eng.wait_ge(S[name], c + 1)

        def preload(eng, names):
            for name in names:
                if name in EARLY:
                    eng.sem_inc(S[name], 1)

        def half_of(h):
            return slice(64 * (h % 2), 64 * (h % 2) + 64)

        def levels_of(n):
            return n.bit_length() - 1

        with nc.Block() as block:
            @block.sync
            def _(sp):
                def load(c, p, n=P):
                    sp.dma_start(inputs[:, p, :, 0:n], feat[:, :, bass.ds(c * P, n)]).then_inc(in_landed[p], 16)

                def load_gate_w(block, p):
                    sp.dma_start(gate_w[:, p].rearrange("p k m -> p (k m)"),
                                 d["w_in"][bass.ds(block + F_LATE, 1)].rearrange("a p n -> p (a n)")) \
                        .then_inc(gate_w_landed[p], 16)

                def store_gates(c):
                    for t in range(TILES):
                        sp.wait_ge(gate_taken, c * TILES + (t + 3))
                        sp.dma_start(gates[:, bass.ds(c + EARLY_GATES, 1), t * TW:(t + 1) * TW]
                                     .rearrange("p a n -> p (a n)"), gate_row[:, t % 2]) \
                            .then_inc(gate_stored[t % 2], 16)

                def store(c, n=P):
                    now(sp, "outg_ready", c)
                    sp.dma_start(outs[:, 0:4, bass.ds(c * P, n)], out_sb[1][:, :, 0:n]).then_inc(outg_stored, 16)
                    now(sp, "out_ready", c)
                    sp.dma_start(outs[:, 8:12, bass.ds(c * P, n)], out_sb[0][:, :, 0:n]).then_inc(out_stored, 16)

                sp.sem_inc(out_stored, 16)
                sp.sem_inc(outg_stored, 16)
                for q in range(2):
                    sp.sem_inc(gate_stored[q], 16)
                load(0, 0)
                load_gate_w(0, 0)
                sp.dma_start(masks[:, :], d["masks"]).then_inc(masks_landed, 16)
                load(1, 1)
                load_gate_w(1, 1)
                with sp.Fori(0, CHUNKS // 2 - 1) as i:
                    for p in range(2):
                        c = i * 2 + p
                        store_gates(c)
                        load_gate_w(i * 2 + (p + 2), p)
                        store(c)
                        load(i * 2 + (p + 2), p)
                store_gates(CHUNKS - 2)
                store(CHUNKS - 2)
                load(CHUNKS, 0, NS_)
                store_gates(CHUNKS - 1)
                store(CHUNKS - 1)
                now(sp, "dS_taken", CHUNKS - 1)
                now(sp, "dSg_taken", CHUNKS - 1)
                sp.dma_start(d["new_gdn_prompt"].rearrange("h d v -> d h v"), state[:, :, :]).then_inc(state_stored, 16)
                for h in range(HEADS):
                    sp.dma_start(d["new_gla_prompt"][h], gla_state[half_of(h), h]).then_inc(state_stored, 16)
                sp.wait_ge(state_stored, 5 * 16)
                sp.dma_start(state[:, :, :], d["state_gdn"].rearrange("h d v -> d h v")).then_inc(state_landed, 16)
                for h in range(HEADS):
                    sp.dma_start(gla_state[half_of(h), h], d["state_gla"][h]).then_inc(state_landed, 16)
                late.load_in_chunk_phase(sp, d)
                store(CHUNKS, NS_)
                now(sp, "dS_taken", CHUNKS)
                now(sp, "dSg_taken", CHUNKS)
                sp.dma_start(d["new_gdn_sample"].rearrange("h d v -> d h v"), state[:, :, :]).then_inc(state_stored, 16)
                for h in range(HEADS):
                    sp.dma_start(d["new_gla_sample"][h], gla_state[half_of(h), h]).then_inc(state_stored, 16)
                sp.wait_ge(state_stored, 10 * 16)
                sp.wait_ge(out_stored, 16 * (CHUNKS + 2))
                sp.wait_ge(outg_stored, 16 * (CHUNKS + 2))
                for q in range(2):
                    sp.wait_ge(gate_stored[q], 16 * (LATE_GATES * TILES // 2 + 1))

            def per_chunk(eng, chunk):
                with eng.Fori(0, CHUNKS // 2) as i:
                    chunk(i * 2, i, 0, P)
                    chunk(i * 2 + 1, i, 1, P)
                chunk(CHUNKS, CHUNKS // 2, 0, NS_)

            @block.tensor
            def _(pe):
                matmul, transpose = nc.tensor.matmul, nc.tensor.transpose

                def chunk(c, i, p, n):
                    I = inputs[:, p]
                    L = levels_of(n)
                    sample = isinstance(c, int) and c == CHUNKS
                    steps = [0]

                    def gate_products(count):
                        for g in range(steps[0], 0 if sample else steps[0] + count):
                            t, k = g // KD, g % KD
                            if g == 0:
                                pe.wait_ge(gate_w_landed[p], i * 16 + 16)
                            if k == 0:
                                pe.wait_ge(gate_taken, c * TILES + (t + 1))
                            mm = matmul(gate_bank[:, t % 2, 0:TW], gate_w[:, p, k],
                                        h_all[:, k, t * TW:(t + 1) * TW], start=(k == 0), stop=(k == KD - 1))
                            if k == KD - 1:
                                mm.then_inc(gate_ready, 1)
                        steps[0] += count

                    gate_products(4)
                    pe.wait_ge(in_landed[p], i * 16 + 16)
                    before(pe, "SSQ_taken", c)
                    transpose(ring[0][0:n, 0], I[:, R_GB, 0:n], ident).then_inc(S["gbt"], 1)
                    before(pe, "SSQg_taken", c)
                    for h in range(HEADS):
                        mm = transpose(ring[1][0:n, h], I[:, R_GDN_V + h, 0:n], ident)
                    mm.then_inc(S["vt"], 1)
                    before(pe, "dSg_taken", c)
                    for h in range(HEADS):
                        mm = transpose(ring[2][0:n, h], I[:, R_GDN_K + h, 0:n], ident)
                    mm.then_inc(S["kt"], 1)
                    gate_products(2)
                    now(pe, "gb_taken", c)
                    matmul(ring[0][0:n, 1, 0:HEADS], upper[0:n, 0:n], decay_beta[0:n, 0, :],
                           start=True, stop=True).then_inc(S["gcol"], 1)
                    gate_products(2)
                    now(pe, "gcol_taken", c)
                    for h in range(HEADS):
                        mm = matmul(ring[0][:, h, 0:n], decay_beta[0:n, 0, h:h + 1].to_broadcast([n, P]),
                                    upper[0:n, 0:n], start=True, stop=True)
                    mm.then_inc(S["grow"], 1)
                    now(pe, "vt_taken", c)
                    for h in range(HEADS):
                        k = I[:, R_GDN_K + h, 0:n]
                        mm = matmul(ring[1][0:n, h, 0:n], k, k, start=True, stop=True)
                    mm.then_inc(S["KK"], 1)
                    now(pe, "kt_taken", c)
                    for h in range(HEADS):
                        mm = matmul(ring[2][0:n, h, 0:n], I[:, R_GDN_K + h, 0:n], I[:, R_GDN_Q + h, 0:n],
                                    start=True, stop=True)
                    mm.then_inc(S["QK"], 1)
                    gate_products(2)
                    now(pe, "grow_taken", c)
                    for h in range(HEADS):
                        mm = transpose(ring[0][0:n, h], I[:, R_GLA_V + h, 0:n], ident)
                    mm.then_inc(S["vtg"], 1)
                    gate_products(6)
                    now(pe, "M0_ready", c)
                    now(pe, "KK_taken", c)
                    for h in range(HEADS):
                        mm = transpose(ring[1][0:n, h, 0:n], M0[0:n, h, 0:n], ident[0:n, 0:n])
                    mm.then_inc(S["m0t"], 1)
                    gate_products(2)
                    now(pe, "QK_taken", c)
                    now(pe, "k_dec_ready", c)
                    before(pe, "dS_taken", c)
                    if sample:
                        pe.wait_ge(state_landed, 5 * 16)
                    for h in range(HEADS):
                        mm = matmul(ring[2][0:n, h], k_dec[:, h, 0:n], state[:, h], start=True, stop=True)
                    mm.then_inc(S["R"], 1)

                    def pairs(h):
                        rows = half_of(h)
                        b = h // 2
                        if h == 0:
                            now(pe, "KF_ready", c)
                            now(pe, "QF_ready", c)
                            pe.wait_ge(pairs_masked, c * HEADS + 1)
                        else:
                            pe.wait_ge(pairs_masked, c * HEADS + h + 1)
                        for l in range(L):
                            s = 1 << l
                            mm = matmul(halves_packed(pair_bank[0:n, l:l + 1, 0:n // 2], s)[:, 0],
                                        KF[rows, l, b, 0:n], second_halves(QF[rows, l + 1, b:b + 1, 0:n], s)[:, 0],
                                        start=True, stop=True)
                        mm.then_inc(pairs_ready, 1)

                    def own_pairs(first, signal):
                        for h in (first, first + 2):
                            rows, b = half_of(h), h // 2
                            mm = matmul(ring[0][0:n, h, 0:n], I[rows, R_GLA_K + b, 0:n], I[rows, R_GLA_Q + b, 0:n],
                                        start=True, stop=True)
                        mm.then_inc(S[signal], 1)

                    def first_pairs():
                        now(pe, "vtg_taken", c)
                        own_pairs(0, "diag_even")
                        pairs(0)
                        now(pe, "diag_even", c)
                        own_pairs(1, "diag")

                    def key_turns():
                        now(pe, "diag_taken", c)
                        for b in range(2):
                            mm = transpose(ring[0][0:n, b], KF[:, LEVELS, b, 0:n], ident)
                        mm.then_inc(S["kdtg"], 1)

                    between = {0: first_pairs, 1: lambda: pairs(1), 2: lambda: pairs(2),
                               3: lambda: pairs(3), 4: key_turns}
                    for l in range(1, L):
                        s = 1 << l
                        gate_products(2)
                        if l == 1:
                            now(pe, "m0t_taken", c)
                            now(pe, "X_ready", c)
                        else:
                            pe.wait_ge(xt_updated, c * (LEVELS - 1) + (l - 1))
                        for h in range(HEADS):
                            mm = matmul(halves_packed(z_bank[0:n, h:h + 1, 0:n // 2], s)[:, 0], M[0:n, h, 0:n],
                                        second_halves(XT[0:n, h:h + 1, 0:n], s)[:, 0], start=True, stop=True)
                        mm.then_inc(z_ready, 1)
                        if l > 1:
                            for h in range(HEADS):
                                mm = transpose(x_bank[0:n, h, 0:n], XT[0:n, h, 0:n], ident[0:n, 0:n])
                            mm.then_inc(x_turned, 1)
                        if l - 1 in between:
                            between[l - 1]()
                        gate_products(1)
                        pe.wait_ge(z_taken, c * (LEVELS - 1) + l)
                        if l > 1:
                            pe.wait_ge(x_taken, c * TURNS + (l - 1))
                        for h in range(HEADS):
                            mm = matmul(halves_packed(xt_bank[0:n, h:h + 1, 0:n // 2], s)[:, 0], X[0:n, h, 0:n],
                                        halves_packed(Z[0:n, h:h + 1, 0:n // 2], s)[:, 0], start=True, stop=True)
                        mm.then_inc(xt_products, 1)
                    if L - 1 < 5:
                        key_turns()
                    gate_products(4)
                    now(pe, "gla_att_ready", c)
                    now(pe, "m0t_taken", c)
                    before(pe, "dSg_taken", c)
                    for h in range(HEADS):
                        matmul(ring[1][:, h, 0:n], gla_v[0:n, h], gla_att[0:n, h, 0:n], start=True, stop=False)
                        mm = matmul(ring[1][:, h, 0:n], gla_state[:, h], QF[:, 0, h // 2, 0:n],
                                    start=False, stop=True)
                    mm.then_inc(S["Og"], 1)
                    now(pe, "R_taken", c)
                    now(pe, "XTb_ready", c)
                    for h in range(HEADS):
                        mm = matmul(ring[2][0:n, h], XTb[0:n, h, 0:n], rhs[0:n, h], start=True, stop=True)
                    mm.then_inc(S["U"], 1)
                    gate_products(3)
                    now(pe, "kdtg_taken", c)
                    now(pe, "q_dec_ready", c)
                    now(pe, "U_taken", c)
                    for h in range(HEADS):
                        matmul(ring[0][:, h, 0:n], U[0:n, h], att[0:n, h, 0:n], start=True, stop=False)
                        mm = matmul(ring[0][:, h, 0:n], state[:, h], q_dec[:, h, 0:n], start=False, stop=True)
                    mm.then_inc(S["O"], 1)
                    now(pe, "Og_scaled", c)
                    now(pe, "Og_squared", c)
                    for h in range(HEADS):
                        mm = matmul(ring[1][:, h], k_tok[0:n, h], U[0:n, h], start=True, stop=True)
                    mm.then_inc(S["dS"], 1)
                    for h in range(HEADS):
                        mm = matmul(ring[2][:, h], gla_k[0:n, h // 2], gla_v[0:n, h], start=True, stop=True)
                    mm.then_inc(S["dSg"], 1)
                    gate_products(3)
                    now(pe, "O_scaled", c)
                    now(pe, "O_squared", c)
                    matmul(ring[0][:, :, 0:n], ones, sq[0][:, :, 0:n], start=True, stop=True).then_inc(S["SSQ"], 1)
                    gate_products(2)
                    now(pe, "dS_taken", c)
                    matmul(ring[1][:, :, 0:n], ones, sq[1][:, :, 0:n], start=True, stop=True).then_inc(S["SSQg"], 1)

                pe.wait_ge(masks_landed, 16)
                preload(pe, PE_)
                per_chunk(pe, chunk)

            @block.scalar
            def _(act):
                copy, activation = nc.scalar.copy, nc.scalar.activation

                def head_norm(c, n, which, ready, taken, done):
                    s = sq[which][:, :, 0:n]
                    now(act, ready, c)
                    activation(s, ring[which][:, :, 0:n], ACT.Ln, bias=eps[:, 0:1], scale=1.0 / P) \
                        .then_inc(S[taken], 1)
                    now(act, taken, c)
                    activation(s, s, ACT.Exp, scale=-0.5).then_inc(S[done], 1)

                def gates_out(c, t):
                    if isinstance(c, int) and c == CHUNKS:
                        return
                    act.wait_ge(gate_ready, c * TILES + (t + 1))
                    act.wait_ge(gate_stored[t % 2], c * (TILES // 2 * 16) + (t // 2 + 1) * 16)
                    copy(gate_row[:, t % 2], gate_bank[:, t % 2, 0:TW]).then_inc(gate_taken, 1)

                def chunk(c, i, p, n):
                    L = levels_of(n)
                    now(act, "vt", c)
                    before(act, "R_taken", c)
                    copy(v_tok[0:n], ring[1][0:n]).then_inc(S["vt_taken"], 1)
                    now(act, "grow", c)
                    before(act, "dec_args", c)
                    copy(g_row[:, :, 0:n], ring[0][:, :, 0:n]).then_inc(S["grow_taken"], 1)
                    now(act, "grow_taken", c)
                    before(act, "dS_taken", c)
                    before(act, "q_dec_ready", c)
                    activation(e_row[:, :, 0:n], g_row[:, :, 0:n], ACT.Exp).then_inc(S["e_row_ready"], 1)
                    gates_out(c, 0)
                    now(act, "dcol_diff", c)
                    activation(d_col[0:n], d_col[0:n], ACT.Exp).then_inc(S["d_col_ready"], 1)
                    now(act, "dec_args", c)
                    activation(dec_kk[0:n, :, 0:n], dec_kk[0:n, :, 0:n], ACT.Exp, scale=-1.0) \
                        .then_inc(S["dec_kk_ready"], 1)
                    activation(dec_qk[0:n, :, 0:n], dec_qk[0:n, :, 0:n], ACT.Exp) \
                        .then_inc(S["dec_qk_ready"], 1)
                    now(act, "F_diffs", c)
                    activation(F[:, :, :, 0:n], F[:, :, :, 0:n], ACT.Abs).then_inc(S["F_abs"], 1)
                    now(act, "F_abs", c)
                    activation(F[:, :, :, 0:n], F[:, :, :, 0:n], ACT.Exp, scale=-1.0 / 16).then_inc(S["F_ready"], 1)
                    now(act, "vtg", c)
                    before(act, "dSg", c)
                    copy(gla_v[0:n], ring[0][0:n]).then_inc(S["vtg_taken"], 1)
                    for t in range(1, 4):
                        gates_out(c, t)
                    now(act, "kdtg", c)
                    copy(gla_k[0:n], ring[0][0:n, 0:2]).then_inc(S["kdtg_taken"], 1)
                    now(act, "Og", c)
                    before(act, "outg_ready", c)
                    activation(sq[1][:, :, 0:n], ring[1][:, :, 0:n], ACT.Square).then_inc(S["Og_squared"], 1)
                    now(act, "U", c)
                    copy(U[0:n], ring[2][0:n]).then_inc(S["U_taken"], 1)
                    gates_out(c, 4)
                    now(act, "O", c)
                    before(act, "out_ready", c)
                    activation(sq[0][:, :, 0:n], ring[0][:, :, 0:n], ACT.Square).then_inc(S["O_squared"], 1)
                    head_norm(c, n, 0, "SSQ", "SSQ_taken", "rs_ready")
                    gates_out(c, 5)
                    head_norm(c, n, 1, "SSQg", "SSQg_taken", "rsg_ready")

                use_log_exp_tables(nc)
                act.wait_ge(eps_ready, 1)
                preload(act, ACT_)
                act.sem_inc(gate_taken, 2)
                per_chunk(act, chunk)

            @block.gpsimd
            def _(pool):
                tt = nc.gpsimd.tensor_tensor

                def chunk(c, i, p, n):
                    I = inputs[:, p]

                    def over_heads(x):
                        return x.rearrange("p (a b) -> p a b", a=1).to_broadcast([n, HEADS, n])
                    now(pool, "grow_taken", c)
                    now(pool, "gcol_taken", c)
                    tt(diff[0:n, :, 0:n], g_row[0:n, :, 0:n],
                       g_col[0:n].rearrange("p (a b) -> p a b", b=1).to_broadcast([n, HEADS, n]),
                       ALU.subtract).then_inc(S["diff_ready"], 1)
                    now(pool, "diff_ready", c)
                    before(pool, "KK_taken", c)
                    tt(dec_kk[0:n, :, 0:n], diff[0:n, :, 0:n], over_heads(masks[0:n, M_POS:M_POS + n]), ALU.add)
                    before(pool, "QK_taken", c)
                    tt(dec_qk[0:n, :, 0:n], diff[0:n, :, 0:n], over_heads(masks[0:n, M_NEG:M_NEG + n]),
                       ALU.add).then_inc(S["dec_args"], 1)
                    now(pool, "e_row_ready", c)
                    before(pool, "O", c)
                    tt(k_dec[:, :, 0:n], I[:, R_GDN_K:R_GDN_K + 4, 0:n], e_row[:, :, 0:n],
                       ALU.mult).then_inc(S["k_dec_ready"], 1)
                    now(pool, "KK_taken", c)
                    tt(M0[0:n, :, 0:n], M[0:n, :, 0:n], over_heads(masks[0:n, M_LOW:M_LOW + n]),
                       ALU.mult).then_inc(S["M0_ready"], 1)
                    now(pool, "M0_ready", c)
                    tt(X[0:n, :, 0:n], over_heads(ident[0:n, 0:n]), M0[0:n, :, 0:n],
                       ALU.subtract).then_inc(S["X_ready"], 1)
                    now(pool, "F_ready", c)
                    before(pool, "Og", c)
                    q = I[:, R_GLA_Q:R_GLA_Q + 2, 0:n].rearrange("p (l b) t -> p l b t", l=1)
                    for b in range(2):
                        last = tt(QF[:, :, b, 0:n], q[:, :, b].to_broadcast([P, LEVELS + 1, n]),
                                  F[:, 0:LEVELS + 1, b, 0:n], ALU.mult)
                    last.then_inc(S["QF_ready"], 1)
                    tt(q_dec[:, :, 0:n], I[:, R_GDN_Q:R_GDN_Q + 4, 0:n], e_row[:, :, 0:n],
                       ALU.mult).then_inc(S["q_dec_ready"], 1)
                    now(pool, "diag_taken", c)
                    pool.wait_ge(pairs_masked, c * HEADS + (HEADS + 1))
                    L = levels_of(n)
                    for l in range(L):
                        s = 1 << l
                        own = second_halves(gla_att[0:n, :, 0:n], s)
                        ins = tt(own, own, halves_packed(masked[0:n, :, l, 0:n // 2], s), ALU.add)
                        if l < L - 1:
                            ins.then_inc(att_added, 1)
                            pool.wait_ge(att_added, c * (LEVELS - 1) + (l + 1))
                        else:
                            ins.then_inc(S["gla_att_ready"], 1)
                    now(pool, "rs_ready", c)
                    now(pool, "O_scaled", c)
                    pool.wait_ge(out_stored, c * 16 + 16)
                    tt(out_sb[0][:, :, 0:n], oz[0][:, :, 0:n], sq[0][:, :, 0:n], ALU.mult).then_inc(S["out_ready"], 1)
                    now(pool, "rsg_ready", c)
                    pool.wait_ge(outg_stored, c * 16 + 16)
                    tt(out_sb[1][:, :, 0:n], oz[1][:, :, 0:n], sq[1][:, :, 0:n], ALU.mult).then_inc(S["outg_ready"], 1)

                preload(pool, POOL_)
                per_chunk(pool, chunk)

            @block.vector
            def _(dve):
                tt, stt, cp = nc.vector.tensor_tensor, nc.vector.scalar_tensor_tensor, nc.vector.tensor_copy

                def chunk(c, i, p, n):
                    I = inputs[:, p]
                    L = levels_of(n)

                    def over_heads(x, m=HEADS):
                        return x.rearrange("p (a b) -> p a b", a=1).to_broadcast([n, m, n])

                    def per_token(x, w=P):
                        return x.rearrange("p (a b) -> p a b", b=1).to_broadcast([n, HEADS, w])
                    beta = decay_beta[0:n, 1]
                    dve.wait_ge(in_landed[p], i * 16 + 16)
                    for b in range(2):
                        last = nc.vector.tensor_tensor_scan(b_sum[:, b, 0:n], ones[:, 0:n], I[:, R_LOGF + b, 0:n],
                                                            0.0, ALU.mult, ALU.add)
                    last.then_inc(S["b_ready"], 1)
                    now(dve, "gbt", c)
                    cp(decay_beta[0:n], ring[0][0:n, 0].rearrange("p (a b) -> p a b", b=32)[:, 1:3, 0:HEADS]) \
                        .then_inc(S["gb_taken"], 1)
                    now(dve, "b_ready", c)
                    before(dve, "QF_ready", c)
                    for b in range(2):
                        bs = b_sum[:, b, 0:n]
                        cp(F[:, 0, b, 0:n], bs)
                        for l in range(LEVELS):
                            s = 1 << l
                            if l >= L:
                                cp(F[:, l + 1, b, 0:n], bs)
                                continue
                            blocks = bs.rearrange("p (m t) -> p m t", t=2 * s)
                            tt(F[:, l + 1, b, 0:n].rearrange("p (m t) -> p m t", t=2 * s), blocks,
                               blocks[:, :, s - 1:s].to_broadcast([P, n // (2 * s), 2 * s]), ALU.subtract)
                        last = tt(F[:, LEVELS + 1, b, 0:n], bs, bs[:, n - 1:n].to_broadcast([P, n]), ALU.subtract)
                    last.then_inc(S["F_diffs"], 1)
                    now(dve, "gcol", c)
                    cp(g_col[0:n], ring[0][0:n, 1, 0:HEADS]).then_inc(S["gcol_taken"], 1)
                    now(dve, "grow_taken", c)
                    now(dve, "gcol_taken", c)
                    tt(d_col[0:n], g_row[0:n, :, n - 1], g_col[0:n], ALU.subtract).then_inc(S["dcol_diff"], 1)
                    now(dve, "d_col_ready", c)
                    now(dve, "kt", c)
                    tt(k_tok[0:n], ring[2][0:n], per_token(d_col[0:n]), ALU.mult).then_inc(S["kt_taken"], 1)
                    now(dve, "KK", c)
                    now(dve, "dec_kk_ready", c)
                    for h in range(HEADS):
                        last = stt(M[0:n, h, 0:n], ring[1][0:n, h, 0:n], beta[:, h:h + 1], dec_kk[0:n, h, 0:n],
                                   ALU.mult, ALU.mult)
                    last.then_inc(S["KK_taken"], 1)
                    now(dve, "QK", c)
                    now(dve, "dec_qk_ready", c)
                    tt(att[0:n, :, 0:n], ring[2][0:n, :, 0:n], dec_qk[0:n, :, 0:n], ALU.mult).then_inc(S["QK_taken"], 1)
                    now(dve, "F_ready", c)
                    before(dve, "kdtg", c)
                    for b in range(2):
                        k = I[:, R_GLA_K + b:R_GLA_K + b + 1, 0:n].to_broadcast([P, LEVELS + 1, n])
                        last = tt(KF[:, :, b, 0:n], k, F[:, 1:LEVELS + 2, b, 0:n], ALU.mult)
                    last.then_inc(S["KF_ready"], 1)
                    now(dve, "m0t", c)
                    tt(XT[0:n, :, 0:n], over_heads(ident[0:n, 0:n]), ring[1][0:n, :, 0:n],
                       ALU.subtract).then_inc(S["m0t_taken"], 1)
                    now(dve, "R", c)
                    now(dve, "vt_taken", c)
                    tt(rhs[0:n], v_tok[0:n], ring[2][0:n], ALU.subtract).then_inc(S["R_taken"], 1)

                    def take_pairs(h):
                        dve.wait_ge(pairs_ready, c * HEADS + h + 1)
                        tt(masked[0:n, h, 0:L, 0:n // 2], pair_bank[0:n, 0:L, 0:n // 2],
                           level_masks[0:n, 0:L, 0:n // 2], ALU.mult).then_inc(pairs_masked, 1)

                    for l in range(1, L):
                        s = 1 << l
                        dve.wait_ge(z_ready, c * (LEVELS - 1) + l)
                        level = level_masks[0:n, l:l + 1, 0:n // 2].to_broadcast([n, HEADS, n // 2])
                        tt(halves_packed(Z[0:n, :, 0:n // 2], s), halves_packed(z_bank[0:n, :, 0:n // 2], s),
                           halves_packed(level, s), ALU.mult).then_inc(z_taken, 1)
                        if l > 1:
                            dve.wait_ge(x_turned, c * TURNS + (l - 1))
                            cp(X[0:n, :, 0:n], x_bank[0:n, :, 0:n]).then_inc(x_taken, 1)
                        if l == 1:
                            now(dve, "diag", c)
                            tt(gla_att[0:n, :, 0:n], ring[0][0:n, :, 0:n], over_heads(ident[0:n, 0:n]),
                               ALU.mult).then_inc(S["diag_taken"], 1)
                        if l <= HEADS:
                            take_pairs(l - 1)
                        dve.wait_ge(xt_products, c * (LEVELS - 1) + l)
                        new = second_halves(XT[0:n, :, 0:n], s)
                        tt(new, new, halves_packed(xt_bank[0:n, :, 0:n // 2], s),
                           ALU.subtract).then_inc(xt_updated, 1)
                    dve.wait_ge(xt_updated, c * (LEVELS - 1) + (L - 1))
                    tt(XTb[0:n, :, 0:n], XT[0:n, :, 0:n], per_token(beta, n), ALU.mult).then_inc(S["XTb_ready"], 1)

                    def scale_outputs(name, which, z):
                        now(dve, name + "_squared", c)
                        before(dve, "out_ready" if which == 0 else "outg_ready", c)
                        tt(oz[which][:, :, 0:n], ring[which][:, :, 0:n], I[:, z:z + 4, 0:n],
                           ALU.mult).then_inc(S[name + "_scaled"], 1)
                    scale_outputs("Og", 1, R_GLA_Z)
                    scale_outputs("O", 0, R_GDN_Z)
                    now(dve, "dS", c)
                    for h in range(HEADS):
                        last = stt(state[:, h], state[:, h], e_row[:, h, n - 1:n], ring[1][:, h], ALU.mult, ALU.add)
                    last.then_inc(S["dS_taken"], 1)
                    now(dve, "dSg", c)
                    for h in range(HEADS):
                        rows = half_of(h)
                        last = stt(gla_state[rows, h], gla_state[rows, h], F[rows, 0, h // 2, n - 1:n],
                                   ring[2][rows, h], ALU.mult, ALU.add)
                    last.then_inc(S["dSg_taken"], 1)

                nc.vector.memset(eps[:, :], EPS).then_inc(eps_ready, 1)
                nc.vector.memset(state[:, :, :], 0.0)
                nc.vector.memset(gla_state[:, :, :], 0.0).then_inc(state_zero, 1)
                dve.wait_ge(state_zero, 1)
                dve.wait_ge(masks_landed, 16)
                preload(dve, DVE_)
                dve.sem_inc(pairs_masked, 1)
                per_chunk(dve, chunk)


class LateWeights:
    FIRST = 4
    BYTES = 4

    def __init__(self, nc, held, offset):
        wo_bytes = 12 * DM * self.BYTES
        self.split_tiles = offset
        self.wo_raw = nc.alloc_sbuf_tensor_at("wo_raw", [P, 12, DM], F32, offset=offset)
        self.w_out_first = nc.alloc_sbuf_tensor_at("w_out_first", [P, self.FIRST, DM], F32,
                                                   offset=offset + wo_bytes)
        self.o_raw = offset + wo_bytes + self.FIRST * DM * self.BYTES
        self.w_out_then = nc.alloc_sbuf_tensor_at("w_out_then", [P, 3, DM], F32, offset=self.o_raw)
        self.words = (self.o_raw - offset) // self.BYTES + 3 * DM
        self.wo_landed = held.add(nc.alloc_semaphore("wo_landed"))
        self.first_landed = held.add(nc.alloc_semaphore("w_out_first_landed"))
        self.then_landed = held.add(nc.alloc_semaphore("w_out_then_landed"))

    def load_in_chunk_phase(self, sp, d):
        sp.dma_start(self.wo_raw[:, :, :], d["wo"].rearrange("(k p) n -> p k n", p=P)).then_inc(self.wo_landed, 16)
        sp.dma_start(self.w_out_first[:, :, :], d["w_out"][0:self.FIRST * P, :].rearrange("(k p) n -> p k n", p=P)) \
            .then_inc(self.first_landed, 16)

    def load_in_branch_phase(self, sp, d):
        sp.dma_start(self.w_out_then[:, :, :], d["w_out"][self.FIRST * P:7 * P, :]
                     .rearrange("(k p) n -> p k n", p=P)).then_inc(self.then_landed, 16)


def branch_phase(nc, d, late):
    K = 12
    TT = 256
    TILES_B = NP_ // TT
    with ExitStack() as ctx, Held(nc) as held:
        def sb(name, shape, dt=F32):
            return ctx.enter_context(nc.sbuf_tensor(name, shape, dt))

        def sem(name):
            return held.add(nc.alloc_semaphore(name))

        wo_hi = sb("wo_hi", [P, K, DM], F32R)
        wo_lo = sb("wo_lo", [P, K, DM], F32R)
        o_raw = nc.alloc_sbuf_tensor_at("o_raw", [P, K, TT], F32, offset=late.o_raw)
        o_hi = nc.alloc_sbuf_tensor_at("o_hi", [P, 2, K, TT], F32R, offset=late.split_tiles)
        o_lo = nc.alloc_sbuf_tensor_at("o_lo", [P, 2, K, TT], F32R,
                                       offset=late.split_tiles + 2 * K * TT * late.BYTES)
        gate = sb("gate", [P, 2, 12, TT])
        prod = sb("prod", [P, 2, 3, TT])
        part = sb("part", [P, 2, TT])
        merged = sb("merged", [P, 2, TT])
        y = ctx.enter_context(nc.psum_tensor("y", [P, 2, 4, TT], F32))

        wo_high, wo_split = sem("wo_high"), sem("wo_split")
        o_landed, o_high, o_split = sem("o_landed"), sem("o_high"), sem("o_split")
        gate_landed = [sem("gate_landed0"), sem("gate_landed1")]
        gates_open = sem("gates_open")
        y_ready, y_gated = sem("y_ready"), sem("y_gated")
        part_ready, merged_ready = sem("part_ready"), sem("merged_ready")
        merged_stored = [sem("merged_stored0"), sem("merged_stored1")]
        outs, gates = d["branch_out"], d["gates"]

        def load_o(sp, t, n=TT):
            sp.dma_start(o_raw[:, :, 0:n], outs[:, :, bass.ds(t * TT, n)]).then_inc(o_landed, 16)

        def load_gates(sp, t, half, n=TT):
            sp.dma_start(gate[:, half, :, 0:n],
                         gates[:, half * 12:half * 12 + 12, bass.ds(t * TT, n)]).then_inc(gate_landed[half], 16)

        with nc.Block() as block:
            @block.sync
            def _(sp):
                load_o(sp, 0)
                load_gates(sp, 0, 0)
                load_gates(sp, 0, 1)

            @block.scalar
            def _(act):
                act.wait_ge(late.wo_landed, 16)
                for k in range(K):
                    nc.scalar.copy(wo_hi[:, k], late.wo_raw[:, k]).then_inc(wo_high, 1)

            @block.vector
            def _(dve):
                for k in range(K):
                    dve.wait_ge(wo_high, k + 1)
                    nc.vector.tensor_tensor(wo_lo[:, k], late.wo_raw[:, k], wo_hi[:, k].bitcast(F32),
                                            ALU.subtract).then_inc(wo_split, 1)
                dve.wait_ge(wo_split, K)

        with nc.Block() as block:
            def per_tile(eng, tile):
                tile(0, 0, 0, TT)
                tile(1, 0, 1, TT)
                with eng.Fori(1, TILES_B // 2) as i:
                    tile(i * 2, i, 0, TT)
                    tile(i * 2 + 1, i, 1, TT)
                tile(TILES_B, TILES_B // 2, 0, NS_)

            @block.sync
            def _(sp):
                def store(t, m, n=TT):
                    sp.wait_ge(merged_ready, t * KD + (m + 1))
                    sp.dma_start(d["merged"][:, m, bass.ds(t * TT, n)], merged[:, m % 2, 0:n]) \
                        .then_inc(merged_stored[m % 2], 16)

                def tile(t, n=TT, ahead=TT):
                    if ahead:
                        sp.wait_ge(o_split, t + 1)
                        load_o(sp, t + 1, ahead)
                    for m in range(KD):
                        store(t, m, n)
                        if ahead and m % 4 == 3:
                            load_gates(sp, t + 1, m // 4, ahead)
                tile(0)
                with sp.Fori(1, TILES_B - 1) as t:
                    tile(t)
                tile(TILES_B - 1, TT, NS_)
                sp.wait_ge(o_split, TILES_B + 1)
                late.load_in_branch_phase(sp, d)
                tile(TILES_B, NS_, 0)
                for q in range(2):
                    sp.wait_ge(merged_stored[q], 16 * 4 * (TILES_B + 1))

            @block.scalar
            def _(act):
                def tile(t, i, p, n):
                    act.wait_ge(o_landed, t * 16 + 16)
                    if not (isinstance(t, int) and t < 2):
                        act.wait_ge(y_ready, (t - 1) * KD)
                    nc.scalar.copy(o_hi[:, p, :, 0:n], o_raw[:, :, 0:n]).then_inc(o_high, 1)
                    for half in range(2):
                        act.wait_ge(gate_landed[half], t * 16 + 16)
                        g = gate[:, half, :, 0:n]
                        nc.scalar.activation(g, g, ACT.Sigmoid).then_inc(gates_open, 1)
                per_tile(act, tile)

            @block.tensor
            def _(pe):
                def tile(t, i, p, n):
                    pe.wait_ge(o_split, t + 1)
                    for m in range(KD):
                        if not (isinstance(t, int) and t == 0 and m < 2):
                            pe.wait_ge(y_gated, t * KD + (m - 1))
                        cols = slice(m * P, (m + 1) * P)
                        for b in range(3):
                            out = y[:, m % 2, b, 0:n]
                            for k in range(4 * b, 4 * b + 4):
                                nc.tensor.matmul(out, wo_hi[:, k, cols], o_hi[:, p, k, 0:n],
                                                 start=(k == 4 * b), stop=False)
                                nc.tensor.matmul(out, wo_hi[:, k, cols], o_lo[:, p, k, 0:n],
                                                 start=False, stop=False)
                                mm = nc.tensor.matmul(out, wo_lo[:, k, cols], o_hi[:, p, k, 0:n],
                                                      start=False, stop=(k == 4 * b + 3))
                        mm.then_inc(y_ready, 1)
                per_tile(pe, tile)

            @block.vector
            def _(dve):
                def low(t, p, n):
                    dve.wait_ge(o_high, t + 1)
                    nc.vector.tensor_tensor(o_lo[:, p, :, 0:n], o_raw[:, :, 0:n],
                                            o_hi[:, p, :, 0:n].bitcast(F32), ALU.subtract).then_inc(o_split, 1)

                def gated(t, m, n):
                    dve.wait_ge(y_ready, t * KD + (m + 1))
                    if m % 4 == 0:
                        dve.wait_ge(gates_open, t * 2 + (m // 4 + 1))
                    if not (isinstance(t, int) and t == 0 and m < 2):
                        dve.wait_ge(merged_ready, t * KD + (m - 1))
                    g = gate[:, m // 4, 3 * (m % 4):3 * (m % 4) + 3, 0:n]
                    nc.vector.tensor_tensor(prod[:, m % 2, :, 0:n], y[:, m % 2, 0:3, 0:n], g,
                                            ALU.mult).then_inc(y_gated, 1)

                def tile(t, i, p, n):
                    for m in range(KD):
                        gated(t, m, n)
                        if m == 3 and not (isinstance(t, int) and t == TILES_B):
                            if isinstance(t, int):
                                low(t + 1, 1 - p, TT)
                            else:
                                low(t + 1, 1 - p, TT)
                low(0, 0, TT)
                tile(0, 0, 0, TT)
                with dve.Fori(0, TILES_B // 2 - 1) as i:
                    tile(i * 2 + 1, i, 1, TT)
                    tile(i * 2 + 2, i, 0, TT)
                for m in range(KD):
                    gated(TILES_B - 1, m, TT)
                    if m == 3:
                        low(TILES_B, 0, NS_)
                for m in range(KD):
                    gated(TILES_B, m, NS_)

            @block.gpsimd
            def _(pool):
                def tile(t, i, p, n):
                    for m in range(KD):
                        q = m % 2
                        pool.wait_ge(y_gated, t * KD + (m + 1))
                        nc.gpsimd.tensor_tensor(part[:, q, 0:n], prod[:, q, 0, 0:n], prod[:, q, 1, 0:n],
                                                ALU.add).then_inc(part_ready, 1)
                        pool.wait_ge(part_ready, t * KD + (m + 1))
                        if not (isinstance(t, int) and t == 0 and m < 2):
                            pool.wait_ge(merged_stored[q], t * (4 * 16) + (m // 2) * 16)
                        nc.gpsimd.tensor_tensor(merged[:, q, 0:n], part[:, q, 0:n], prod[:, q, 2, 0:n],
                                                ALU.add).then_inc(merged_ready, 1)
                per_tile(pool, tile)


def output_phase(nc, d, late):
    with ExitStack() as ctx, Held(nc) as held:
        def sb(name, shape, dt=F32):
            return ctx.enter_context(nc.sbuf_tensor(name, shape, dt))

        def sem(name):
            return held.add(nc.alloc_semaphore(name))

        w_hi = sb("wout_hi", [P, KD, DM], F32R)
        w_lo = sb("wout_lo", [P, KD, DM], F32R)
        w_last = sb("wout_last", [P, DM])
        m_raw = sb("m_raw", [P, 2, KD, P])
        m_hi = sb("m_hi", [P, 2, KD, P], F32R)
        m_lo = sb("m_lo", [P, 2, KD, P], F32R)
        x_in = sb("x_again", [P, 2, DM])
        squares = sb("y_squares", [P, DM])
        normed = sb("normed", [P, 2, DM])
        result = sb("result", [P, 2, DM])
        gain = sb("post_gain", [P, DM])
        stat = sb("stat", [P, 2, 3])
        eps = sb("post_eps", [P, 1])
        y = ctx.enter_context(nc.psum_tensor("y_tok", [P, 2, DM], F32))

        w_last_landed = sem("w_last_landed")
        w_high, w_split = sem("wout_high"), sem("wout_split")
        gain_landed = sem("post_gain_landed")
        m_landed = [sem("m_landed0"), sem("m_landed1")]
        x_landed = [sem("x_again0"), sem("x_again1")]
        m_high, m_split = sem("m_high"), sem("m_split")
        y_ready = sem("y_tok_ready")
        sum_ready, log_ready, rstd_ready = sem("sum_ready"), sem("log_ready"), sem("post_rstd_ready")
        normed_ready, result_ready = sem("normed_ready"), sem("result_ready")
        stored = [sem("stored0"), sem("stored1")]
        eps_set = sem("post_eps_set")

        def w_raw(k):
            if k < late.FIRST:
                return late.w_out_first[:, k]
            return late.w_out_then[:, k - late.FIRST] if k < KD - 1 else w_last[:, :]

        with nc.Block() as block:
            def per_tile(eng, tile):
                tile(0, 0, 0, P)
                tile(1, 0, 1, P)
                with eng.Fori(1, CHUNKS // 2) as i:
                    tile(i * 2, i, 0, P)
                    tile(i * 2 + 1, i, 1, P)
                tile(CHUNKS, CHUNKS // 2, 0, NS_)

            @block.sync
            def _(sp):
                def load(t, p, n=P):
                    x = d["x_prompt"][bass.ds(t * P, P), :] if n == P else d["x_sample"]
                    sp.dma_start(m_raw[:, p, :, 0:n], d["merged"][:, :, bass.ds(t * P, n)]).then_inc(m_landed[p], 16)
                    sp.dma_start(x_in[0:n, p], x).then_inc(x_landed[p], 16)

                def store(t, p, n=P):
                    y_out = d["y_prompt"][bass.ds(t * P, P), :] if n == P else d["y_sample"]
                    sp.wait_ge(result_ready, t + 1)
                    sp.dma_start(y_out, result[0:n, p]).then_inc(stored[p], 16)

                load(0, 0)
                sp.dma_start(w_last[:, :], d["w_out"][(KD - 1) * P:KD * P, :]).then_inc(w_last_landed, 16)
                sp.dma_start(gain[:, :], d["norm_post"].to_broadcast([P, DM])).then_inc(gain_landed, 16)
                load(1, 1)
                with sp.Fori(0, CHUNKS // 2 - 1) as i:
                    for p in range(2):
                        store(i * 2 + p, p)
                        load(i * 2 + (p + 2), p)
                store(CHUNKS - 2, 0)
                load(CHUNKS, 0, NS_)
                store(CHUNKS - 1, 1)
                store(CHUNKS, 0, NS_)
                sp.wait_ge(stored[0], 16 * (CHUNKS // 2 + 1))
                sp.wait_ge(stored[1], 16 * (CHUNKS // 2))

            @block.scalar
            def _(act):
                def high(t, i, p, n):
                    act.wait_ge(m_landed[p], i * 16 + 16)
                    if not (isinstance(t, int) and t < 2):
                        act.wait_ge(y_ready, t - 1)
                    nc.scalar.copy(m_hi[:, p, :, 0:n], m_raw[:, p, :, 0:n]).then_inc(m_high, 1)

                def statistics(t, p, n):
                    act.wait_ge(y_ready, t + 1)
                    if not (isinstance(t, int) and t < 2):
                        act.wait_ge(normed_ready, t - 1)
                    nc.scalar.activation(squares[0:n], y[0:n, p], ACT.Square,
                                         accum_out=stat[0:n, p, 0:1]).then_inc(sum_ready, 1)
                    act.wait_ge(sum_ready, t + 1)
                    nc.scalar.activation(stat[0:n, p, 1:2], stat[0:n, p, 0:1], ACT.Ln, bias=eps[0:n, 0:1],
                                         scale=1.0 / DM).then_inc(log_ready, 1)
                    act.wait_ge(log_ready, t + 1)
                    nc.scalar.activation(stat[0:n, p, 2:3], stat[0:n, p, 1:2], ACT.Exp,
                                         scale=-0.5).then_inc(rstd_ready, 1)

                use_log_exp_tables(nc)
                act.wait_ge(eps_set, 1)
                high(0, 0, 0, P)
                for k in range(KD):
                    if k == 0:
                        act.wait_ge(late.first_landed, 16)
                    if k == late.FIRST:
                        act.wait_ge(late.then_landed, 16)
                    if k == KD - 1:
                        act.wait_ge(w_last_landed, 16)
                    nc.scalar.copy(w_hi[:, k], w_raw(k)).then_inc(w_high, 1)
                high(1, 0, 1, P)
                for p in range(2):
                    statistics(p, p, P)
                    high(p + 2, 1, p, P)
                with act.Fori(1, CHUNKS // 2 - 1) as i:
                    for p in range(2):
                        statistics(i * 2 + p, p, P)
                        high(i * 2 + (p + 2), i + 1, p, P)
                statistics(CHUNKS - 2, 0, P)
                high(CHUNKS, CHUNKS // 2, 0, NS_)
                statistics(CHUNKS - 1, 1, P)
                statistics(CHUNKS, 0, NS_)

            @block.tensor
            def _(pe):
                def tile(t, i, p, n):
                    pe.wait_ge(m_split, t + 1)
                    if not (isinstance(t, int) and t < 2):
                        pe.wait_ge(normed_ready, t - 1)
                    for half in range(2):
                        cols = slice(half * 512, half * 512 + 512)
                        out = y[0:n, p, cols]
                        for k in range(KD):
                            if isinstance(t, int) and t == 0 and half == 0:
                                pe.wait_ge(w_split, k + 1)
                            nc.tensor.matmul(out, m_hi[:, p, k, 0:n], w_hi[:, k, cols], start=(k == 0), stop=False)
                            nc.tensor.matmul(out, m_hi[:, p, k, 0:n], w_lo[:, k, cols], start=False, stop=False)
                            mm = nc.tensor.matmul(out, m_lo[:, p, k, 0:n], w_hi[:, k, cols], start=False,
                                                  stop=(k == KD - 1))
                    mm.then_inc(y_ready, 1)
                tile(0, 0, 0, P)
                tile(1, 0, 1, P)
                tile(2, 1, 0, P)
                tile(3, 1, 1, P)
                with pe.Fori(1, CHUNKS // 4) as i:
                    for u in range(4):
                        tile(i * 4 + u, None, u % 2, P)
                tile(CHUNKS, None, 0, NS_)

            @block.vector
            def _(dve):
                def low(t, p, n):
                    dve.wait_ge(m_high, t + 1)
                    nc.vector.tensor_tensor(m_lo[:, p, :, 0:n], m_raw[:, p, :, 0:n],
                                            m_hi[:, p, :, 0:n].bitcast(F32), ALU.subtract).then_inc(m_split, 1)

                def norm(t, p, n):
                    dve.wait_ge(rstd_ready, t + 1)
                    if not (isinstance(t, int) and t < 2):
                        dve.wait_ge(result_ready, t - 1)
                    nc.vector.scalar_tensor_tensor(normed[0:n, p], y[0:n, p], stat[0:n, p, 2:3], gain[0:n],
                                                   ALU.mult, ALU.mult).then_inc(normed_ready, 1)

                nc.vector.memset(eps[:, :], EPS).then_inc(eps_set, 1)
                low(0, 0, P)
                for k in range(KD):
                    dve.wait_ge(w_high, k + 1)
                    nc.vector.tensor_tensor(w_lo[:, k], w_raw(k), w_hi[:, k].bitcast(F32),
                                            ALU.subtract).then_inc(w_split, 1)
                low(1, 1, P)
                dve.wait_ge(gain_landed, 16)
                norm(0, 0, P)
                low(2, 0, P)
                norm(1, 1, P)
                low(3, 1, P)
                with dve.Fori(1, CHUNKS // 2 - 1) as i:
                    for p in range(2):
                        norm(i * 2 + p, p, P)
                        low(i * 2 + (p + 2), p, P)
                norm(CHUNKS - 2, 0, P)
                low(CHUNKS, 0, NS_)
                norm(CHUNKS - 1, 1, P)
                norm(CHUNKS, 0, NS_)

            @block.gpsimd
            def _(pool):
                def tile(t, i, p, n):
                    pool.wait_ge(x_landed[p], i * 16 + 16)
                    if not (isinstance(t, int) and t < 2):
                        pool.wait_ge(stored[p], i * 16)
                    pool.wait_ge(normed_ready, t + 1)
                    nc.gpsimd.tensor_tensor(result[0:n, p], normed[0:n, p], x_in[0:n, p],
                                            ALU.add).then_inc(result_ready, 1)
                per_tile(pool, tile)


def program(nc, d):
    with Held(nc) as held:
        h_offset = (nc.sbuf_base + 31) // 32 * 32
        late = LateWeights(nc, held, h_offset)
        with ExitStack() as ctx:
            h_all = nc.alloc_sbuf_tensor_at("h_all", [P, KD, NT], F32, offset=h_offset)
            hi = ctx.enter_context(nc.sbuf_tensor("h_hi", [P, KD, NT], F32R))
            consts = ctx.enter_context(nc.sbuf_tensor("constants", [P, C_END], F32))
            with ExitStack() as early:
                lo = early.enter_context(nc.sbuf_tensor("h_lo", [P, KD, NT], F32R))
                norm_phase(nc, d, hi, lo, consts)
                project_phase(nc, d, hi, lo, h_all, consts)
            chunk_phase(nc, d, consts, h_all, late)
        with nc.sbuf_tensor("late_bytes", [P, late.words], F32):
            branch_phase(nc, d, late)
            output_phase(nc, d, late)


def shape_constants():
    import numpy as np
    c = np.zeros((P, C_END), np.float32)
    m = np.zeros((P, M_END), np.float32)
    i = np.arange(P)
    row, col = i[:, None], i[None, :]
    c[:, C_IDENT:C_IDENT + P] = np.eye(P)
    c[:, C_ONES:C_ONES + P] = 1
    c[:, C_CNT:C_CNT + 16] = 1.0 / (1 + np.arange(16))
    m[:, M_UPPER:M_UPPER + P] = row <= col
    m[:, M_NEG:M_NEG + P] = np.where(row <= col, 0, -1e30)
    m[:, M_POS:M_POS + P] = np.where(row > col, 0, 1e30)
    for n in range(LEVELS):
        s = 1 << n
        low = (row // (2 * s) == col // (2 * s)) & (row // s % 2 == 1) & (col // s % 2 == 0)
        if n == 0:
            m[:, M_LOW:M_LOW + P] = low
        m[:, M_PAIRS + n * HALF:M_PAIRS + (n + 1) * HALF] = low.T[:, i // s % 2 == 1]
    return c, m


def laid_out(x):
    import numpy as np
    x = {k: np.asarray(v) for k, v in x.items()}
    w = x["w_in"][0]
    blocks = np.zeros((F_END, P, DM), np.float32)

    def put(f, cols):
        part = w[:, cols:cols + P]
        blocks[f] = part.reshape(KD, P, P).transpose(1, 0, 2).reshape(P, DM)
    special = np.zeros((DM, P), np.float32)
    special[:, AT_F:AT_F + 16] = w[:, 1024:1040]
    special[:, AT_G:AT_G + 4] = w[:, 4112:4116]
    special[:, AT_B:AT_B + 4] = w[:, 4116:4120]
    blocks[F_SPECIAL] = special.reshape(KD, P, P).transpose(1, 0, 2).reshape(P, DM)
    for n in range(8):
        put(F_COPY + n, n * P)
    for n in range(4):
        put(F_SILU + n, 1040 + n * P)
        put(F_SILU + 4 + n, 4120 + n * P)
        put(F_POOL + 2 * n, 1552 + n * P)
        put(F_POOL + 2 * n + 1, 2064 + n * P)
    for n in range(12):
        put(F_CONV + n, 2576 + n * P)
    for n in range(24):
        put(F_GATE + n, 4632 + (n % 3) * DM + (n // 3) * P)

    def columns(v, n):
        return np.ascontiguousarray(v.reshape(n, P).T)
    return {
        "x_prompt": x["x_prompt"][0], "x_sample": x["x_sample"][0], "norm_pre": x["norm_pre"],
        "consts": shape_constants()[0], "masks": shape_constants()[1], "w_in": blocks, "gla_bf": columns(x["gla_bf"], 2),
        "pool_scale": columns(x["pool_scale"], 4), "gla_norm": columns(x["gla_norm"], 4),
        "gdn_norm": columns(x["gdn_norm"], 4),
        "gdn_conv": np.ascontiguousarray(x["gdn_conv"][0].reshape(4, 12, P).transpose(2, 1, 0)).reshape(P, 48),
        "scalars": np.tile(np.array([[EPS, np.log(P ** -0.5)]], np.float32), (P, 1)),
        "gdn_a_log": x["gdn_a_log"].reshape(4, 1), "gdn_dt_bias": x["gdn_dt_bias"].reshape(4, 1),
        "gla_wf2": x["gla_wf2"][0], "pool_w": np.ascontiguousarray(x["pool_w"][0].transpose(1, 0, 2)),
        "conv_cache": np.ascontiguousarray(x["cache_gdn_conv"][0, 0].reshape(3, 12, P).transpose(2, 1, 0)),
        "pool_cache": np.ascontiguousarray(x["cache_pool"][0, 0].reshape(15, 4, P).transpose(2, 1, 0)),
        "state_gla": x["state_gla"][0, 0], "state_gdn": x["state_gdn"][0, 0],
        "wo": np.concatenate([x["gla_wo"][0], x["pool_wo"][0], x["gdn_wo"][0]]),
        "w_out": x["w_out"][0], "norm_post": x["norm_post"],
    }


_OUTS = {
    "y_prompt": (NP_, DM), "y_sample": (NS_, DM),
    "new_gla_prompt": (HEADS, 64, P), "new_gdn_prompt": (HEADS, P, P),
    "new_conv_prompt": (P, 12, CONV_HALO), "new_pool_prompt": (P, 4, POOL_HALO),
    "new_gla_sample": (HEADS, 64, P), "new_gdn_sample": (HEADS, P, P),
    "new_conv_sample": (P, 12, CONV_HALO), "new_pool_sample": (P, 4, POOL_HALO),
}
_SCRATCH = {"feat": (P, R_END, NT), "gates": (P, 24, NT), "branch_out": (P, 12, NT), "merged": (P, KD, NT)}


def kernel(**inputs):
    import numpy as np
    import concourse.bacc as bacc
    from concourse.bass_utils import run_bass_kernel_spmd

    nc = bacc.Bacc("TRN2", target_bir_lowering=False, num_devices=1)
    arrays, d = {}, {}
    for name, a in laid_out(inputs).items():
        a = np.ascontiguousarray(a)
        arrays[f"in_{name}"] = a
        d[name] = nc.dram_tensor(f"in_{name}", a.shape, F32, kind="ExternalInput").ap()
    for name, shape in _OUTS.items():
        d[name] = nc.dram_tensor(f"out_{name}", shape, F32, kind="ExternalOutput").ap()
    for name, shape in _SCRATCH.items():
        d[name] = nc.dram_tensor(f"scratch_{name}", shape, F32, kind="Internal").ap()
    program(nc, d)
    r = run_bass_kernel_spmd(nc, [arrays], core_ids=[0]).results[0]
    got = {name: r[f"out_{name}"] for name in _OUTS}

    def cache(a):
        return np.ascontiguousarray(a.transpose(2, 1, 0)).reshape(1, 1, a.shape[2], -1)
    out = [got["y_prompt"][None], got["y_sample"][None]]
    for group in ("prompt", "sample"):
        out += [got[f"new_gla_{group}"][None, None], got[f"new_gdn_{group}"][None, None],
                cache(got[f"new_conv_{group}"]), cache(got[f"new_pool_{group}"])]
    return tuple(out)
```

```python
from contextlib import ExitStack

import concourse.bass as bass
from concourse import mybir

F32 = mybir.dt.float32
F32R = mybir.dt.float32r
ALU = mybir.AluOpType
ACT = mybir.ActivationFunctionType

P = 128
DM = 1024
KD = DM // P
NP_ = 2048
NS_ = 64
NT = NP_ + NS_
TILES = 6
TW = NT // TILES
HEADS = 4
CHUNKS = NP_ // P
EPS = 1e-6
LEVELS = 7
ROW = 2144
POOL_HALO = 15
CONV_HALO = 3

C_IDENT = 0
C_ONES = C_IDENT + P
C_CNT = C_ONES + P
C_END = C_CNT + 16

M_UPPER = 0
M_NEG = M_UPPER + P
M_POS = M_NEG + P
M_LOW = M_POS + P
M_PAIRS = M_LOW + P
HALF = P // 2
M_END = M_PAIRS + LEVELS * HALF

F_SPECIAL = 0
F_COPY = 1
F_SILU = F_COPY + 8
F_POOL = F_SILU + 8
F_CONV = F_POOL + 8
F_GATE = F_CONV + 12
F_END = F_GATE + 24

LATE_GATES = CHUNKS
HALF_TOKENS = NT // 2
EARLY_GATES = 24 - LATE_GATES
F_LATE = F_GATE + EARLY_GATES

A_SPECIAL = 0
A_COPY = 1
A_POOL = A_COPY + 8
A_CONV = A_POOL + 4
A_GATE = A_CONV + 12

R_GLA_Q, R_GLA_K, R_GLA_V = 0, 2, 4
R_LOGF = 8
R_GB = 10
R_GLA_Z = 11
R_GDN_Z = 15
R_GDN_Q, R_GDN_K, R_GDN_V = 19, 23, 27
R_END = 31

S_NEGA, S_DT, S_BF, S_PSCALE, S_ZNORM, S_CONV, S_EPS, S_QS = 0, 1, 2, 4, 8, 16, 64, 65
S_END = 66

AT_F, AT_G, AT_B = 0, 32, 64


def at_least(eng, sem, value):
    if isinstance(value, int) and value <= 0:
        return
    eng.wait_ge(sem, value)


class Held:

    def __init__(self, nc):
        self.nc, self.semaphores = nc, []

    def add(self, semaphore):
        self.semaphores.append(semaphore)
        return semaphore

    def __enter__(self):
        return self

    def __exit__(self, *error):
        self.nc.clear_and_free_semaphores(self.semaphores)
        self.nc.all_engine_barrier()


def use_log_exp_tables(nc):
    nc.scalar.preload_act_table_set("natural_log_exp_and_others")


def second_halves(x, s):
    return x.rearrange("p h (m t) -> p h m t", t=2 * s)[:, :, :, s:2 * s]


def halves_packed(x, s):
    return x.rearrange("p h (m t) -> p h m t", t=s)


def column(tensor, n):
    return tensor[:, n:n + 1] if isinstance(n, int) else tensor[:, bass.ds(n, 1)]


class BlockWeights:

    def __init__(self, nc, context, held):
        def sb(name, shape, dt=F32):
            return context.enter_context(nc.sbuf_tensor(name, shape, dt))

        self.raw = sb("w_raw", [P, 2, DM])
        self.hi = sb("w_hi", [P, 2, KD, P], F32R)
        self.lo = sb("w_lo", [P, 2, KD, P], F32R)
        self.zero = sb("zero", [P, 1])
        self.zero_set = held.add(nc.alloc_semaphore("zero_set"))
        self.landed = [held.add(nc.alloc_semaphore(f"w_landed{p}")) for p in range(2)]
        self.high_ready = held.add(nc.alloc_semaphore("w_high"))
        self.split_ready = held.add(nc.alloc_semaphore("w_split"))

    def load(self, sp, d, f, p):
        sp.dma_start(self.raw[:, p], d["w_in"][bass.ds(f, 1)].rearrange("a p n -> p (a n)")) \
            .then_inc(self.landed[p], 16)

    def split(self, nc, pool, i, f, p):
        pool.wait_ge(self.landed[p], i * 16 + 16)
        raw = self.raw[:, p].rearrange("p (k m) -> p k m", k=KD)
        zeros = self.zero[:, 0:1].rearrange("p (a b) -> p a b", b=1).to_broadcast([P, KD, P])
        nc.gpsimd.tensor_tensor(self.hi[:, p], raw, zeros, ALU.add).then_inc(self.high_ready, 1)
        pool.wait_ge(self.high_ready, f + 1)
        nc.gpsimd.tensor_tensor(self.lo[:, p], raw, self.hi[:, p].bitcast(F32),
                                ALU.subtract).then_inc(self.split_ready, 1)


def norm_phase(nc, d, hi, lo, consts, weights):
    tiles = CHUNKS + 1
    with ExitStack() as ctx, Held(nc) as held:
        def sb(name, shape, dt=F32):
            return ctx.enter_context(nc.sbuf_tensor(name, shape, dt))

        def sem(name):
            return held.add(nc.alloc_semaphore(name))

        IN = 4
        x_in = sb("x_in", [P, IN, DM])
        x_scaled = sb("x_scaled", [P, 2, DM])
        squares = sb("squares", [P, DM])
        gain = sb("gain", [P, DM])
        sums = sb("sums", [P, 2])
        logs = sb("logs", [P, 2])
        rstd = sb("rstd", [P, 2])
        eps = sb("eps", [P, 1])
        turned = ctx.enter_context(nc.psum_tensor("turned", [P, 2, KD, P], F32))
        ident = consts[:, C_IDENT:C_IDENT + P]

        gain_landed = sem("gain_landed")
        x_landed = [sem(f"x_landed{b}") for b in range(IN)]
        eps_set = sem("eps_set")
        sums_ready = sem("sums_ready")
        logs_ready = sem("logs_ready")
        rstd_ready = sem("rstd_ready")
        scaled_ready = sem("scaled_ready")
        turned_ready = sem("turned_ready")
        hi_ready = sem("hi_ready")
        lo_ready = sem("lo_ready")

        def width(t):
            return P if t < CHUNKS else NS_

        def pieces(t):
            start, end, middle = t * P, t * P + width(t), HALF_TOKENS
            parts = []
            if start < middle:
                parts.append((0, slice(start, min(end, middle)), slice(0, min(end, middle) - start)))
            if end > middle:
                first = max(start, middle)
                parts.append((1, slice(first - middle, end - middle), slice(first - start, end - start)))
            return parts

        with nc.Block() as block:
            @block.sync
            def _(sp):
                def load(t):
                    x = d["x_prompt"][t * P:(t + 1) * P, :] if t < CHUNKS else d["x_sample"]
                    sp.dma_start(x_in[0:width(t), t % IN], x).then_inc(x_landed[t % IN], 16)

                load(0)
                sp.dma_start(consts[:, :], d["consts"]).then_inc(gain_landed, 16)
                sp.dma_start(gain[:, :], d["norm_pre"].to_broadcast([P, DM])).then_inc(gain_landed, 16)
                for t in range(1, IN):
                    load(t)
                for t in range(IN, tiles):
                    sp.wait_ge(scaled_ready, t - IN + 1)
                    load(t)
                    if t in (IN, IN + 1):
                        weights.load(sp, d, t - IN, t - IN)

            @block.scalar
            def _(act):
                def statistics(t):
                    u = t % 2
                    act.wait_ge(x_landed[t % IN], (t // IN + 1) * 16)
                    nc.scalar.activation(squares[0:width(t), :], x_in[0:width(t), t % IN], ACT.Square,
                                         accum_out=sums[0:width(t), u:u + 1]).then_inc(sums_ready, 1)
                    act.wait_ge(sums_ready, t + 1)
                    nc.scalar.activation(logs[:, u:u + 1], sums[:, u:u + 1], ACT.Ln, bias=eps[:, 0:1],
                                         scale=1.0 / DM).then_inc(logs_ready, 1)
                    act.wait_ge(logs_ready, t + 1)
                    nc.scalar.activation(rstd[:, u:u + 1], logs[:, u:u + 1], ACT.Exp,
                                         scale=-0.5).then_inc(rstd_ready, 1)

                def high(t):
                    act.wait_ge(turned_ready, t + 1)
                    for half, cols, own in pieces(t):
                        last = nc.scalar.copy(hi[half][:, :, cols], turned[:, t % 2, :, own])
                    last.then_inc(hi_ready, 1)

                use_log_exp_tables(nc)
                act.wait_ge(eps_set, 1)
                statistics(0)
                for t in range(tiles - 1):
                    statistics(t + 1)
                    high(t)
                high(tiles - 1)

            @block.vector
            def _(dve):
                nc.vector.memset(eps[:, :], EPS).then_inc(eps_set, 1)

                def scale(t):
                    n = width(t)
                    dve.wait_ge(rstd_ready, t + 1)
                    if t >= 2:
                        dve.wait_ge(turned_ready, t - 1)
                    nc.vector.scalar_tensor_tensor(x_scaled[0:n, t % 2], x_in[0:n, t % IN],
                                                   rstd[0:n, t % 2:t % 2 + 1], gain[0:n, :],
                                                   ALU.mult, ALU.mult).then_inc(scaled_ready, 1)

                def low(t):
                    dve.wait_ge(hi_ready, t + 1)
                    for half, cols, own in pieces(t):
                        last = nc.vector.tensor_tensor(lo[half][:, :, cols], turned[:, t % 2, :, own],
                                                       hi[half][:, :, cols].bitcast(F32), ALU.subtract)
                    last.then_inc(lo_ready, 1)

                dve.wait_ge(gain_landed, 32)
                scale(0)
                for t in range(tiles - 1):
                    scale(t + 1)
                    low(t)
                low(tiles - 1)

            @block.tensor
            def _(pe):
                pe.wait_ge(gain_landed, 32)
                for t in range(tiles):
                    n = width(t)
                    pe.wait_ge(scaled_ready, t + 1)
                    if t >= 2:
                        pe.wait_ge(lo_ready, t - 1)
                    for k in range(KD):
                        mm = nc.tensor.transpose(turned[:, t % 2, k, 0:n], x_scaled[0:n, t % 2, k * P:(k + 1) * P],
                                                 ident[0:n, 0:n])
                    mm.then_inc(turned_ready, 1)

            @block.gpsimd
            def _(pool):
                nc.gpsimd.memset(weights.zero[:, :], 0.0).then_inc(weights.zero_set, 1)
                pool.wait_ge(weights.zero_set, 1)
                for f in range(2):
                    weights.split(nc, pool, 0, f, f)


def project_phase(nc, d, hi, lo, consts, weights):
    with ExitStack() as ctx, Held(nc) as held:
        def sb(name, shape, dt=F32):
            return ctx.enter_context(nc.sbuf_tensor(name, shape, dt))

        def sem(name):
            return held.add(nc.alloc_semaphore(name))

        w_hi, w_lo = weights.hi, weights.lo
        X = sb("row_x", [P, 2, ROW])
        Y = sb("row_y", [P, 2, ROW])
        T = sb("row_t", [P, ROW])
        sig = sb("sig", [P, 2, TW])
        small = sb("small", [P, S_END])
        wf2 = sb("wf2", [16, 256])
        pool_w = sb("pool_w", [P, 4, P])
        conv_cache = sb("conv_cache", [P, 12, CONV_HALO])
        conv_out = sb("conv_out", [P, 2, 12, CONV_HALO])
        pool_out = sb("pool_out", [P, 2, 4, POOL_HALO])
        dense = ctx.enter_context(nc.psum_tensor("dense", [P, 2, 512], F32))
        side = ctx.enter_context(nc.psum_tensor("side", [P, 2, 512], F32))
        ones = consts[:, C_ONES:C_ONES + P]

        params_landed = sem("params_landed")
        w_split = weights.split_ready
        dense_ready = sem("dense_ready")
        act_free = sem("act_free")
        dve_free = sem("dve_free")
        side_ready = sem("side_ready")
        side_free = sem("side_free")
        norm_free = sem("norm_free")
        act_done = sem("act_done")
        dve_done = sem("dve_done")
        special_ready = sem("special_ready")
        special_stored = sem("special_stored")
        logf_ready = sem("logf_ready")
        copy_stored = [sem("copy_stored0"), sem("copy_stored1")]
        sig_ready = sem("sig_ready")
        silu_stored = [sem("silu_stored0"), sem("silu_stored1")]
        pool_step = sem("pool_step")
        pool_d_ready = sem("pool_d_ready")
        pool_stored = sem("pool_stored")
        halo_set = sem("halo_set")
        conv_step = sem("conv_step")
        special_step = sem("special_step")
        conv_ready = sem("conv_ready")
        conv_sig_ready = sem("conv_sig_ready")
        conv_silu_ready = sem("conv_silu_ready")
        squares_ready = sem("squares_ready")
        norm_ready = sem("norm_ready")
        qkv_ready = sem("qkv_ready")
        qkv_stored = [sem("qkv_stored0"), sem("qkv_stored1")]
        caches_stored = sem("caches_stored")
        h_saved = sem("h_saved")
        gate_stored = [sem("gate_stored0"), sem("gate_stored1")]

        feat, gates, outs = d["feat"], d["gates"], d["branch_out"]
        PARAMS = 12 * 16

        with nc.Block() as block:
            @block.gpsimd
            def _(pool):
                with pool.Fori(1, F_LATE // 2) as i:
                    for p in range(2):
                        pool.wait_ge(dense_ready, i * (2 * TILES) + (p - 1) * TILES)
                        weights.split(nc, pool, i, i * 2 + p, p)
                pool.wait_ge(dense_ready, (F_LATE - 2) * TILES)
                weights.split(nc, pool, F_LATE // 2, F_LATE - 1, 0)

            @block.tensor
            def _(pe):
                def project(f, p, own, before):
                    pe.wait_ge(w_split, f + 1)
                    for t in range(TILES):
                        if t >= 2:
                            pe.wait_ge(own[0], own[1] * TILES + (t - 1))
                        elif before is not None:
                            pe.wait_ge(before[0], before[1] * TILES + (TILES + t - 1))
                        h_hi, h_lo = hi[t // 3], lo[t // 3]
                        for k in range(KD):
                            cols = slice(t % 3 * TW, (t % 3 + 1) * TW)
                            out = dense[:, t % 2, 0:TW]
                            nc.tensor.matmul(out, w_hi[:, p, k], h_hi[:, k, cols], start=(k == 0), stop=False)
                            nc.tensor.matmul(out, w_hi[:, p, k], h_lo[:, k, cols], start=False, stop=False)
                            mm = nc.tensor.matmul(out, w_lo[:, p, k], h_hi[:, k, cols], start=False,
                                                  stop=(k == KD - 1))
                        mm.then_inc(dense_ready, 1)

                def by_act(n):
                    return act_free, n

                def by_dve(n):
                    return dve_free, n

                def forget_gates(b):
                    for t in range(TILES):
                        n = b * TILES + t
                        at_least(pe, side_free, n - 1)
                        nc.tensor.matmul(side[:, n % 2, 0:TW], wf2[:, b * P:(b + 1) * P],
                                         X[0:16, 0, t * TW:(t + 1) * TW], start=True, stop=True) \
                            .then_inc(side_ready, 1)

                project(F_SPECIAL, 0, by_act(A_SPECIAL), None)
                project(F_COPY, 1, by_act(A_COPY), by_act(A_SPECIAL))
                pe.wait_ge(special_ready, 1)
                forget_gates(0)
                project(F_COPY + 1, 0, by_act(A_COPY + 1), by_act(A_COPY))
                project(F_COPY + 2, 1, by_act(A_COPY + 2), by_act(A_COPY + 1))
                forget_gates(1)
                project(F_COPY + 3, 0, by_act(A_COPY + 3), by_act(A_COPY + 2))
                with pe.Fori(2, 4) as i:
                    for u in range(2):
                        project(i * 2 + (F_COPY + u), 1 - u, by_act(i * 2 + (A_COPY + u)),
                                by_act(i * 2 + (A_COPY + u - 1)))
                project(F_SILU, 1, by_dve(0), by_act(A_COPY + 7))
                project(F_SILU + 1, 0, by_dve(1), by_dve(0))
                with pe.Fori(1, 4) as i:
                    for u in range(2):
                        project(i * 2 + (F_SILU + u), 1 - u, by_dve(i * 2 + u), by_dve(i * 2 + (u - 1)))

                def pool_map(g):
                    pe.wait_ge(pool_d_ready, g + 1)
                    for t in range(TILES):
                        n = (2 + g) * TILES + t
                        pe.wait_ge(side_free, n - 1)
                        nc.tensor.matmul(side[:, n % 2, 0:TW], pool_w[:, g], X[:, 1, t * TW:(t + 1) * TW],
                                         start=True, stop=True).then_inc(side_ready, 1)

                for g in range(4):
                    project(F_POOL + 2 * g, 1, by_act(A_POOL + g), by_dve(7 + g))
                    if g >= 1:
                        pool_map(g - 1)
                    project(F_POOL + 2 * g + 1, 0, by_dve(8 + g), by_act(A_POOL + g))
                pool_map(3)

                def square_sums(j):
                    pe.wait_ge(squares_ready, j + 1)
                    for t in range(TILES):
                        if isinstance(j, int) and j == 0 and t < 2:
                            pe.wait_ge(side_free, 6 * TILES + t - 1)
                        else:
                            pe.wait_ge(norm_free, j * TILES + (t - 1))
                        nc.tensor.matmul(side[:, t % 2, 0:TW], ones, T[:, t * TW:(t + 1) * TW],
                                         start=True, stop=True).then_inc(side_ready, 1)

                def conv_project(j, p):
                    project(j + F_CONV, p, by_act(j + A_CONV), by_act(j + (A_CONV - 1)))

                project(F_CONV, 1, by_act(A_CONV), by_dve(11))
                conv_project(1, 0)
                square_sums(0)
                with pe.Fori(0, 3) as i:
                    conv_project(i * 2 + 2, 1)
                    square_sums(i * 2 + 1)
                    conv_project(i * 2 + 3, 0)
                    square_sums(i * 2 + 2)
                conv_project(8, 1)
                square_sums(7)
                conv_project(9, 0)
                with pe.Fori(0, 1 + EARLY_GATES // 2) as i:
                    conv_project(i * 2 + 10, 1)
                    conv_project(i * 2 + 11, 0)

            @block.scalar
            def _(act):
                def tiles(f, write):
                    for t in range(TILES):
                        act.wait_ge(dense_ready, f * TILES + (t + 1))
                        write(t, dense[:, t % 2, 0:TW])

                use_log_exp_tables(nc)
                act.wait_ge(params_landed, PARAMS)
                nc.scalar.activation(small[AT_G:AT_G + 4, S_NEGA:S_NEGA + 1],
                                     small[AT_G:AT_G + 4, S_NEGA:S_NEGA + 1], ACT.Exp).then_inc(act_done, 1)

                def special(t, tile):
                    mm = nc.scalar.copy(X[:, 0, t * TW:(t + 1) * TW], tile)
                    mm.then_inc(act_free, 1)
                tiles(F_SPECIAL, special)
                act.wait_ge(act_free, TILES)
                nc.scalar.activation(X[AT_B:AT_B + 4, 0, 0:NT], X[AT_B:AT_B + 4, 0, 0:NT], ACT.Exp,
                                     scale=-1.0).then_inc(special_ready, 1)

                def softplus_part(n):
                    act.wait_ge(dve_done, n + 1)
                    v = T[AT_G:AT_G + 4, 0:NT] if n == 0 else X[:, 1, 0:NT]
                    nc.scalar.activation(v, v, ACT.Exp, scale=-1.0).then_inc(act_done, 1)
                    act.wait_ge(act_done, 2 * n + 2)
                    nc.scalar.activation(v, v, ACT.Ln, bias=1.0).then_inc(act_done, 1)

                def copy_block(i, f, p, scale=1.0):
                    def write(t, tile):
                        out = Y[:, p, t * TW:(t + 1) * TW]
                        nc.scalar.mul(out, tile, scale).then_inc(act_free, 1)
                    tiles(f, write)

                softplus_part(0)
                copy_block(0, F_COPY, 1, 0.125)
                copy_block(0, F_COPY + 1, 0, 0.125)
                softplus_part(1)
                act.wait_ge(copy_stored[1], 16)
                copy_block(1, F_COPY + 2, 1)
                act.wait_ge(copy_stored[0], 16)
                copy_block(1, F_COPY + 3, 0)
                softplus_part(2)
                with act.Fori(2, 4) as i:
                    for p in (1, 0):
                        act.wait_ge(copy_stored[p], i * 16)
                        copy_block(i, i * 2 + (F_COPY + 1 - p), p)

                def sigmoid_tiles(f, m):
                    def write(t, tile):
                        if not (isinstance(m, int) and m == 0 and t < 2):
                            act.wait_ge(dve_free, m * TILES + (t - 1))
                        nc.scalar.activation(sig[:, t % 2], tile, ACT.Sigmoid).then_inc(sig_ready, 1)
                    tiles(f, write)

                sigmoid_tiles(F_SILU, 0)
                sigmoid_tiles(F_SILU + 1, 1)
                with act.Fori(1, 4) as i:
                    sigmoid_tiles(i * 2 + F_SILU, i * 2)
                    sigmoid_tiles(i * 2 + (F_SILU + 1), i * 2 + 1)

                for g in range(4):
                    f = F_POOL + 2 * g
                    if g >= 1:
                        act.wait_ge(pool_d_ready, g)

                    def write(t, tile):
                        if t < TILES - 1:
                            nc.scalar.copy(X[:, 0, POOL_HALO + t * TW:POOL_HALO + (t + 1) * TW],
                                           tile).then_inc(act_free, 1)
                        else:
                            cut = NP_ - t * TW
                            nc.scalar.copy(X[:, 0, POOL_HALO + t * TW:POOL_HALO + NP_], tile[:, 0:cut])
                            nc.scalar.copy(X[:, 0, 2 * POOL_HALO + NP_:2 * POOL_HALO + NT],
                                           tile[:, cut:TW]).then_inc(act_free, 1)
                    tiles(f, write)
                    sigmoid_tiles(f + 1, 8 + g)

                def conv_block(p):
                    def write(t, tile):
                        if t < TILES - 1:
                            nc.scalar.copy(X[:, p, CONV_HALO + t * TW:CONV_HALO + (t + 1) * TW],
                                           tile).then_inc(act_free, 1)
                        else:
                            cut = NP_ - t * TW
                            nc.scalar.copy(X[:, p, CONV_HALO + t * TW:CONV_HALO + NP_], tile[:, 0:cut])
                            nc.scalar.copy(X[:, p, 2 * CONV_HALO + NP_:2 * CONV_HALO + NT],
                                           tile[:, cut:TW]).then_inc(act_free, 1)
                    return write

                def conv_sigmoid(j, p):
                    act.wait_ge(conv_ready, j + 1)
                    nc.scalar.activation(T[:, 0:NT], Y[:, p, 0:NT], ACT.Sigmoid).then_inc(conv_sig_ready, 1)

                def squares(j, p):
                    act.wait_ge(conv_silu_ready, j + 1)
                    nc.scalar.activation(T[:, 0:NT], Y[:, p, 0:NT], ACT.Square).then_inc(squares_ready, 1)

                def norm_logs(j, t):
                    act.wait_ge(side_ready, j * TILES + (6 * TILES + t + 1))
                    nc.scalar.activation(T[:, t * TW:(t + 1) * TW], side[:, t % 2, 0:TW], ACT.Ln,
                                         bias=small[:, S_EPS:S_EPS + 1]).then_inc(norm_free, 1)

                def norm_exp(j, q_scale):
                    act.wait_ge(norm_free, j * TILES + TILES)
                    if q_scale:
                        nc.scalar.activation(T[:, 0:NT], T[:, 0:NT], ACT.Exp, scale=-0.5,
                                             bias=small[:, S_QS:S_QS + 1]).then_inc(norm_ready, 1)
                    else:
                        nc.scalar.activation(T[:, 0:NT], T[:, 0:NT], ACT.Exp,
                                             scale=-0.5).then_inc(norm_ready, 1)

                def conv_slot(j, p, normed=None, square=True):
                    write = conv_block(p)
                    if normed is not None:
                        use_log_exp_tables(nc)
                        for t in range(TILES):
                            norm_logs(j - 2, t)
                    at_least(act, conv_ready, j - 1)
                    for t in range(TILES):
                        act.wait_ge(dense_ready, j * TILES + (F_CONV * TILES + t + 1))
                        write(t, dense[:, t % 2, 0:TW])
                        if t == 0 and normed is not None:
                            norm_exp(j - 2, normed)
                        if t == 3 and not (isinstance(j, int) and j == 0):
                            at_least(act, qkv_ready, j - 1)
                            conv_sigmoid(j - 1, 1 - p)
                        if t == 4 and square:
                            squares(j - 1, 1 - p)

                act.wait_ge(halo_set, 1)
                act.wait_ge(side_free, 6 * TILES)
                conv_slot(0, 1, square=False)
                conv_slot(1, 0)
                with act.Fori(0, 2) as i:
                    conv_slot(i * 2 + 2, 1, True)
                    conv_slot(i * 2 + 3, 0, True)
                conv_slot(6, 1, False)
                conv_slot(7, 0, False)
                conv_slot(8, 1, False)
                conv_slot(9, 0, False, square=False)
                conv_slot(10, 1, square=False)
                conv_slot(11, 0, square=False)

                def gate_block(i, f, p):
                    def write(t, tile):
                        nc.scalar.copy(Y[:, p, t * TW:(t + 1) * TW], tile).then_inc(act_free, 1)
                    tiles(f, write)

                act.wait_ge(qkv_ready, 11)
                conv_sigmoid(11, 0)
                act.wait_ge(qkv_stored[1], 6 * 16)
                gate_block(0, F_GATE, 1)
                act.wait_ge(qkv_stored[0], 6 * 16)
                gate_block(0, F_GATE + 1, 0)
                with act.Fori(1, EARLY_GATES // 2) as i:
                    for p in (1, 0):
                        act.wait_ge(gate_stored[p], i * 16)
                        gate_block(i, i * 2 + (F_GATE + 1 - p), p)

            @block.vector
            def _(dve):
                dve.wait_ge(params_landed, PARAMS)
                g_rows = slice(AT_G, AT_G + 4)
                b_rows = slice(AT_B, AT_B + 4)
                dve.wait_ge(special_ready, 1)
                links = [0]

                def link(ins):
                    links[0] += 1
                    ins.then_inc(special_step, 1)
                    dve.wait_ge(special_step, links[0])

                link(nc.vector.tensor_scalar(X[g_rows, 0, 0:NT], X[g_rows, 0, 0:NT],
                                             small[g_rows, S_DT:S_DT + 1], None, ALU.add))
                nc.vector.scalar_tensor_tensor(T[g_rows, 0:NT], X[g_rows, 0, 0:NT], -1.0, X[g_rows, 0, 0:NT],
                                               ALU.mult, ALU.max).then_inc(dve_done, 1)
                link(nc.vector.tensor_scalar(X[b_rows, 0, 0:NT], X[b_rows, 0, 0:NT], 1.0, None, ALU.add))
                nc.vector.reciprocal(X[b_rows, 0, 0:NT], X[b_rows, 0, 0:NT])
                dve.wait_ge(act_done, 3)
                link(nc.vector.scalar_tensor_tensor(X[g_rows, 0, 0:NT], X[g_rows, 0, 0:NT], 0.0,
                                                    T[g_rows, 0:NT], ALU.max, ALU.add))
                link(nc.vector.tensor_scalar(X[g_rows, 0, 0:NT], X[g_rows, 0, 0:NT],
                                             small[g_rows, S_NEGA:S_NEGA + 1], -1.0, ALU.mult, ALU.mult))
                for b in range(2):
                    if b == 1:
                        dve.wait_ge(special_stored, 16)
                    for t in range(TILES):
                        n = b * TILES + t
                        dve.wait_ge(side_ready, n + 1)
                        nc.vector.tensor_scalar(T[:, t * TW:(t + 1) * TW], side[:, n % 2, 0:TW],
                                                small[:, S_BF + b:S_BF + b + 1], None,
                                                ALU.add).then_inc(side_free, 1)
                    dve.wait_ge(side_free, (b + 1) * TILES)
                    nc.vector.scalar_tensor_tensor(X[:, 1, 0:NT], T[:, 0:NT], -1.0, T[:, 0:NT],
                                                   ALU.mult, ALU.max).then_inc(dve_done, 1)
                    dve.wait_ge(act_done, 5 + 2 * b)
                    nc.vector.scalar_tensor_tensor(T[:, 0:NT], T[:, 0:NT], 0.0, X[:, 1, 0:NT],
                                                   ALU.min, ALU.subtract).then_inc(logf_ready, 1)

                def silu_block(f, m, p):
                    for t in range(TILES):
                        dve.wait_ge(sig_ready, m * TILES + (t + 1))
                        b = f - F_SILU
                        nc.vector.scalar_tensor_tensor(Y[:, p, t * TW:(t + 1) * TW], dense[:, t % 2, 0:TW],
                                                       column(small, b + S_ZNORM), sig[:, t % 2],
                                                       ALU.mult, ALU.mult).then_inc(dve_free, 1)

                dve.wait_ge(copy_stored[1], 4 * 16)
                silu_block(F_SILU, 0, 1)
                dve.wait_ge(copy_stored[0], 4 * 16)
                silu_block(F_SILU + 1, 1, 0)
                with dve.Fori(1, 4) as i:
                    for p in (1, 0):
                        dve.wait_ge(silu_stored[p], i * 16)
                        silu_block(i * 2 + (F_SILU + 1 - p), i * 2 + (1 - p), p)

                def step(ins):
                    steps[0] += 1
                    ins.then_inc(pool_step, 1)
                    dve.wait_ge(pool_step, steps[0])
                steps = [0]
                dve.wait_ge(special_stored, 3 * 16)
                dve.wait_ge(silu_stored[0], 4 * 16)
                dve.wait_ge(silu_stored[1], 4 * 16)

                def windows(g):
                    win = 2 << g
                    span = NT + 2 * POOL_HALO
                    U = X[:, 0]
                    nc.vector.memset(U[:, 0:POOL_HALO], 0.0)
                    step(nc.vector.tensor_copy(U[:, POOL_HALO + NP_:2 * POOL_HALO + NP_],
                                               pool_out[:, 1, g]))
                    nc.vector.tensor_copy(pool_out[:, 0, g], U[:, NP_:NP_ + POOL_HALO])
                    step(nc.vector.tensor_copy(pool_out[:, 1, g], U[:, NT + POOL_HALO:NT + 2 * POOL_HALO]))
                    src, w = U, 1
                    turn = [T, X[:, 1]]
                    for n in range(g + 1):
                        dst = turn[(g - n) % 2]
                        step(nc.vector.tensor_tensor(dst[:, 2 * w - 1:span], src[:, 2 * w - 1:span],
                                                     src[:, w - 1:span - w], ALU.add))
                        src, w = dst, 2 * w
                        yield
                    step(nc.vector.scalar_tensor_tensor(
                        src[:, POOL_HALO:POOL_HALO + win - 1], src[:, POOL_HALO:POOL_HALO + win - 1],
                        float(win), consts[:, C_CNT:C_CNT + win - 1], ALU.mult, ALU.mult))
                    D = X[:, 1]
                    nc.vector.scalar_tensor_tensor(D[:, 0:NP_], src[:, POOL_HALO:POOL_HALO + NP_], 1.0 / win,
                                                   U[:, POOL_HALO:POOL_HALO + NP_], ALU.mult, ALU.subtract)
                    nc.vector.scalar_tensor_tensor(
                        D[:, NP_:NT], src[:, 2 * POOL_HALO + NP_:2 * POOL_HALO + NT], 1.0 / win,
                        U[:, 2 * POOL_HALO + NP_:2 * POOL_HALO + NT], ALU.mult,
                        ALU.subtract).then_inc(pool_d_ready, 1)

                def mapped(g):
                    if g >= 1:
                        dve.wait_ge(pool_stored, 16 * g)
                    for t in range(TILES):
                        n = (2 + g) * TILES + t
                        dve.wait_ge(side_ready, n + 1)
                        nc.vector.scalar_tensor_tensor(
                            Y[:, 1, t * TW:(t + 1) * TW], side[:, n % 2, 0:TW],
                            small[:, S_PSCALE + g:S_PSCALE + g + 1], Y[:, 0, t * TW:(t + 1) * TW],
                            ALU.mult, ALU.mult).then_inc(side_free, 1)

                for g in range(4):
                    if g >= 1:
                        mapped(g - 1)
                    dve.wait_ge(act_free, (A_POOL + g) * TILES + TILES)
                    steps_left = windows(g)
                    for t in range(TILES):
                        next(steps_left, None)
                        dve.wait_ge(sig_ready, (8 + g) * TILES + t + 1)
                        nc.vector.tensor_tensor(Y[:, 0, t * TW:(t + 1) * TW], dense[:, t % 2, 0:TW],
                                                sig[:, t % 2], ALU.mult).then_inc(dve_free, 1)
                mapped(3)

                for p in range(2):
                    last = nc.vector.memset(X[:, p, 0:CONV_HALO], 0.0)
                last.then_inc(halo_set, 1)
                SLOT_LINKS = 4

                def conv(j, p, stored=None):
                    def tap(n, ins):
                        ins.then_inc(conv_step, 1)
                        dve.wait_ge(conv_step, j * SLOT_LINKS + n)

                    dve.wait_ge(act_free, j * TILES + (A_CONV * TILES + TILES))
                    tap(1, nc.vector.tensor_copy(X[:, p, CONV_HALO + NP_:2 * CONV_HALO + NP_],
                                                 conv_cache[:, bass.ds(j, 1), :].rearrange("p a b -> p (a b)")))
                    for s, end in ((0, CONV_HALO + NP_), (1, 2 * CONV_HALO + NT)):
                        nc.vector.tensor_copy(conv_out[:, s, bass.ds(j, 1), :].rearrange("p a b -> p (a b)"),
                                              X[:, p, end - CONV_HALO:end])
                    if stored is not None:
                        dve.wait_ge(qkv_stored[p], stored)

                    def w(i):
                        return small[:, bass.ds(j * 4 + (S_CONV + i), 1)]
                    runs = ((0, NP_, 0), (NP_, NT, CONV_HALO))
                    for i in range(4):
                        for a, b, off in runs:
                            src = X[:, p, a + off + i:b + off + i]
                            if i == 0:
                                ins = nc.vector.tensor_scalar(Y[:, p, a:b], src, w(0), None, ALU.mult)
                            else:
                                ins = nc.vector.scalar_tensor_tensor(Y[:, p, a:b], src, w(i), Y[:, p, a:b],
                                                                     ALU.mult, ALU.add)
                        if i < 3:
                            tap(2 + i, ins)
                        else:
                            ins.then_inc(conv_ready, 1)

                def conv_silu(j, p, last=False):
                    dve.wait_ge(conv_sig_ready, j + 1)
                    ins = nc.vector.tensor_tensor(Y[:, p, 0:NT], Y[:, p, 0:NT], T[:, 0:NT], ALU.mult)
                    ins.then_inc(qkv_ready if last else conv_silu_ready, 1)

                def conv_norm(j, p):
                    dve.wait_ge(norm_ready, j + 1)
                    nc.vector.tensor_tensor(Y[:, p, 0:NT], Y[:, p, 0:NT], T[:, 0:NT],
                                            ALU.mult).then_inc(qkv_ready, 1)

                dve.wait_ge(pool_stored, 4 * 16)
                conv(0, 1)
                conv_silu(0, 1)
                conv(1, 0)
                conv_norm(0, 1)
                conv_silu(1, 0)
                with dve.Fori(0, 3) as i:
                    conv(i * 2 + 2, 1, i * 16 + 16)
                    conv_norm(i * 2 + 1, 0)
                    conv_silu(i * 2 + 2, 1)
                    conv(i * 2 + 3, 0, i * 16 + 16)
                    conv_norm(i * 2 + 2, 1)
                    conv_silu(i * 2 + 3, 0)
                conv(8, 1, 4 * 16)
                conv_norm(7, 0)
                conv_silu(8, 1, last=True)
                conv(9, 0, 4 * 16)
                conv_silu(9, 0, last=True)
                conv(10, 1, 5 * 16)
                conv_silu(10, 1, last=True)
                conv(11, 0, 5 * 16)
                conv_silu(11, 0, last=True)

            @block.sync
            def _(sp):
                for dst, src in (
                        (small[:, S_BF:S_BF + 2], d["gla_bf"]),
                        (small[:, S_PSCALE:S_PSCALE + 4], d["pool_scale"]),
                        (small[:, S_ZNORM:S_ZNORM + 4], d["gla_norm"]),
                        (small[:, S_ZNORM + 4:S_ZNORM + 8], d["gdn_norm"]),
                        (small[:, S_CONV:S_CONV + 48], d["gdn_conv"]),
                        (small[:, S_EPS:S_EPS + 2], d["scalars"]),
                        (small[AT_G:AT_G + 4, S_NEGA:S_NEGA + 1], d["gdn_a_log"]),
                        (small[AT_G:AT_G + 4, S_DT:S_DT + 1], d["gdn_dt_bias"]),
                        (wf2[:, :], d["gla_wf2"]),
                        (pool_w[:, :, :], d["pool_w"]),
                        (conv_cache[:, :, :], d["conv_cache"]),
                        (pool_out[:, 1], d["pool_cache"]),
                ):
                    sp.dma_start(dst, src).then_inc(params_landed, 16)

                def load_next(f, p):
                    sp.wait_ge(w_split, f + 1)
                    weights.load(sp, d, f + 2, p)

                def store(dst, row, ready, count, stored):
                    sp.wait_ge(ready, count)
                    sp.dma_start(dst, row).then_inc(stored, 16)

                load_next(0, 0)

                def copied(i, p):
                    load_next(i * 2 + (F_COPY + 1 - p), p)
                    sp.wait_ge(act_free, i * (2 * TILES) + (A_COPY + 2 - p) * TILES)
                    sp.dma_start(feat[:, bass.ds(i * 2 + (1 - p), 1)].rearrange("p a n -> p (a n)"),
                                 Y[:, p, 0:NT]).then_inc(copy_stored[p], 16)

                copied(0, 1)
                copied(0, 0)
                store(feat[:, R_LOGF], T[:, 0:NT], logf_ready, 1, special_stored)
                copied(1, 1)
                copied(1, 0)
                store(feat[:, R_LOGF + 1], T[:, 0:NT], logf_ready, 2, special_stored)
                store(feat[:, R_GB], X[:, 0, 0:NT], logf_ready, 2, special_stored)
                with sp.Fori(2, 4) as i:
                    for p in (1, 0):
                        copied(i, p)
                sp.dma_start(d["h_second"][:, 0], hi[1][:, :, :].bitcast(F32)).then_inc(h_saved, 16)
                sp.dma_start(d["h_second"][:, 1], lo[1][:, :, :].bitcast(F32)).then_inc(h_saved, 16)
                with sp.Fori(0, 4) as i:
                    for p in (1, 0):
                        load_next(i * 2 + (F_SILU + 1 - p), p)
                        sp.wait_ge(dve_free, i * (2 * TILES) + (2 - p) * TILES)
                        sp.dma_start(feat[:, bass.ds(i * 2 + (R_GLA_Z + 1 - p), 1)]
                                     .rearrange("p a n -> p (a n)"), Y[:, p, 0:NT]) \
                            .then_inc(silu_stored[p], 16)
                for g in range(4):
                    load_next(F_POOL + 2 * g, 1)
                    if g >= 1:
                        store(outs[:, 3 + g], Y[:, 1, 0:NT], side_free, (2 + g) * TILES, pool_stored)
                    load_next(F_POOL + 2 * g + 1, 0)
                store(outs[:, 7], Y[:, 1, 0:NT], side_free, 6 * TILES, pool_stored)
                load_next(F_CONV, 1)
                load_next(F_CONV + 1, 0)
                with sp.Fori(0, 5) as i:
                    for p in (1, 0):
                        load_next(i * 2 + (F_CONV + 3 - p), p)
                        sp.wait_ge(qkv_ready, i * 2 + (2 - p))
                        sp.dma_start(feat[:, bass.ds(i * 2 + (R_GDN_Q + 1 - p), 1)]
                                     .rearrange("p a n -> p (a n)"), Y[:, p, 0:NT]) \
                            .then_inc(qkv_stored[p], 16)
                load_next(F_GATE, 1)
                store(feat[:, R_GDN_V + 2], Y[:, 1, 0:NT], qkv_ready, 11, qkv_stored[1])
                load_next(F_GATE + 1, 0)
                store(feat[:, R_GDN_V + 3], Y[:, 0, 0:NT], qkv_ready, 12, qkv_stored[0])
                sp.dma_start(d["new_pool_prompt"], pool_out[:, 0]).then_inc(caches_stored, 16)
                sp.dma_start(d["new_pool_sample"], pool_out[:, 1]).then_inc(caches_stored, 16)
                sp.dma_start(d["new_conv_prompt"], conv_out[:, 0]).then_inc(caches_stored, 16)
                sp.dma_start(d["new_conv_sample"], conv_out[:, 1]).then_inc(caches_stored, 16)
                with sp.Fori(0, EARLY_GATES // 2 - 2) as i:
                    for p in (1, 0):
                        load_next(i * 2 + (F_GATE + 3 - p), p)
                        sp.wait_ge(act_free, i * (2 * TILES) + (A_GATE + 2 - p) * TILES)
                        sp.dma_start(gates[:, bass.ds(i * 2 + (1 - p), 1)].rearrange("p a n -> p (a n)"),
                                     Y[:, p, 0:NT]).then_inc(gate_stored[p], 16)
                for n in range(EARLY_GATES - 4, EARLY_GATES):
                    p = 1 - n % 2
                    store(gates[:, n], Y[:, p, 0:NT], act_free, (A_GATE + n + 1) * TILES, gate_stored[p])
                sp.wait_ge(caches_stored, 4 * 16)
                sp.wait_ge(h_saved, 2 * 16)
                for p in range(2):
                    sp.wait_ge(gate_stored[p], EARLY_GATES // 2 * 16)


def chunk_phase(nc, d, consts, h_hi, h_lo, late):
    TURNS = LEVELS - 2
    with ExitStack() as ctx, Held(nc) as held:
        def sb(name, shape, dt=F32):
            return ctx.enter_context(nc.sbuf_tensor(name, shape, dt))

        def bank(name, shape=(P, HEADS, P)):
            return ctx.enter_context(nc.psum_tensor(name, list(shape), F32))

        masks = sb("masks", [P, M_END])
        gate_w = sb("gate_w", [P, 2, KD, P])
        gate_w_hi = sb("gate_w_hi", [P, 2, KD, P], F32R)
        gate_w_lo = sb("gate_w_lo", [P, 2, KD, P], F32R)
        zero = sb("chunk_zero", [P, 1])
        gate_row = sb("gate_row", [P, 2, TW])
        eps = sb("chunk_eps", [P, 1])
        inputs = sb("inputs", [P, 2, R_END, P])
        decay_beta = sb("decay_beta", [P, 2, HEADS])
        g_col = sb("g_col", [P, HEADS])
        g_row = sb("g_row", [P, HEADS, P])
        e_row = sb("e_row", [P, HEADS, P])
        d_col = sb("d_col", [P, HEADS])
        dec_kk = sb("dec_kk", [P, HEADS, P])
        dec_qk = sb("dec_qk", [P, HEADS, P])
        M = sb("M", [P, HEADS, P])
        M0 = sb("M0", [P, HEADS, P])
        X = sb("X", [P, HEADS, P])
        XT = sb("XT", [P, HEADS, P])
        Z = sb("Z", [P, HEADS, HALF])
        att = sb("att", [P, HEADS, P])
        k_dec = sb("k_dec", [P, HEADS, P])
        q_dec = sb("q_dec", [P, HEADS, P])
        k_tok = sb("k_tok", [P, HEADS, P])
        v_tok = sb("v_tok", [P, HEADS, P])
        U = sb("U", [P, HEADS, P])
        state = sb("state", [P, HEADS, P])
        b_sum = sb("b_sum", [P, 2, P])
        F = sb("F", [P, LEVELS + 2, 2, P])
        KF = sb("KF", [P, LEVELS + 1, 2, P])
        QF = sb("QF", [P, LEVELS + 1, 2, P])
        masked = sb("masked", [P, HEADS, LEVELS, HALF])
        gla_att = sb("gla_att", [P, HEADS, P])
        gla_v = sb("gla_v", [P, HEADS, P])
        gla_k = sb("gla_k", [P, 2, P])
        gla_state = sb("gla_state", [P, HEADS, P])
        sq = [sb("sq_gdn", [P, HEADS, P]), sb("sq_gla", [P, HEADS, P])]
        out_sb = [sb("out_gdn", [P, HEADS, P]), sb("out_gla", [P, HEADS, P])]

        level_bank = bank("level_bank", (P, 2, HEADS, HALF))
        z_bank, xt_bank = level_bank[:, 0], level_bank[:, 1]
        x_bank = bank("x_bank")
        pair_bank = bank("pair_bank", (P, 8, HALF))
        gate_bank = bank("gate_bank", (P, 2, 512))
        ring = [bank("ring0"), bank("ring1"), bank("ring2")]

        ident = consts[:, C_IDENT:C_IDENT + P]
        ones = consts[:, C_ONES:C_ONES + P]
        upper = masks[:, M_UPPER:M_UPPER + P]
        level_masks = masks[:, M_PAIRS:M_END].rearrange("p (l t) -> p l t", t=HALF)

        PE_ = ("gbt", "gcol", "vt", "kt", "grow", "KK", "QK", "vtg", "diag_even", "diag",
                 "m0t", "R", "kdtg", "Og", "U", "O", "dS",
                 "dSg", "SSQ", "SSQg")
        DVE_ = ("gb_taken", "gcol_taken", "kt_taken", "KK_taken", "QK_taken", "m0t_taken", "R_taken",
                "O_scaled", "Og_scaled", "dS_taken", "dSg_taken", "b_ready", "F_diffs", "KF_ready",
                "XTb_ready", "M0_ready", "X_ready", "dcol_diff",
                "diag_taken")
        ACT_ = ("vt_taken", "grow_taken", "e_row_ready", "d_col_ready", "dec_qk_ready", "dec_kk_ready",
                "vtg_taken", "kdtg_taken", "U_taken", "F_abs", "F_ready", "O_squared", "Og_squared", "SSQ_taken",
                "SSQg_taken", "rs_ready", "rsg_ready")
        POOL_ = ("diff_ready", "dec_args", "k_dec_ready", "q_dec_ready", "QF_ready",
                 "gla_att_ready", "out_ready", "outg_ready")
        EARLY = {"SSQ_taken", "SSQg_taken", "dSg_taken", "dSg", "dS_taken", "O", "Og", "out_ready", "outg_ready",
                 "R_taken", "dec_args", "KK_taken", "QK_taken", "QF_ready", "q_dec_ready", "kdtg"}
        S = {n: held.add(nc.alloc_semaphore(n)) for n in PE_ + DVE_ + ACT_ + POOL_}
        z_ready = held.add(nc.alloc_semaphore("z_ready"))
        z_taken = held.add(nc.alloc_semaphore("z_taken"))
        xt_products = held.add(nc.alloc_semaphore("xt_products"))
        xt_updated = held.add(nc.alloc_semaphore("xt_updated"))
        x_turned = held.add(nc.alloc_semaphore("x_turned"))
        x_taken = held.add(nc.alloc_semaphore("x_taken"))
        pairs_ready = held.add(nc.alloc_semaphore("pairs_ready"))
        pairs_masked = held.add(nc.alloc_semaphore("pairs_masked"))
        att_added = held.add(nc.alloc_semaphore("att_added"))
        h_landed = [held.add(nc.alloc_semaphore(f"h_landed{t}")) for t in range(3)]
        h_good = [held.add(nc.alloc_semaphore(f"h_good{t}")) for t in range(3)]
        gate_w_high = held.add(nc.alloc_semaphore("gate_w_high"))
        gate_w_split = held.add(nc.alloc_semaphore("gate_w_split"))
        zero_set = held.add(nc.alloc_semaphore("chunk_zero_set"))
        gate_w_landed = [held.add(nc.alloc_semaphore(f"gate_w_landed{p}")) for p in range(2)]
        gate_ready = held.add(nc.alloc_semaphore("gate_ready"))
        gate_taken = held.add(nc.alloc_semaphore("gate_taken"))
        gate_stored = [held.add(nc.alloc_semaphore(f"late_gate_stored{p}")) for p in range(2)]
        in_landed = [held.add(nc.alloc_semaphore(f"in_landed{p}")) for p in range(2)]
        masks_landed = held.add(nc.alloc_semaphore("masks_landed"))
        eps_ready = held.add(nc.alloc_semaphore("eps_ready"))
        state_landed = held.add(nc.alloc_semaphore("state_landed"))
        state_stored = held.add(nc.alloc_semaphore("state_stored"))
        state_zero = held.add(nc.alloc_semaphore("state_zero"))
        out_stored = held.add(nc.alloc_semaphore("out_stored"))
        outg_stored = held.add(nc.alloc_semaphore("outg_stored"))
        feat, outs, gates = d["feat"], d["branch_out"], d["gates"]

        def now(eng, name, c):
            eng.wait_ge(S[name], c + (2 if name in EARLY else 1))

        def before(eng, name, c):
            assert name in EARLY, name
            eng.wait_ge(S[name], c + 1)

        def preload(eng, names):
            for name in names:
                if name in EARLY:
                    eng.sem_inc(S[name], 1)

        def half_of(h):
            return slice(64 * (h % 2), 64 * (h % 2) + 64)

        def levels_of(n):
            return n.bit_length() - 1

        with nc.Block() as block:
            @block.sync
            def _(sp):
                def load(c, p, n=P):
                    sp.dma_start(inputs[:, p, :, 0:n], feat[:, :, bass.ds(c * P, n)]).then_inc(in_landed[p], 16)

                def load_gate_w(c, r, half):
                    block = c * 2 + (F_LATE + r - half * LATE_GATES)
                    sp.dma_start(gate_w[:, r].rearrange("p k m -> p (k m)"),
                                 d["w_in"][bass.ds(block, 1)].rearrange("a p n -> p (a n)")) \
                        .then_inc(gate_w_landed[r], 16)

                def gate_traffic(c, half, next_half):
                    if next_half is not None:
                        sp.wait_ge(gate_w_split, c * 2 + 1)
                        load_gate_w(c + 1, 0, next_half)
                    for T in range(TILES):
                        r, t = T // 3, T % 3
                        sp.wait_ge(gate_taken, c * TILES + (T + 3))
                        sp.dma_start(gates[:, bass.ds(c * 2 + (EARLY_GATES + r - half * LATE_GATES), 1),
                                           half * HALF_TOKENS + t * TW:half * HALF_TOKENS + (t + 1) * TW]
                                     .rearrange("p a n -> p (a n)"), gate_row[:, T % 2]) \
                            .then_inc(gate_stored[T % 2], 16)
                        if T == 0 and next_half is not None:
                            sp.wait_ge(gate_w_split, c * 2 + 2)
                            load_gate_w(c + 1, 1, next_half)
                    if half == 1 and next_half is not None:
                        for t in range(3):
                            sp.sem_inc(h_good[t], 1)

                def store(c, n=P):
                    now(sp, "outg_ready", c)
                    sp.dma_start(outs[:, 0:4, bass.ds(c * P, n)], out_sb[1][:, :, 0:n]).then_inc(outg_stored, 16)
                    now(sp, "out_ready", c)
                    sp.dma_start(outs[:, 8:12, bass.ds(c * P, n)], out_sb[0][:, :, 0:n]).then_inc(out_stored, 16)

                sp.sem_inc(out_stored, 16)
                sp.sem_inc(outg_stored, 16)
                for q in range(2):
                    sp.sem_inc(gate_stored[q], 16)
                sp.dma_start(masks[:, :], d["masks"]).then_inc(masks_landed, 16)
                load_gate_w(0, 0, 0)
                load(0, 0)
                load_gate_w(0, 1, 0)
                load(1, 1)

                for t in range(3):
                    sp.sem_inc(h_good[t], CHUNKS // 2)

                def outputs(c, p):
                    store(c)
                    load(c + 2, p)
                with sp.Fori(0, CHUNKS // 4 - 1) as i:
                    for p in range(2):
                        gate_traffic(i * 2 + p, 0, 0)
                        outputs(i * 2 + p, p)
                gate_traffic(CHUNKS // 2 - 2, 0, 0)
                outputs(CHUNKS // 2 - 2, 0)
                gate_traffic(CHUNKS // 2 - 1, 0, 1)
                outputs(CHUNKS // 2 - 1, 1)
                for t in range(3):
                    sp.wait_ge(h_landed[t], 2 * 16)
                    sp.sem_inc(h_good[t], 1)
                with sp.Fori(CHUNKS // 4, CHUNKS // 2 - 1) as i:
                    for p in range(2):
                        gate_traffic(i * 2 + p, 1, 1)
                        outputs(i * 2 + p, p)
                gate_traffic(CHUNKS - 2, 1, 1)
                store(CHUNKS - 2)
                load(CHUNKS, 0, NS_)
                gate_traffic(CHUNKS - 1, 1, None)
                store(CHUNKS - 1)
                now(sp, "dS_taken", CHUNKS - 1)
                now(sp, "dSg_taken", CHUNKS - 1)
                sp.dma_start(d["new_gdn_prompt"].rearrange("h d v -> d h v"), state[:, :, :]) \
                    .then_inc(state_stored, 16)
                for h in range(HEADS):
                    sp.dma_start(d["new_gla_prompt"][h], gla_state[half_of(h), h]).then_inc(state_stored, 16)
                sp.wait_ge(state_stored, 5 * 16)
                sp.dma_start(state[:, :, :], d["state_gdn"].rearrange("h d v -> d h v")).then_inc(state_landed, 16)
                for h in range(HEADS):
                    sp.dma_start(gla_state[half_of(h), h], d["state_gla"][h]).then_inc(state_landed, 16)
                late.load_in_chunk_phase(sp, d)
                store(CHUNKS, NS_)
                now(sp, "dS_taken", CHUNKS)
                now(sp, "dSg_taken", CHUNKS)
                sp.dma_start(d["new_gdn_sample"].rearrange("h d v -> d h v"), state[:, :, :]) \
                    .then_inc(state_stored, 16)
                for h in range(HEADS):
                    sp.dma_start(d["new_gla_sample"][h], gla_state[half_of(h), h]).then_inc(state_stored, 16)
                sp.wait_ge(state_stored, 10 * 16)
                sp.wait_ge(out_stored, 16 * (CHUNKS + 2))
                sp.wait_ge(outg_stored, 16 * (CHUNKS + 2))
                for q in range(2):
                    sp.wait_ge(gate_stored[q], 16 * (LATE_GATES * TILES // 2 + 1))

            def per_chunk(eng, chunk):
                with eng.Fori(0, CHUNKS // 2) as i:
                    chunk(i * 2, i, 0, P)
                    chunk(i * 2 + 1, i, 1, P)
                chunk(CHUNKS, CHUNKS // 2, 0, NS_)

            @block.tensor
            def _(pe):
                matmul, transpose = nc.tensor.matmul, nc.tensor.transpose

                def chunk(c, i, p, n):
                    I = inputs[:, p]
                    L = levels_of(n)
                    sample = isinstance(c, int) and c == CHUNKS
                    steps = [0]

                    def gate_products(count):
                        count *= 3
                        for g in range(steps[0], 0 if sample else steps[0] + count):
                            T, k, part = g // (3 * KD), g // 3 % KD, g % 3
                            r, t = T // 3, T % 3
                            if g % (9 * KD) == 0:
                                pe.wait_ge(gate_w_split, c * 2 + (r + 1))
                            if k == 0 and part == 0:
                                pe.wait_ge(gate_taken, c * TILES + (T + 1))
                                pe.wait_ge(h_good[t], c + 1)
                            w = gate_w_lo if part == 2 else gate_w_hi
                            h = h_lo if part == 1 else h_hi
                            mm = matmul(gate_bank[:, T % 2, 0:TW], w[:, r, k], h[:, k, t * TW:(t + 1) * TW],
                                        start=(k == 0 and part == 0), stop=(k == KD - 1 and part == 2))
                            if k == KD - 1 and part == 2:
                                mm.then_inc(gate_ready, 1)
                        steps[0] += count

                    gate_products(2)
                    pe.wait_ge(in_landed[p], i * 16 + 16)
                    before(pe, "SSQ_taken", c)
                    transpose(ring[0][0:n, 0], I[:, R_GB, 0:n], ident).then_inc(S["gbt"], 1)
                    before(pe, "SSQg_taken", c)
                    for h in range(HEADS):
                        mm = transpose(ring[1][0:n, h], I[:, R_GDN_V + h, 0:n], ident)
                    mm.then_inc(S["vt"], 1)
                    before(pe, "dSg_taken", c)
                    for h in range(HEADS):
                        mm = transpose(ring[2][0:n, h], I[:, R_GDN_K + h, 0:n], ident)
                    mm.then_inc(S["kt"], 1)
                    gate_products(2)
                    now(pe, "gb_taken", c)
                    matmul(ring[0][0:n, 1, 0:HEADS], upper[0:n, 0:n], decay_beta[0:n, 0, :],
                           start=True, stop=True).then_inc(S["gcol"], 1)
                    gate_products(5)
                    now(pe, "gcol_taken", c)
                    for h in range(HEADS):
                        mm = matmul(ring[0][:, h, 0:n], decay_beta[0:n, 0, h:h + 1].to_broadcast([n, P]),
                                    upper[0:n, 0:n], start=True, stop=True)
                    mm.then_inc(S["grow"], 1)
                    now(pe, "vt_taken", c)
                    for h in range(HEADS):
                        k = I[:, R_GDN_K + h, 0:n]
                        mm = matmul(ring[1][0:n, h, 0:n], k, k, start=True, stop=True)
                    mm.then_inc(S["KK"], 1)
                    gate_products(5)
                    now(pe, "kt_taken", c)
                    for h in range(HEADS):
                        mm = matmul(ring[2][0:n, h, 0:n], I[:, R_GDN_K + h, 0:n], I[:, R_GDN_Q + h, 0:n],
                                    start=True, stop=True)
                    mm.then_inc(S["QK"], 1)
                    gate_products(2)
                    now(pe, "grow_taken", c)
                    for h in range(HEADS):
                        mm = transpose(ring[0][0:n, h], I[:, R_GLA_V + h, 0:n], ident)
                    mm.then_inc(S["vtg"], 1)
                    gate_products(6)
                    now(pe, "M0_ready", c)
                    now(pe, "KK_taken", c)
                    for h in range(HEADS):
                        mm = transpose(ring[1][0:n, h, 0:n], M0[0:n, h, 0:n], ident[0:n, 0:n])
                    mm.then_inc(S["m0t"], 1)
                    gate_products(1)
                    now(pe, "QK_taken", c)
                    now(pe, "k_dec_ready", c)
                    before(pe, "dS_taken", c)
                    if sample:
                        pe.wait_ge(state_landed, 5 * 16)
                    for h in range(HEADS):
                        mm = matmul(ring[2][0:n, h], k_dec[:, h, 0:n], state[:, h], start=True, stop=True)
                    mm.then_inc(S["R"], 1)

                    def pairs(h):
                        rows = half_of(h)
                        b = h // 2
                        if h == 0:
                            now(pe, "KF_ready", c)
                            now(pe, "QF_ready", c)
                            pe.wait_ge(pairs_masked, c * HEADS + 1)
                        else:
                            pe.wait_ge(pairs_masked, c * HEADS + h + 1)
                        for l in range(L):
                            s = 1 << l
                            mm = matmul(halves_packed(pair_bank[0:n, l:l + 1, 0:n // 2], s)[:, 0],
                                        KF[rows, l, b, 0:n], second_halves(QF[rows, l + 1, b:b + 1, 0:n], s)[:, 0],
                                        start=True, stop=True)
                        mm.then_inc(pairs_ready, 1)

                    def own_pairs(first, signal):
                        for h in (first, first + 2):
                            rows, b = half_of(h), h // 2
                            mm = matmul(ring[0][0:n, h, 0:n], I[rows, R_GLA_K + b, 0:n], I[rows, R_GLA_Q + b, 0:n],
                                        start=True, stop=True)
                        mm.then_inc(S[signal], 1)

                    def diagonal():
                        now(pe, "vtg_taken", c)
                        own_pairs(0, "diag_even")
                        now(pe, "diag_even", c)
                        own_pairs(1, "diag")

                    def key_turns():
                        now(pe, "diag_taken", c)
                        for b in range(2):
                            mm = transpose(ring[0][0:n, b], KF[:, LEVELS, b, 0:n], ident)
                        mm.then_inc(S["kdtg"], 1)

                    between = {0: diagonal, 1: lambda: pairs(0), 2: lambda: pairs(1), 3: lambda: pairs(2),
                               4: lambda: pairs(3), 5: key_turns}
                    for l in range(1, L):
                        s = 1 << l
                        gate_products(3 if l == 1 else 2)
                        if l == 1:
                            now(pe, "m0t_taken", c)
                            now(pe, "X_ready", c)
                        else:
                            pe.wait_ge(xt_updated, c * (LEVELS - 1) + (l - 1))
                        for h in range(HEADS):
                            mm = matmul(halves_packed(z_bank[0:n, h:h + 1, 0:n // 2], s)[:, 0], M[0:n, h, 0:n],
                                        second_halves(XT[0:n, h:h + 1, 0:n], s)[:, 0], start=True, stop=True)
                        mm.then_inc(z_ready, 1)
                        if l > 1:
                            for h in range(HEADS):
                                mm = transpose(x_bank[0:n, h, 0:n], XT[0:n, h, 0:n], ident[0:n, 0:n])
                            mm.then_inc(x_turned, 1)
                        if l - 1 in between:
                            between[l - 1]()
                        gate_products({1: 1, LEVELS - 1: 2}.get(l, 0))
                        pe.wait_ge(z_taken, c * (LEVELS - 1) + l)
                        if l > 1:
                            pe.wait_ge(x_taken, c * TURNS + (l - 1))
                        for h in range(HEADS):
                            mm = matmul(halves_packed(xt_bank[0:n, h:h + 1, 0:n // 2], s)[:, 0], X[0:n, h, 0:n],
                                        halves_packed(Z[0:n, h:h + 1, 0:n // 2], s)[:, 0], start=True, stop=True)
                        mm.then_inc(xt_products, 1)
                    if L - 1 < 6:
                        key_turns()
                    gate_products(3)
                    now(pe, "R_taken", c)
                    now(pe, "XTb_ready", c)
                    for h in range(HEADS):
                        mm = matmul(ring[2][0:n, h], XT[0:n, h, 0:n], U[0:n, h], start=True, stop=True)
                    mm.then_inc(S["U"], 1)
                    gate_products(1)
                    now(pe, "gla_att_ready", c)
                    now(pe, "m0t_taken", c)
                    before(pe, "dSg_taken", c)
                    for h in range(HEADS):
                        matmul(ring[1][:, h, 0:n], gla_v[0:n, h], gla_att[0:n, h, 0:n], start=True, stop=False)
                        mm = matmul(ring[1][:, h, 0:n], gla_state[:, h], QF[:, 0, h // 2, 0:n],
                                    start=False, stop=True)
                    mm.then_inc(S["Og"], 1)
                    gate_products(1)
                    now(pe, "kdtg_taken", c)
                    now(pe, "q_dec_ready", c)
                    now(pe, "U_taken", c)
                    for h in range(HEADS):
                        matmul(ring[0][:, h, 0:n], U[0:n, h], att[0:n, h, 0:n], start=True, stop=False)
                        mm = matmul(ring[0][:, h, 0:n], state[:, h], q_dec[:, h, 0:n], start=False, stop=True)
                    mm.then_inc(S["O"], 1)
                    now(pe, "Og_scaled", c)
                    now(pe, "Og_squared", c)
                    for h in range(HEADS):
                        mm = matmul(ring[1][:, h], k_tok[0:n, h], U[0:n, h], start=True, stop=True)
                    mm.then_inc(S["dS"], 1)
                    for h in range(HEADS):
                        mm = matmul(ring[2][:, h], gla_k[0:n, h // 2], gla_v[0:n, h], start=True, stop=True)
                    mm.then_inc(S["dSg"], 1)
                    gate_products(2)
                    now(pe, "O_scaled", c)
                    now(pe, "O_squared", c)
                    matmul(ring[0][:, :, 0:n], ones, sq[0][:, :, 0:n], start=True, stop=True).then_inc(S["SSQ"], 1)
                    gate_products(2)
                    now(pe, "dS_taken", c)
                    matmul(ring[1][:, :, 0:n], ones, sq[1][:, :, 0:n], start=True, stop=True).then_inc(S["SSQg"], 1)

                pe.wait_ge(masks_landed, 16)
                preload(pe, PE_)
                per_chunk(pe, chunk)

            @block.scalar
            def _(act):
                copy, activation = nc.scalar.copy, nc.scalar.activation

                def head_norm(c, n, which, ready, taken, done):
                    s = sq[which][:, :, 0:n]
                    now(act, ready, c)
                    activation(s, ring[which][:, :, 0:n], ACT.Ln, bias=eps[:, 0:1], scale=1.0 / P) \
                        .then_inc(S[taken], 1)
                    now(act, taken, c)
                    activation(s, s, ACT.Exp, scale=-0.5).then_inc(S[done], 1)

                def gates_out(c, t):
                    if isinstance(c, int) and c == CHUNKS:
                        return
                    act.wait_ge(gate_ready, c * TILES + (t + 1))
                    act.wait_ge(gate_stored[t % 2], c * (TILES // 2 * 16) + (t // 2 + 1) * 16)
                    copy(gate_row[:, t % 2], gate_bank[:, t % 2, 0:TW]).then_inc(gate_taken, 1)

                def chunk(c, i, p, n):
                    L = levels_of(n)
                    now(act, "vt", c)
                    before(act, "R_taken", c)
                    copy(v_tok[0:n], ring[1][0:n]).then_inc(S["vt_taken"], 1)
                    now(act, "grow", c)
                    before(act, "dec_args", c)
                    copy(g_row[:, :, 0:n], ring[0][:, :, 0:n]).then_inc(S["grow_taken"], 1)
                    now(act, "grow_taken", c)
                    before(act, "dS_taken", c)
                    before(act, "q_dec_ready", c)
                    activation(e_row[:, :, 0:n], g_row[:, :, 0:n], ACT.Exp).then_inc(S["e_row_ready"], 1)
                    gates_out(c, 0)
                    now(act, "dcol_diff", c)
                    activation(d_col[0:n], d_col[0:n], ACT.Exp).then_inc(S["d_col_ready"], 1)
                    now(act, "dec_args", c)
                    activation(dec_kk[0:n, :, 0:n], dec_kk[0:n, :, 0:n], ACT.Exp, scale=-1.0) \
                        .then_inc(S["dec_kk_ready"], 1)
                    activation(dec_qk[0:n, :, 0:n], dec_qk[0:n, :, 0:n], ACT.Exp) \
                        .then_inc(S["dec_qk_ready"], 1)
                    now(act, "F_diffs", c)
                    activation(F[:, :, :, 0:n], F[:, :, :, 0:n], ACT.Abs).then_inc(S["F_abs"], 1)
                    gates_out(c, 1)
                    now(act, "F_abs", c)
                    activation(F[:, :, :, 0:n], F[:, :, :, 0:n], ACT.Exp, scale=-1.0 / 16).then_inc(S["F_ready"], 1)
                    now(act, "vtg", c)
                    before(act, "dSg", c)
                    copy(gla_v[0:n], ring[0][0:n]).then_inc(S["vtg_taken"], 1)
                    gates_out(c, 2)
                    gates_out(c, 3)
                    now(act, "kdtg", c)
                    copy(gla_k[0:n], ring[0][0:n, 0:2]).then_inc(S["kdtg_taken"], 1)
                    now(act, "U", c)
                    copy(U[0:n], ring[2][0:n]).then_inc(S["U_taken"], 1)
                    now(act, "Og", c)
                    before(act, "outg_ready", c)
                    activation(sq[1][:, :, 0:n], ring[1][:, :, 0:n], ACT.Square).then_inc(S["Og_squared"], 1)
                    gates_out(c, 4)
                    now(act, "O", c)
                    before(act, "out_ready", c)
                    activation(sq[0][:, :, 0:n], ring[0][:, :, 0:n], ACT.Square).then_inc(S["O_squared"], 1)
                    head_norm(c, n, 0, "SSQ", "SSQ_taken", "rs_ready")
                    gates_out(c, 5)
                    head_norm(c, n, 1, "SSQg", "SSQg_taken", "rsg_ready")

                use_log_exp_tables(nc)
                act.wait_ge(eps_ready, 1)
                preload(act, ACT_)
                act.sem_inc(gate_taken, 2)
                per_chunk(act, chunk)

            @block.gpsimd
            def _(pool):
                tt = nc.gpsimd.tensor_tensor
                zeros = zero[:, 0:1].rearrange("p (a b) -> p a b", b=1).to_broadcast([P, KD, P])

                def split_gate_w(c, r):
                    pool.wait_ge(gate_w_landed[r], c * 16 + 16)
                    tt(gate_w_hi[:, r], gate_w[:, r], zeros, ALU.add).then_inc(gate_w_high, 1)
                    pool.wait_ge(gate_w_high, c * 2 + (r + 1))
                    tt(gate_w_lo[:, r], gate_w[:, r], gate_w_hi[:, r].bitcast(F32),
                       ALU.subtract).then_inc(gate_w_split, 1)

                def load_h(t):
                    pool.wait_ge(gate_taken, (CHUNKS // 2 - 1) * TILES + (t + 6))
                    cols = slice(t * TW, (t + 1) * TW)
                    for part, h in enumerate((h_hi, h_lo)):
                        nc.gpsimd.dma_start(h[:, :, cols], d["h_second"][:, part, :, cols].bitcast(F32R)) \
                            .then_inc(h_landed[t], 16)

                def chunk(c, p, n):
                    I = inputs[:, p]
                    sample = isinstance(c, int) and c == CHUNKS
                    swap = isinstance(c, int) and c == CHUNKS // 2 - 1

                    def over_heads(x):
                        return x.rearrange("p (a b) -> p a b", a=1).to_broadcast([n, HEADS, n])
                    now(pool, "grow_taken", c)
                    now(pool, "gcol_taken", c)
                    before(pool, "QK_taken", c)
                    tt(dec_qk[0:n, :, 0:n], g_row[0:n, :, 0:n],
                       g_col[0:n].rearrange("p (a b) -> p a b", b=1).to_broadcast([n, HEADS, n]),
                       ALU.subtract).then_inc(S["diff_ready"], 1)
                    now(pool, "diff_ready", c)
                    before(pool, "KK_taken", c)
                    tt(dec_kk[0:n, :, 0:n], dec_qk[0:n, :, 0:n], over_heads(masks[0:n, M_POS:M_POS + n]), ALU.add)
                    tt(dec_qk[0:n, :, 0:n], dec_qk[0:n, :, 0:n], over_heads(masks[0:n, M_NEG:M_NEG + n]),
                       ALU.add).then_inc(S["dec_args"], 1)
                    now(pool, "e_row_ready", c)
                    before(pool, "O", c)
                    tt(k_dec[:, :, 0:n], I[:, R_GDN_K:R_GDN_K + 4, 0:n], e_row[:, :, 0:n],
                       ALU.mult).then_inc(S["k_dec_ready"], 1)
                    now(pool, "F_ready", c)
                    before(pool, "Og", c)
                    q = I[:, R_GLA_Q:R_GLA_Q + 2, 0:n].rearrange("p (l b) t -> p l b t", l=1)
                    for b in range(2):
                        last = tt(QF[:, :, b, 0:n], q[:, :, b].to_broadcast([P, LEVELS + 1, n]),
                                  F[:, 0:LEVELS + 1, b, 0:n], ALU.mult)
                    last.then_inc(S["QF_ready"], 1)
                    tt(q_dec[:, :, 0:n], I[:, R_GDN_Q:R_GDN_Q + 4, 0:n], e_row[:, :, 0:n],
                       ALU.mult).then_inc(S["q_dec_ready"], 1)
                    if not (isinstance(c, int) and c >= CHUNKS - 1):
                        pool.wait_ge(gate_ready, c * TILES + 3)
                        split_gate_w(c + 1, 0)
                    if swap:
                        load_h(0)
                    now(pool, "diag_taken", c)
                    pool.wait_ge(pairs_masked, c * HEADS + (HEADS + 1))
                    L = levels_of(n)
                    for l in range(L):
                        s = 1 << l
                        own = second_halves(gla_att[0:n, :, 0:n], s)
                        ins = tt(own, own, halves_packed(masked[0:n, :, l, 0:n // 2], s), ALU.add)
                        if l < L - 1:
                            ins.then_inc(att_added, 1)
                            pool.wait_ge(att_added, c * (LEVELS - 1) + (l + 1))
                        else:
                            ins.then_inc(S["gla_att_ready"], 1)
                    if swap:
                        load_h(1)
                    now(pool, "rs_ready", c)
                    now(pool, "O_scaled", c)
                    tt(out_sb[0][:, :, 0:n], out_sb[0][:, :, 0:n], sq[0][:, :, 0:n], ALU.mult) \
                        .then_inc(S["out_ready"], 1)
                    now(pool, "rsg_ready", c)
                    tt(out_sb[1][:, :, 0:n], out_sb[1][:, :, 0:n], sq[1][:, :, 0:n], ALU.mult) \
                        .then_inc(S["outg_ready"], 1)
                    if not (isinstance(c, int) and c >= CHUNKS - 1):
                        pool.wait_ge(gate_ready, c * TILES + TILES)
                        split_gate_w(c + 1, 1)
                    if swap:
                        load_h(2)

                preload(pool, POOL_)
                nc.gpsimd.memset(zero[:, :], 0.0).then_inc(zero_set, 1)
                pool.wait_ge(zero_set, 1)
                for r in range(2):
                    split_gate_w(0, r)
                with pool.Fori(0, CHUNKS // 4 - 1) as i:
                    chunk(i * 2, 0, P)
                    chunk(i * 2 + 1, 1, P)
                chunk(CHUNKS // 2 - 2, 0, P)
                chunk(CHUNKS // 2 - 1, 1, P)
                with pool.Fori(CHUNKS // 4, CHUNKS // 2 - 1) as i:
                    chunk(i * 2, 0, P)
                    chunk(i * 2 + 1, 1, P)
                chunk(CHUNKS - 2, 0, P)
                chunk(CHUNKS - 1, 1, P)
                chunk(CHUNKS, 0, NS_)

            @block.vector
            def _(dve):
                tt, stt, cp = nc.vector.tensor_tensor, nc.vector.scalar_tensor_tensor, nc.vector.tensor_copy

                def chunk(c, i, p, n):
                    I = inputs[:, p]
                    L = levels_of(n)

                    def over_heads(x, m=HEADS):
                        return x.rearrange("p (a b) -> p a b", a=1).to_broadcast([n, m, n])

                    def per_token(x, w=P):
                        return x.rearrange("p (a b) -> p a b", b=1).to_broadcast([n, HEADS, w])
                    beta = decay_beta[0:n, 1]
                    dve.wait_ge(in_landed[p], i * 16 + 16)
                    for b in range(2):
                        last = nc.vector.tensor_tensor_scan(b_sum[:, b, 0:n], ones[:, 0:n], I[:, R_LOGF + b, 0:n],
                                                            0.0, ALU.mult, ALU.add)
                    last.then_inc(S["b_ready"], 1)
                    now(dve, "gbt", c)
                    cp(decay_beta[0:n], ring[0][0:n, 0].rearrange("p (a b) -> p a b", b=32)[:, 1:3, 0:HEADS]) \
                        .then_inc(S["gb_taken"], 1)
                    now(dve, "b_ready", c)
                    before(dve, "QF_ready", c)
                    for b in range(2):
                        bs = b_sum[:, b, 0:n]
                        cp(F[:, 0, b, 0:n], bs)
                        for l in range(LEVELS):
                            s = 1 << l
                            if l >= L:
                                cp(F[:, l + 1, b, 0:n], bs)
                                continue
                            blocks = bs.rearrange("p (m t) -> p m t", t=2 * s)
                            tt(F[:, l + 1, b, 0:n].rearrange("p (m t) -> p m t", t=2 * s), blocks,
                               blocks[:, :, s - 1:s].to_broadcast([P, n // (2 * s), 2 * s]), ALU.subtract)
                        last = tt(F[:, LEVELS + 1, b, 0:n], bs, bs[:, n - 1:n].to_broadcast([P, n]), ALU.subtract)
                    last.then_inc(S["F_diffs"], 1)
                    now(dve, "gcol", c)
                    cp(g_col[0:n], ring[0][0:n, 1, 0:HEADS]).then_inc(S["gcol_taken"], 1)
                    now(dve, "grow_taken", c)
                    now(dve, "gcol_taken", c)
                    tt(d_col[0:n], g_row[0:n, :, n - 1], g_col[0:n], ALU.subtract).then_inc(S["dcol_diff"], 1)
                    now(dve, "d_col_ready", c)
                    now(dve, "kt", c)
                    tt(k_tok[0:n], ring[2][0:n], per_token(d_col[0:n]), ALU.mult).then_inc(S["kt_taken"], 1)
                    now(dve, "KK", c)
                    now(dve, "dec_kk_ready", c)
                    for h in range(HEADS):
                        last = stt(M[0:n, h, 0:n], ring[1][0:n, h, 0:n], beta[:, h:h + 1], dec_kk[0:n, h, 0:n],
                                   ALU.mult, ALU.mult)
                    last.then_inc(S["KK_taken"], 1)
                    now(dve, "KK_taken", c)
                    tt(M0[0:n, :, 0:n], M[0:n, :, 0:n], over_heads(masks[0:n, M_LOW:M_LOW + n]),
                       ALU.mult).then_inc(S["M0_ready"], 1)
                    now(dve, "M0_ready", c)
                    tt(X[0:n, :, 0:n], over_heads(ident[0:n, 0:n]), M0[0:n, :, 0:n],
                       ALU.subtract).then_inc(S["X_ready"], 1)
                    now(dve, "QK", c)
                    now(dve, "dec_qk_ready", c)
                    tt(att[0:n, :, 0:n], ring[2][0:n, :, 0:n], dec_qk[0:n, :, 0:n], ALU.mult) \
                        .then_inc(S["QK_taken"], 1)
                    now(dve, "m0t", c)
                    tt(XT[0:n, :, 0:n], over_heads(ident[0:n, 0:n]), ring[1][0:n, :, 0:n],
                       ALU.subtract).then_inc(S["m0t_taken"], 1)
                    now(dve, "R", c)
                    now(dve, "vt_taken", c)
                    tt(U[0:n], v_tok[0:n], ring[2][0:n], ALU.subtract).then_inc(S["R_taken"], 1)
                    now(dve, "F_ready", c)
                    before(dve, "kdtg", c)
                    for b in range(2):
                        k = I[:, R_GLA_K + b:R_GLA_K + b + 1, 0:n].to_broadcast([P, LEVELS + 1, n])
                        last = tt(KF[:, :, b, 0:n], k, F[:, 1:LEVELS + 2, b, 0:n], ALU.mult)
                    last.then_inc(S["KF_ready"], 1)

                    def take_pairs(h):
                        dve.wait_ge(pairs_ready, c * HEADS + h + 1)
                        tt(masked[0:n, h, 0:L, 0:n // 2], pair_bank[0:n, 0:L, 0:n // 2],
                           level_masks[0:n, 0:L, 0:n // 2], ALU.mult).then_inc(pairs_masked, 1)

                    for l in range(1, L):
                        s = 1 << l
                        dve.wait_ge(z_ready, c * (LEVELS - 1) + l)
                        level = level_masks[0:n, l:l + 1, 0:n // 2].to_broadcast([n, HEADS, n // 2])
                        tt(halves_packed(Z[0:n, :, 0:n // 2], s), halves_packed(z_bank[0:n, :, 0:n // 2], s),
                           halves_packed(level, s), ALU.mult).then_inc(z_taken, 1)
                        if l > 1:
                            dve.wait_ge(x_turned, c * TURNS + (l - 1))
                            cp(X[0:n, :, 0:n], x_bank[0:n, :, 0:n]).then_inc(x_taken, 1)
                        if l == 1:
                            now(dve, "diag", c)
                            tt(gla_att[0:n, :, 0:n], ring[0][0:n, :, 0:n], over_heads(ident[0:n, 0:n]),
                               ALU.mult).then_inc(S["diag_taken"], 1)
                        if 2 <= l <= HEADS + 1:
                            take_pairs(l - 2)
                        dve.wait_ge(xt_products, c * (LEVELS - 1) + l)
                        new = second_halves(XT[0:n, :, 0:n], s)
                        tt(new, new, halves_packed(xt_bank[0:n, :, 0:n // 2], s),
                           ALU.subtract).then_inc(xt_updated, 1)
                    dve.wait_ge(xt_updated, c * (LEVELS - 1) + (L - 1))
                    tt(XT[0:n, :, 0:n], XT[0:n, :, 0:n], per_token(beta, n), ALU.mult).then_inc(S["XTb_ready"], 1)

                    def scale_outputs(name, which, z):
                        now(dve, name + "_squared", c)
                        dve.wait_ge(out_stored if which == 0 else outg_stored, c * 16 + 16)
                        tt(out_sb[which][:, :, 0:n], ring[which][:, :, 0:n], I[:, z:z + 4, 0:n],
                           ALU.mult).then_inc(S[name + "_scaled"], 1)
                    scale_outputs("Og", 1, R_GLA_Z)
                    scale_outputs("O", 0, R_GDN_Z)
                    now(dve, "dS", c)
                    for h in range(HEADS):
                        last = stt(state[:, h], state[:, h], e_row[:, h, n - 1:n], ring[1][:, h], ALU.mult, ALU.add)
                    last.then_inc(S["dS_taken"], 1)
                    now(dve, "dSg", c)
                    for h in range(HEADS):
                        rows = half_of(h)
                        last = stt(gla_state[rows, h], gla_state[rows, h], F[rows, 0, h // 2, n - 1:n],
                                   ring[2][rows, h], ALU.mult, ALU.add)
                    last.then_inc(S["dSg_taken"], 1)

                nc.vector.memset(eps[:, :], EPS).then_inc(eps_ready, 1)
                nc.vector.memset(state[:, :, :], 0.0)
                nc.vector.memset(gla_state[:, :, :], 0.0).then_inc(state_zero, 1)
                dve.wait_ge(state_zero, 1)
                dve.wait_ge(masks_landed, 16)
                preload(dve, DVE_)
                dve.sem_inc(pairs_masked, 1)
                per_chunk(dve, chunk)


class LateWeights:
    FIRST = 4
    BYTES = 4

    def __init__(self, nc, held, offset):
        wo_bytes = 12 * DM * self.BYTES
        self.split_tiles = offset
        self.wo_raw = nc.alloc_sbuf_tensor_at("wo_raw", [P, 12, DM], F32, offset=offset)
        self.w_out_first = nc.alloc_sbuf_tensor_at("w_out_first", [P, self.FIRST, DM], F32,
                                                   offset=offset + wo_bytes)
        self.o_raw = offset + wo_bytes + self.FIRST * DM * self.BYTES
        self.w_out_then = nc.alloc_sbuf_tensor_at("w_out_then", [P, 3, DM], F32, offset=self.o_raw)
        self.words = (self.o_raw - offset) // self.BYTES + 3 * DM
        self.wo_landed = held.add(nc.alloc_semaphore("wo_landed"))
        self.first_landed = held.add(nc.alloc_semaphore("w_out_first_landed"))
        self.then_landed = held.add(nc.alloc_semaphore("w_out_then_landed"))

    def load_in_chunk_phase(self, sp, d):
        sp.dma_start(self.wo_raw[:, :, :], d["wo"].rearrange("(k p) n -> p k n", p=P)).then_inc(self.wo_landed, 16)
        sp.dma_start(self.w_out_first[:, :, :], d["w_out"][0:self.FIRST * P, :].rearrange("(k p) n -> p k n", p=P)) \
            .then_inc(self.first_landed, 16)

    def load_in_branch_phase(self, sp, d):
        sp.dma_start(self.w_out_then[:, :, :], d["w_out"][self.FIRST * P:7 * P, :]
                     .rearrange("(k p) n -> p k n", p=P)).then_inc(self.then_landed, 16)


def branch_phase(nc, d, late):
    K = 12
    TT = 256
    TILES_B = NP_ // TT
    with ExitStack() as ctx, Held(nc) as held:
        def sb(name, shape, dt=F32):
            return ctx.enter_context(nc.sbuf_tensor(name, shape, dt))

        def sem(name):
            return held.add(nc.alloc_semaphore(name))

        wo_hi = sb("wo_hi", [P, K, DM], F32R)
        wo_lo = sb("wo_lo", [P, K, DM], F32R)
        o_raw = nc.alloc_sbuf_tensor_at("o_raw", [P, K, TT], F32, offset=late.o_raw)
        o_hi = nc.alloc_sbuf_tensor_at("o_hi", [P, 2, K, TT], F32R, offset=late.split_tiles)
        o_lo = nc.alloc_sbuf_tensor_at("o_lo", [P, 2, K, TT], F32R,
                                       offset=late.split_tiles + 2 * K * TT * late.BYTES)
        gate = sb("gate", [P, 2, 12, TT])
        prod = sb("prod", [P, 2, 3, TT])
        part = sb("part", [P, 2, TT])
        merged = sb("merged", [P, 2, TT])
        y = ctx.enter_context(nc.psum_tensor("y", [P, 2, 4, TT], F32))

        wo_high, wo_split = sem("wo_high"), sem("wo_split")
        o_landed, o_high, o_split = sem("o_landed"), sem("o_high"), sem("o_split")
        first_high, first_split = sem("first_high"), sem("first_split")
        gate_landed = [sem("gate_landed0"), sem("gate_landed1")]
        gates_open = sem("gates_open")
        y_ready, y_gated = sem("y_ready"), sem("y_gated")
        part_ready, merged_ready = sem("part_ready"), sem("merged_ready")
        merged_stored = [sem("merged_stored0"), sem("merged_stored1")]
        outs, gates = d["branch_out"], d["gates"]

        def load_o(sp, t, n=TT):
            sp.dma_start(o_raw[:, :, 0:n], outs[:, :, bass.ds(t * TT, n)]).then_inc(o_landed, 16)

        def load_gates(sp, t, half, n=TT):
            sp.dma_start(gate[:, half, :, 0:n],
                         gates[:, half * 12:half * 12 + 12, bass.ds(t * TT, n)]).then_inc(gate_landed[half], 16)

        with nc.Block() as block:
            @block.sync
            def _(sp):
                load_o(sp, 0)
                load_gates(sp, 0, 0)
                load_gates(sp, 0, 1)

            @block.scalar
            def _(act):
                act.wait_ge(late.wo_landed, 16)
                for k in range(K):
                    nc.scalar.copy(wo_hi[:, k], late.wo_raw[:, k]).then_inc(wo_high, 1)

            @block.vector
            def _(dve):
                for k in range(K):
                    dve.wait_ge(wo_high, k + 1)
                    nc.vector.tensor_tensor(wo_lo[:, k], late.wo_raw[:, k], wo_hi[:, k].bitcast(F32),
                                            ALU.subtract).then_inc(wo_split, 1)
                dve.wait_ge(wo_split, K)

        with nc.Block() as block:
            def per_tile(eng, tile):
                tile(0, 0, 0, TT)
                tile(1, 0, 1, TT)
                with eng.Fori(1, TILES_B // 2) as i:
                    tile(i * 2, i, 0, TT)
                    tile(i * 2 + 1, i, 1, TT)
                tile(TILES_B, TILES_B // 2, 0, NS_)

            @block.sync
            def _(sp):
                def store(t, m, n=TT):
                    sp.wait_ge(merged_ready, t * KD + (m + 1))
                    sp.dma_start(d["merged"][:, m, bass.ds(t * TT, n)], merged[:, m % 2, 0:n]) \
                        .then_inc(merged_stored[m % 2], 16)

                def tile(t, n=TT, ahead=TT):
                    if ahead:
                        sp.wait_ge(o_split, t + 1)
                        load_o(sp, t + 1, ahead)
                    for m in range(KD):
                        store(t, m, n)
                        if ahead and m % 4 == 3:
                            load_gates(sp, t + 1, m // 4, ahead)
                tile(0)
                with sp.Fori(1, TILES_B - 1) as t:
                    tile(t)
                tile(TILES_B - 1, TT, NS_)
                sp.wait_ge(o_split, TILES_B + 1)
                late.load_in_branch_phase(sp, d)
                tile(TILES_B, NS_, 0)
                for q in range(2):
                    sp.wait_ge(merged_stored[q], 16 * 4 * (TILES_B + 1))

            @block.scalar
            def _(act):
                def tile(t, i, p, n):
                    act.wait_ge(o_landed, t * 16 + 16)
                    if not (isinstance(t, int) and t < 2):
                        act.wait_ge(y_ready, (t - 1) * KD)
                    if isinstance(t, int) and t == 0:
                        for b in range(3):
                            rows = slice(4 * b, 4 * b + 4)
                            nc.scalar.copy(o_hi[:, p, rows, 0:n], o_raw[:, rows, 0:n]) \
                                .then_inc(o_high if b == 2 else first_high, 1)
                    else:
                        nc.scalar.copy(o_hi[:, p, :, 0:n], o_raw[:, :, 0:n]).then_inc(o_high, 1)
                    for half in range(2):
                        act.wait_ge(gate_landed[half], t * 16 + 16)
                        g = gate[:, half, :, 0:n]
                        nc.scalar.activation(g, g, ACT.Sigmoid).then_inc(gates_open, 1)
                per_tile(act, tile)

            @block.tensor
            def _(pe):
                def tile(t, i, p, n):
                    first = isinstance(t, int) and t == 0
                    if not first:
                        pe.wait_ge(o_split, t + 1)
                    for m in range(KD):
                        if not (isinstance(t, int) and t == 0 and m < 2):
                            pe.wait_ge(y_gated, t * KD + (m - 1))
                        cols = slice(m * P, (m + 1) * P)
                        for b in range(3):
                            if first and m == 0:
                                pe.wait_ge(*((o_split, 1) if b == 2 else (first_split, b + 1)))
                            out = y[:, m % 2, b, 0:n]
                            for k in range(4 * b, 4 * b + 4):
                                nc.tensor.matmul(out, wo_hi[:, k, cols], o_hi[:, p, k, 0:n],
                                                 start=(k == 4 * b), stop=False)
                                nc.tensor.matmul(out, wo_hi[:, k, cols], o_lo[:, p, k, 0:n],
                                                 start=False, stop=False)
                                mm = nc.tensor.matmul(out, wo_lo[:, k, cols], o_hi[:, p, k, 0:n],
                                                      start=False, stop=(k == 4 * b + 3))
                        mm.then_inc(y_ready, 1)
                per_tile(pe, tile)

            @block.vector
            def _(dve):
                def low(t, p, n):
                    dve.wait_ge(o_high, t + 1)
                    nc.vector.tensor_tensor(o_lo[:, p, :, 0:n], o_raw[:, :, 0:n],
                                            o_hi[:, p, :, 0:n].bitcast(F32), ALU.subtract).then_inc(o_split, 1)

                def gated(t, m, n):
                    dve.wait_ge(y_ready, t * KD + (m + 1))
                    if m % 4 == 0:
                        dve.wait_ge(gates_open, t * 2 + (m // 4 + 1))
                    if not (isinstance(t, int) and t == 0 and m < 2):
                        dve.wait_ge(merged_ready, t * KD + (m - 1))
                    g = gate[:, m // 4, 3 * (m % 4):3 * (m % 4) + 3, 0:n]
                    nc.vector.tensor_tensor(prod[:, m % 2, :, 0:n], y[:, m % 2, 0:3, 0:n], g,
                                            ALU.mult).then_inc(y_gated, 1)

                def tile(t, i, p, n):
                    for m in range(KD):
                        gated(t, m, n)
                        if m == 3 and not (isinstance(t, int) and t == TILES_B):
                            low(t + 1, 1 - p, TT)
                for b in range(3):
                    rows = slice(4 * b, 4 * b + 4)
                    dve.wait_ge(*((o_high, 1) if b == 2 else (first_high, b + 1)))
                    nc.vector.tensor_tensor(o_lo[:, 0, rows], o_raw[:, rows], o_hi[:, 0, rows].bitcast(F32),
                                            ALU.subtract).then_inc(o_split if b == 2 else first_split, 1)
                tile(0, 0, 0, TT)
                with dve.Fori(0, TILES_B // 2 - 1) as i:
                    tile(i * 2 + 1, i, 1, TT)
                    tile(i * 2 + 2, i, 0, TT)
                for m in range(KD):
                    gated(TILES_B - 1, m, TT)
                    if m == 3:
                        low(TILES_B, 0, NS_)
                for m in range(KD):
                    gated(TILES_B, m, NS_)

            @block.gpsimd
            def _(pool):
                def tile(t, i, p, n):
                    for m in range(KD):
                        q = m % 2
                        pool.wait_ge(y_gated, t * KD + (m + 1))
                        nc.gpsimd.tensor_tensor(part[:, q, 0:n], prod[:, q, 0, 0:n], prod[:, q, 1, 0:n],
                                                ALU.add).then_inc(part_ready, 1)
                        pool.wait_ge(part_ready, t * KD + (m + 1))
                        if not (isinstance(t, int) and t == 0 and m < 2):
                            pool.wait_ge(merged_stored[q], t * (4 * 16) + (m // 2) * 16)
                        nc.gpsimd.tensor_tensor(merged[:, q, 0:n], part[:, q, 0:n], prod[:, q, 2, 0:n],
                                                ALU.add).then_inc(merged_ready, 1)
                per_tile(pool, tile)


def output_phase(nc, d, late):
    with ExitStack() as ctx, Held(nc) as held:
        def sb(name, shape, dt=F32):
            return ctx.enter_context(nc.sbuf_tensor(name, shape, dt))

        def sem(name):
            return held.add(nc.alloc_semaphore(name))

        w_hi = sb("wout_hi", [P, KD, DM], F32R)
        w_lo = sb("wout_lo", [P, KD, DM], F32R)
        w_last = sb("wout_last", [P, DM])
        m_raw = sb("m_raw", [P, 2, KD, P])
        m_hi = sb("m_hi", [P, 2, KD, P], F32R)
        m_lo = sb("m_lo", [P, 2, KD, P], F32R)
        x_in = sb("x_again", [P, 2, DM])
        squares = sb("y_squares", [P, DM])
        normed = sb("normed", [P, 2, DM])
        result = sb("result", [P, 2, DM])
        gain = sb("post_gain", [P, DM])
        stat = sb("stat", [P, 2, 6])
        eps = sb("post_eps", [P, 1])
        y = ctx.enter_context(nc.psum_tensor("y_tok", [P, 2, DM], F32))

        w_last_landed = sem("w_last_landed")
        w_high, w_split = sem("wout_high"), sem("wout_split")
        gain_landed = sem("post_gain_landed")
        m_landed = [sem("m_landed0"), sem("m_landed1")]
        x_landed = [sem("x_again0"), sem("x_again1")]
        m_high, m_split = sem("m_high"), sem("m_split")
        y_ready = sem("y_tok_ready")
        sum_ready, log_ready, rstd_ready = sem("sum_ready"), sem("log_ready"), sem("post_rstd_ready")
        newton = sem("newton")
        normed_ready, result_ready = sem("normed_ready"), sem("result_ready")
        stored = [sem("stored0"), sem("stored1")]
        eps_set = sem("post_eps_set")

        def w_raw(k):
            if k < late.FIRST:
                return late.w_out_first[:, k]
            return late.w_out_then[:, k - late.FIRST] if k < KD - 1 else w_last[:, :]

        with nc.Block() as block:
            def per_tile(eng, tile):
                tile(0, 0, 0, P)
                tile(1, 0, 1, P)
                with eng.Fori(1, CHUNKS // 2) as i:
                    tile(i * 2, i, 0, P)
                    tile(i * 2 + 1, i, 1, P)
                tile(CHUNKS, CHUNKS // 2, 0, NS_)

            @block.sync
            def _(sp):
                def load_m(t, p, n=P):
                    sp.dma_start(m_raw[:, p, :, 0:n], d["merged"][:, :, bass.ds(t * P, n)]).then_inc(m_landed[p], 16)

                def load_x(t, p, n=P):
                    x = d["x_prompt"][bass.ds(t * P, P), :] if n == P else d["x_sample"]
                    sp.dma_start(x_in[0:n, p], x).then_inc(x_landed[p], 16)

                def load_next_m(t, p, n=P):
                    sp.wait_ge(m_split, t - 1)
                    load_m(t, p, n)

                def store(t, p, n=P):
                    y_out = d["y_prompt"][bass.ds(t * P, P), :] if n == P else d["y_sample"]
                    sp.wait_ge(result_ready, t + 1)
                    sp.dma_start(y_out, result[0:n, p]).then_inc(stored[p], 16)

                load_m(0, 0)
                sp.dma_start(w_last[:, :], d["w_out"][(KD - 1) * P:KD * P, :]).then_inc(w_last_landed, 16)
                sp.dma_start(gain[:, :], d["norm_post"].to_broadcast([P, DM])).then_inc(gain_landed, 16)
                load_m(1, 1)
                load_x(0, 0)
                load_x(1, 1)
                with sp.Fori(0, CHUNKS // 2 - 1) as i:
                    for p in range(2):
                        load_next_m(i * 2 + (p + 2), p)
                        store(i * 2 + p, p)
                        load_x(i * 2 + (p + 2), p)
                load_next_m(CHUNKS, 0, NS_)
                store(CHUNKS - 2, 0)
                load_x(CHUNKS, 0, NS_)
                store(CHUNKS - 1, 1)
                store(CHUNKS, 0, NS_)
                sp.wait_ge(stored[0], 16 * (CHUNKS // 2 + 1))
                sp.wait_ge(stored[1], 16 * (CHUNKS // 2))

            @block.scalar
            def _(act):
                def high(t, i, p, n):
                    act.wait_ge(m_landed[p], i * 16 + 16)
                    if not (isinstance(t, int) and t < 2):
                        act.wait_ge(y_ready, t - 1)
                    nc.scalar.copy(m_hi[:, p, :, 0:n], m_raw[:, p, :, 0:n]).then_inc(m_high, 1)

                def statistics(t, p, n):
                    act.wait_ge(y_ready, t + 1)
                    if not (isinstance(t, int) and t < 2):
                        act.wait_ge(normed_ready, t - 1)
                    nc.scalar.activation(squares[0:n], y[0:n, p], ACT.Square,
                                         accum_out=stat[0:n, p, 0:1]).then_inc(sum_ready, 1)
                    act.wait_ge(sum_ready, t + 1)
                    nc.scalar.activation(stat[0:n, p, 1:2], stat[0:n, p, 0:1], ACT.Ln, bias=eps[0:n, 0:1],
                                         scale=1.0 / DM).then_inc(log_ready, 1)
                    act.wait_ge(log_ready, t + 1)
                    nc.scalar.activation(stat[0:n, p, 2:3], stat[0:n, p, 1:2], ACT.Exp,
                                         scale=-0.5).then_inc(rstd_ready, 1)

                use_log_exp_tables(nc)
                act.wait_ge(eps_set, 1)
                high(0, 0, 0, P)
                for k in range(KD):
                    if k == 0:
                        act.wait_ge(late.first_landed, 16)
                    if k == late.FIRST:
                        act.wait_ge(late.then_landed, 16)
                    if k == KD - 1:
                        act.wait_ge(w_last_landed, 16)
                    nc.scalar.copy(w_hi[:, k], w_raw(k)).then_inc(w_high, 1)
                high(1, 0, 1, P)
                for p in range(2):
                    statistics(p, p, P)
                    high(p + 2, 1, p, P)
                with act.Fori(1, CHUNKS // 2 - 1) as i:
                    for p in range(2):
                        statistics(i * 2 + p, p, P)
                        high(i * 2 + (p + 2), i + 1, p, P)
                statistics(CHUNKS - 2, 0, P)
                high(CHUNKS, CHUNKS // 2, 0, NS_)
                statistics(CHUNKS - 1, 1, P)
                statistics(CHUNKS, 0, NS_)

            @block.tensor
            def _(pe):
                def tile(t, i, p, n):
                    pe.wait_ge(m_split, t + 1)
                    if not (isinstance(t, int) and t < 2):
                        pe.wait_ge(normed_ready, t - 1)
                    for half in range(2):
                        cols = slice(half * 512, half * 512 + 512)
                        out = y[0:n, p, cols]
                        for k in range(KD):
                            if isinstance(t, int) and t == 0 and half == 0:
                                pe.wait_ge(w_split, k + 1)
                            nc.tensor.matmul(out, m_hi[:, p, k, 0:n], w_hi[:, k, cols], start=(k == 0), stop=False)
                            nc.tensor.matmul(out, m_hi[:, p, k, 0:n], w_lo[:, k, cols], start=False, stop=False)
                            mm = nc.tensor.matmul(out, m_lo[:, p, k, 0:n], w_hi[:, k, cols], start=False,
                                                  stop=(k == KD - 1))
                    mm.then_inc(y_ready, 1)
                tile(0, 0, 0, P)
                tile(1, 0, 1, P)
                tile(2, 1, 0, P)
                tile(3, 1, 1, P)
                with pe.Fori(1, CHUNKS // 4) as i:
                    for u in range(4):
                        tile(i * 4 + u, None, u % 2, P)
                tile(CHUNKS, None, 0, NS_)

            @block.vector
            def _(dve):
                def low(t, p, n):
                    dve.wait_ge(m_high, t + 1)
                    nc.vector.tensor_tensor(m_lo[:, p, :, 0:n], m_raw[:, p, :, 0:n],
                                            m_hi[:, p, :, 0:n].bitcast(F32), ALU.subtract).then_inc(m_split, 1)

                def norm(t, p, n):
                    v, vr, vrr, r, better = (stat[0:n, p, i:i + 1] for i in (0, 1, 3, 2, 4))
                    stt = nc.vector.scalar_tensor_tensor
                    dve.wait_ge(rstd_ready, t + 1)
                    nc.vector.tensor_scalar(v, v, 1.0 / DM, EPS, ALU.mult, ALU.add).then_inc(newton, 1)
                    dve.wait_ge(newton, t * 4 + 1)
                    stt(vr, v, -0.5, r, ALU.mult, ALU.mult).then_inc(newton, 1)
                    dve.wait_ge(newton, t * 4 + 2)
                    nc.vector.tensor_tensor(vrr, vr, r, ALU.mult).then_inc(newton, 1)
                    dve.wait_ge(newton, t * 4 + 3)
                    stt(better, vrr, 1.5, r, ALU.add, ALU.mult).then_inc(newton, 1)
                    dve.wait_ge(newton, t * 4 + 4)
                    if not (isinstance(t, int) and t < 2):
                        dve.wait_ge(result_ready, t - 1)
                    nc.vector.scalar_tensor_tensor(normed[0:n, p], y[0:n, p], better, gain[0:n],
                                                   ALU.mult, ALU.mult).then_inc(normed_ready, 1)

                nc.vector.memset(eps[:, :], EPS).then_inc(eps_set, 1)
                low(0, 0, P)
                for k in range(KD):
                    dve.wait_ge(w_high, k + 1)
                    nc.vector.tensor_tensor(w_lo[:, k], w_raw(k), w_hi[:, k].bitcast(F32),
                                            ALU.subtract).then_inc(w_split, 1)
                low(1, 1, P)
                dve.wait_ge(gain_landed, 16)
                norm(0, 0, P)
                low(2, 0, P)
                norm(1, 1, P)
                low(3, 1, P)
                with dve.Fori(1, CHUNKS // 2 - 1) as i:
                    for p in range(2):
                        norm(i * 2 + p, p, P)
                        low(i * 2 + (p + 2), p, P)
                norm(CHUNKS - 2, 0, P)
                low(CHUNKS, 0, NS_)
                norm(CHUNKS - 1, 1, P)
                norm(CHUNKS, 0, NS_)

            @block.gpsimd
            def _(pool):
                def tile(t, i, p, n):
                    pool.wait_ge(x_landed[p], i * 16 + 16)
                    if not (isinstance(t, int) and t < 2):
                        pool.wait_ge(stored[p], i * 16)
                    pool.wait_ge(normed_ready, t + 1)
                    nc.gpsimd.tensor_tensor(result[0:n, p], normed[0:n, p], x_in[0:n, p],
                                            ALU.add).then_inc(result_ready, 1)
                per_tile(pool, tile)


def program(nc, d):
    with Held(nc) as held:
        h_offset = (nc.sbuf_base + 31) // 32 * 32
        late = LateWeights(nc, held, h_offset)
        with ExitStack() as ctx:
            def halves(context, names):
                return [context.enter_context(nc.sbuf_tensor(n, [P, KD, HALF_TOKENS], F32R)) for n in names]
            hi_0, lo_0 = halves(ctx, ("h_hi_first", "h_lo_first"))
            consts = ctx.enter_context(nc.sbuf_tensor("constants", [P, C_END], F32))
            with ExitStack() as early:
                hi_1, lo_1 = halves(early, ("h_hi_second", "h_lo_second"))
                weights = BlockWeights(nc, early, held)
                norm_phase(nc, d, (hi_0, hi_1), (lo_0, lo_1), consts, weights)
                project_phase(nc, d, (hi_0, hi_1), (lo_0, lo_1), consts, weights)
            chunk_phase(nc, d, consts, hi_0, lo_0, late)
        with nc.sbuf_tensor("late_bytes", [P, late.words], F32):
            branch_phase(nc, d, late)
            output_phase(nc, d, late)


def shape_constants():
    import numpy as np
    c = np.zeros((P, C_END), np.float32)
    m = np.zeros((P, M_END), np.float32)
    i = np.arange(P)
    row, col = i[:, None], i[None, :]
    c[:, C_IDENT:C_IDENT + P] = np.eye(P)
    c[:, C_ONES:C_ONES + P] = 1
    c[:, C_CNT:C_CNT + 16] = 1.0 / (1 + np.arange(16))
    m[:, M_UPPER:M_UPPER + P] = row <= col
    m[:, M_NEG:M_NEG + P] = np.where(row <= col, 0, -1e30)
    m[:, M_POS:M_POS + P] = np.where(row > col, 0, 1e30)
    for n in range(LEVELS):
        s = 1 << n
        low = (row // (2 * s) == col // (2 * s)) & (row // s % 2 == 1) & (col // s % 2 == 0)
        if n == 0:
            m[:, M_LOW:M_LOW + P] = low
        m[:, M_PAIRS + n * HALF:M_PAIRS + (n + 1) * HALF] = low.T[:, i // s % 2 == 1]
    return c, m


def laid_out(x):
    import numpy as np
    x = {k: np.asarray(v) for k, v in x.items()}
    w = x["w_in"][0]
    blocks = np.zeros((F_END, P, DM), np.float32)

    def put(f, cols):
        part = w[:, cols:cols + P]
        blocks[f] = part.reshape(KD, P, P).transpose(1, 0, 2).reshape(P, DM)
    special = np.zeros((DM, P), np.float32)
    special[:, AT_F:AT_F + 16] = w[:, 1024:1040]
    special[:, AT_G:AT_G + 4] = w[:, 4112:4116]
    special[:, AT_B:AT_B + 4] = w[:, 4116:4120]
    blocks[F_SPECIAL] = special.reshape(KD, P, P).transpose(1, 0, 2).reshape(P, DM)
    for n in range(8):
        put(F_COPY + n, n * P)
    for n in range(4):
        put(F_SILU + n, 1040 + n * P)
        put(F_SILU + 4 + n, 4120 + n * P)
        put(F_POOL + 2 * n, 1552 + n * P)
        put(F_POOL + 2 * n + 1, 2064 + n * P)
    for n in range(12):
        put(F_CONV + n, 2576 + n * P)
    for n in range(24):
        put(F_GATE + n, 4632 + (n % 3) * DM + (n // 3) * P)

    def columns(v, n):
        return np.ascontiguousarray(v.reshape(n, P).T)
    return {
        "x_prompt": x["x_prompt"][0], "x_sample": x["x_sample"][0], "norm_pre": x["norm_pre"],
        "consts": shape_constants()[0], "masks": shape_constants()[1], "w_in": blocks,
        "gla_bf": columns(x["gla_bf"], 2),
        "pool_scale": columns(x["pool_scale"], 4), "gla_norm": columns(x["gla_norm"], 4),
        "gdn_norm": columns(x["gdn_norm"], 4),
        "gdn_conv": np.ascontiguousarray(x["gdn_conv"][0].reshape(4, 12, P).transpose(2, 1, 0)).reshape(P, 48),
        "scalars": np.tile(np.array([[EPS, np.log(P ** -0.5)]], np.float32), (P, 1)),
        "gdn_a_log": x["gdn_a_log"].reshape(4, 1), "gdn_dt_bias": x["gdn_dt_bias"].reshape(4, 1),
        "gla_wf2": x["gla_wf2"][0], "pool_w": np.ascontiguousarray(x["pool_w"][0].transpose(1, 0, 2)),
        "conv_cache": np.ascontiguousarray(x["cache_gdn_conv"][0, 0].reshape(3, 12, P).transpose(2, 1, 0)),
        "pool_cache": np.ascontiguousarray(x["cache_pool"][0, 0].reshape(15, 4, P).transpose(2, 1, 0)),
        "state_gla": x["state_gla"][0, 0], "state_gdn": x["state_gdn"][0, 0],
        "wo": np.concatenate([x["gla_wo"][0], x["pool_wo"][0], x["gdn_wo"][0]]),
        "w_out": x["w_out"][0], "norm_post": x["norm_post"],
    }


_OUTS = {
    "y_prompt": (NP_, DM), "y_sample": (NS_, DM),
    "new_gla_prompt": (HEADS, 64, P), "new_gdn_prompt": (HEADS, P, P),
    "new_conv_prompt": (P, 12, CONV_HALO), "new_pool_prompt": (P, 4, POOL_HALO),
    "new_gla_sample": (HEADS, 64, P), "new_gdn_sample": (HEADS, P, P),
    "new_conv_sample": (P, 12, CONV_HALO), "new_pool_sample": (P, 4, POOL_HALO),
}
_SCRATCH = {"feat": (P, R_END, NT), "gates": (P, 24, NT), "branch_out": (P, 12, NT), "merged": (P, KD, NT),
            "h_second": (P, 2, KD, HALF_TOKENS)}


def kernel(**inputs):
    import numpy as np
    import concourse.bacc as bacc
    from concourse.bass_utils import run_bass_kernel_spmd

    nc = bacc.Bacc("TRN2", target_bir_lowering=False, num_devices=1)
    arrays, d = {}, {}
    for name, a in laid_out(inputs).items():
        a = np.ascontiguousarray(a)
        arrays[f"in_{name}"] = a
        d[name] = nc.dram_tensor(f"in_{name}", a.shape, F32, kind="ExternalInput").ap()
    for name, shape in _OUTS.items():
        d[name] = nc.dram_tensor(f"out_{name}", shape, F32, kind="ExternalOutput").ap()
    for name, shape in _SCRATCH.items():
        d[name] = nc.dram_tensor(f"scratch_{name}", shape, F32, kind="Internal").ap()
    program(nc, d)
    r = run_bass_kernel_spmd(nc, [arrays], core_ids=[0]).results[0]
    got = {name: r[f"out_{name}"] for name in _OUTS}

    def cache(a):
        return np.ascontiguousarray(a.transpose(2, 1, 0)).reshape(1, 1, a.shape[2], -1)
    out = [got["y_prompt"][None], got["y_sample"][None]]
    for group in ("prompt", "sample"):
        out += [got[f"new_gla_{group}"][None, None], got[f"new_gdn_{group}"][None, None],
                cache(got[f"new_conv_{group}"]), cache(got[f"new_pool_{group}"])]
    return tuple(out)
```
